# Optimizing a Trainium2 kernel written in Bass

```python
import jax, jax.numpy as jnp
from jax import lax
import numpy as np

D_MODEL = 1024
BATCH = 1
SEQ = 512
DEPTH = 2

N_MIXERS = 2
RMS_EPS = 1e-6
LN_EPS = 1e-5
CHUNK = 128
A_WIDTH = 2 * D_MODEL
A_GROUPS = 8
A_GROUP_DIM = A_WIDTH // A_GROUPS
B_WIDTH = 3 * D_MODEL // 2
B_HEADS = 12
B_HEAD_DIM = B_WIDTH // B_HEADS
CONV_WIDTH = 4
RG_C = 8.0

N_A_LAYERS = (DEPTH + 1) // 2
N_B_LAYERS = DEPTH // 2


def rms_norm(x, w):
    xf = x.astype(jnp.float32)
    y = xf * lax.rsqrt(jnp.mean(xf * xf, axis=-1, keepdims=True) + RMS_EPS)
    return (y * w.astype(jnp.float32)).astype(x.dtype)

def layer_norm(x, w, b):
    xf = x.astype(jnp.float32)
    mu = jnp.mean(xf, axis=-1, keepdims=True)
    var = jnp.mean(jnp.square(xf - mu), axis=-1, keepdims=True)
    y = (xf - mu) * lax.rsqrt(var + LN_EPS)
    return (y * w.astype(jnp.float32) + b.astype(jnp.float32)).astype(x.dtype)

def chunked_sgu_mixer(h, w_in, ln_w, ln_b, w_s, b_s, w_out):
    B, S, _ = h.shape
    z = h @ w_in
    u, v, g = jnp.split(z, 3, axis=-1)
    u = jax.nn.gelu(u)
    v = layer_norm(jax.nn.gelu(v), ln_w, ln_b)
    v = v.reshape(B, S // CHUNK, CHUNK, A_GROUPS, A_GROUP_DIM)
    causal = jnp.tril(jnp.ones((CHUNK, CHUNK), dtype=w_s.dtype))
    w_causal = w_s * causal[None]
    s = jnp.einsum('gts,bnsgc->bntgc', w_causal, v) + b_s.T[None, None, :, :, None]
    y = u * s.reshape(B, S, A_WIDTH) * jax.nn.silu(g)
    return y @ w_out

def _linear_combine(left, right):
    a_l, b_l = left
    a_r, b_r = right
    return a_l * a_r, a_r * b_l + b_r

def rglru_mixer(h, w_in, conv_w, conv_b, gate_a_w, gate_a_b, gate_x_w, gate_x_b, lam, w_out):
    B, S, _ = h.shape
    xb, g = jnp.split(h @ w_in, 2, axis=-1)
    xp = jnp.pad(xb, ((0, 0), (CONV_WIDTH - 1, 0), (0, 0)))
    xc = conv_b + conv_w[CONV_WIDTH - 1] * xp[:, CONV_WIDTH - 1:CONV_WIDTH - 1 + S]
    for k in range(CONV_WIDTH - 1):
        xc = xc + conv_w[k] * xp[:, k:k + S]
    xh = xc.reshape(B, S, B_HEADS, B_HEAD_DIM)
    r = jax.nn.sigmoid(jnp.einsum('bshi,hij->bshj', xh, gate_a_w).reshape(B, S, B_WIDTH) + gate_a_b)
    i = jax.nn.sigmoid(jnp.einsum('bshi,hij->bshj', xh, gate_x_w).reshape(B, S, B_WIDTH) + gate_x_b)
    log_a = -RG_C * r.astype(jnp.float32) * jax.nn.softplus(-lam.astype(jnp.float32))
    a = jnp.exp(log_a)
    mult = jnp.sqrt(-jnp.expm1(2.0 * log_a))
    bterm = mult * (i * xc).astype(jnp.float32)
    _, hseq = lax.associative_scan(_linear_combine, (a, bterm), axis=1)
    y = hseq.astype(h.dtype) * jax.nn.silu(g)
    return y @ w_out

def first_inputs(seed: int = 0) -> dict:
    key = jax.random.key(seed)
    ks = jax.random.split(key, 20)
    f32 = jnp.float32
    x = jax.random.normal(ks[0], (BATCH, SEQ, D_MODEL), f32)
    norm_w = 1.0 + 0.05 * jax.random.normal(ks[1], (DEPTH, D_MODEL), f32)
    a_w_in = jax.random.normal(ks[2], (N_A_LAYERS, D_MODEL, 3 * A_WIDTH), f32) * D_MODEL ** -0.5
    a_ln_w = 1.0 + 0.05 * jax.random.normal(ks[3], (N_A_LAYERS, A_WIDTH), f32)
    a_ln_b = 0.02 * jax.random.normal(ks[4], (N_A_LAYERS, A_WIDTH), f32)
    a_w_s = jax.random.normal(ks[5], (N_A_LAYERS, A_GROUPS, CHUNK, CHUNK), f32) * CHUNK ** -0.5
    a_b_s = 1.0 + 0.05 * jax.random.normal(ks[6], (N_A_LAYERS, A_GROUPS, CHUNK), f32)
    a_w_out = jax.random.normal(ks[7], (N_A_LAYERS, A_WIDTH, D_MODEL), f32) * A_WIDTH ** -0.5
    b_w_in = jax.random.normal(ks[8], (N_B_LAYERS, D_MODEL, 2 * B_WIDTH), f32) * D_MODEL ** -0.5
    b_conv_w = jax.random.normal(ks[9], (N_B_LAYERS, CONV_WIDTH, B_WIDTH), f32) * CONV_WIDTH ** -0.5
    b_conv_b = 0.02 * jax.random.normal(ks[10], (N_B_LAYERS, B_WIDTH), f32)
    b_gate_a_w = jax.random.normal(ks[11], (N_B_LAYERS, B_HEADS, B_HEAD_DIM, B_HEAD_DIM), f32) * B_HEAD_DIM ** -0.5
    b_gate_a_b = 0.02 * jax.random.normal(ks[12], (N_B_LAYERS, B_WIDTH), f32)
    b_gate_x_w = jax.random.normal(ks[13], (N_B_LAYERS, B_HEADS, B_HEAD_DIM, B_HEAD_DIM), f32) * B_HEAD_DIM ** -0.5
    b_gate_x_b = 0.02 * jax.random.normal(ks[14], (N_B_LAYERS, B_WIDTH), f32)
    a_c = jax.random.uniform(ks[15], (N_B_LAYERS, B_WIDTH), f32, minval=0.9, maxval=0.999)
    a0 = a_c ** (1.0 / RG_C)
    b_lambda = jnp.log(a0) - jnp.log1p(-a0)
    b_w_out = jax.random.normal(ks[16], (N_B_LAYERS, B_WIDTH, D_MODEL), f32) * B_WIDTH ** -0.5
    norm_f_w = 1.0 + 0.05 * jax.random.normal(ks[17], (D_MODEL,), f32)
    return {
        "x": x, "norm_w": norm_w,
        "a_w_in": a_w_in, "a_ln_w": a_ln_w, "a_ln_b": a_ln_b,
        "a_w_s": a_w_s, "a_b_s": a_b_s, "a_w_out": a_w_out,
        "b_w_in": b_w_in, "b_conv_w": b_conv_w, "b_conv_b": b_conv_b,
        "b_gate_a_w": b_gate_a_w, "b_gate_a_b": b_gate_a_b,
        "b_gate_x_w": b_gate_x_w, "b_gate_x_b": b_gate_x_b,
        "b_lambda": b_lambda, "b_w_out": b_w_out,
        "norm_f_w": norm_f_w,
    }

def first_block(x, norm_w, a_w_in, a_ln_w, a_ln_b, a_w_s, a_b_s, a_w_out,
              b_w_in, b_conv_w, b_conv_b, b_gate_a_w, b_gate_a_b,
              b_gate_x_w, b_gate_x_b, b_lambda, b_w_out, norm_f_w):
    for layer in range(DEPTH):
        h = rms_norm(x, norm_w[layer])
        j = layer // N_MIXERS
        if layer % N_MIXERS == 0:
            y = chunked_sgu_mixer(h, a_w_in[j], a_ln_w[j], a_ln_b[j], a_w_s[j], a_b_s[j], a_w_out[j])
        else:
            y = rglru_mixer(h, b_w_in[j], b_conv_w[j], b_conv_b[j], b_gate_a_w[j], b_gate_a_b[j],
                            b_gate_x_w[j], b_gate_x_b[j], b_lambda[j], b_w_out[j])
        x = x + y
    return rms_norm(x, norm_f_w)


DEPTH_2 = 1

N_MEM = 256
EPS = 1e-6
FOX_HEADS = 8
FOX_HEAD_DIM = 64
FOX_WIDTH = FOX_HEADS * FOX_HEAD_DIM
Q_BLOCK = 128
GDN_HEADS = 4
GDN_HEAD_DIM = 128
GDN_WIDTH = GDN_HEADS * GDN_HEAD_DIM
CHUNK_2 = 64
MIX_WIDTH = FOX_WIDTH + GDN_WIDTH
IN_PROJ_SIZES = (FOX_WIDTH, FOX_WIDTH, FOX_WIDTH, FOX_HEADS,
                 GDN_WIDTH, GDN_WIDTH, GDN_WIDTH, GDN_WIDTH, GDN_HEADS, GDN_HEADS)
IN_PROJ_WIDTH = sum(IN_PROJ_SIZES)
SPLIT_POINTS = tuple(np.cumsum(IN_PROJ_SIZES)[:-1].tolist())
MEM_HEADS = 4
MEM_HEAD_DIM = D_MODEL // MEM_HEADS
D_FF = 2816
FFN_RESIDUAL_WEIGHT = 0.5


def rms_norm_2(x, gain):
    xf = x.astype(jnp.float32)
    y = xf * lax.rsqrt(jnp.mean(xf * xf, axis=-1, keepdims=True) + EPS)
    return (y * gain.astype(jnp.float32)).astype(x.dtype)

def l2_norm(x):
    return x * lax.rsqrt(jnp.sum(x * x, axis=-1, keepdims=True) + EPS)

def swiglu(x, w_gate, w_up, w_down):
    return (jax.nn.silu(x @ w_gate) * (x @ w_up)) @ w_down

def forgetting_attention(q, k, v, f_logit):
    B, S, H, Dh = q.shape
    nb = S // Q_BLOCK
    F = jnp.cumsum(jax.nn.log_sigmoid(f_logit.astype(jnp.float32)), axis=1).transpose(0, 2, 1)
    qb = (q * (Dh ** -0.5)).reshape(B, nb, Q_BLOCK, H, Dh).transpose(1, 0, 3, 2, 4)
    Fq = F.reshape(B, H, nb, Q_BLOCK).transpose(2, 0, 1, 3)
    q_pos = jnp.arange(S).reshape(nb, Q_BLOCK)
    k_pos = jnp.arange(S)

    def block(args):
        q_blk, F_blk, pos_blk = args
        s = jnp.einsum('bhqd,bshd->bhqs', q_blk, k, preferred_element_type=jnp.float32)
        s = s + F_blk[..., None] - F[:, :, None, :]
        s = jnp.where(pos_blk[:, None] >= k_pos[None, :], s, -jnp.inf)
        p = jax.nn.softmax(s, axis=-1).astype(v.dtype)
        return jnp.einsum('bhqs,bshd->bqhd', p, v)

    out = lax.map(block, (qb, Fq, q_pos))
    return out.transpose(1, 0, 2, 3, 4).reshape(B, S, H * Dh)

def causal_conv_silu(x, w):
    S = x.shape[1]
    xp = jnp.pad(x, ((0, 0), (CONV_WIDTH - 1, 0), (0, 0)))
    y = xp[:, 0:S] * w[0]
    for i in range(1, CONV_WIDTH):
        y = y + xp[:, i:i + S] * w[i]
    return jax.nn.silu(y)

def gated_delta_rule_chunked(q, k, v, g, beta):
    B, S, H, Dk = q.shape
    Dv = v.shape[-1]
    n = S // CHUNK_2

    def chunks(t):
        return t.reshape(B, n, CHUNK_2, H, -1).transpose(0, 3, 1, 2, 4)

    q = chunks(q) * (Dk ** -0.5)
    k = chunks(k)
    v = chunks(v)
    beta = beta.reshape(B, n, CHUNK_2, H).transpose(0, 3, 1, 2)
    g = jnp.cumsum(g.reshape(B, n, CHUNK_2, H).transpose(0, 3, 1, 2), axis=-1)
    k_beta = k * beta[..., None]
    v_beta = v * beta[..., None]
    incl = jnp.tril(jnp.ones((CHUNK_2, CHUNK_2), dtype=bool))
    strict = jnp.tril(jnp.ones((CHUNK_2, CHUNK_2), dtype=bool), -1)
    decay = jnp.exp(jnp.where(incl, g[..., :, None] - g[..., None, :], -jnp.inf))
    L = jnp.where(strict, jnp.einsum('bhncd,bhnsd->bhncs', k_beta, k) * decay, 0.0)
    A = L + jnp.eye(CHUNK_2, dtype=L.dtype)
    u = lax.linalg.triangular_solve(A, v_beta, left_side=True, lower=True)
    w = lax.linalg.triangular_solve(A, k_beta * jnp.exp(g)[..., None], left_side=True, lower=True)
    attn_intra = jnp.einsum('bhncd,bhnsd->bhncs', q, k) * decay
    q_decay = q * jnp.exp(g)[..., None]
    g_last = g[..., -1]
    k_tail = k * jnp.exp(g_last[..., None] - g)[..., None]

    def step(state, xs):
        w_c, u_c, qd_c, a_c, kt_c, gl_c = xs
        v_new = u_c - jnp.einsum('bhcd,bhde->bhce', w_c, state)
        o = jnp.einsum('bhcd,bhde->bhce', qd_c, state) + jnp.einsum('bhcs,bhse->bhce', a_c, v_new)
        state = state * jnp.exp(gl_c)[..., None, None] + jnp.einsum('bhcd,bhce->bhde', kt_c, v_new)
        return state, o

    xs = (jnp.moveaxis(w, 2, 0), jnp.moveaxis(u, 2, 0), jnp.moveaxis(q_decay, 2, 0),
          jnp.moveaxis(attn_intra, 2, 0), jnp.moveaxis(k_tail, 2, 0), jnp.moveaxis(g_last, 2, 0))
    state0 = jnp.zeros((B, H, Dk, Dv), jnp.float32)
    _, o = lax.scan(step, state0, xs)
    return o.transpose(1, 0, 3, 2, 4).reshape(B, S, H, Dv)

def hybrid_mixer(u, w_in, fox_f_bias, gdn_conv_w, gdn_a_log, gdn_dt_bias, gdn_out_norm):
    B, S, _ = u.shape
    proj = u @ w_in
    fq, fk, fv, ff, gq, gk, gv, gz, gb, ga = jnp.split(proj, SPLIT_POINTS, axis=-1)
    fox = forgetting_attention(fq.reshape(B, S, FOX_HEADS, FOX_HEAD_DIM),
                               fk.reshape(B, S, FOX_HEADS, FOX_HEAD_DIM),
                               fv.reshape(B, S, FOX_HEADS, FOX_HEAD_DIM),
                               ff + fox_f_bias)
    qkv = causal_conv_silu(jnp.concatenate([gq, gk, gv], axis=-1).astype(jnp.float32),
                           gdn_conv_w.astype(jnp.float32))
    cq, ck, cv = jnp.split(qkv, (GDN_WIDTH, 2 * GDN_WIDTH), axis=-1)
    q = l2_norm(cq.reshape(B, S, GDN_HEADS, GDN_HEAD_DIM))
    k = l2_norm(ck.reshape(B, S, GDN_HEADS, GDN_HEAD_DIM))
    v = cv.reshape(B, S, GDN_HEADS, GDN_HEAD_DIM)
    beta = jax.nn.sigmoid(gb.astype(jnp.float32))
    g = -jnp.exp(gdn_a_log.astype(jnp.float32)) * jax.nn.softplus(
        ga.astype(jnp.float32) + gdn_dt_bias.astype(jnp.float32))
    o = gated_delta_rule_chunked(q, k, v, g, beta)
    o = rms_norm_2(o, gdn_out_norm) * jax.nn.silu(
        gz.astype(jnp.float32).reshape(B, S, GDN_HEADS, GDN_HEAD_DIM))
    gdn = o.reshape(B, S, GDN_WIDTH).astype(u.dtype)
    return jnp.concatenate([fox.astype(u.dtype), gdn], axis=-1)

def memory_cross_attention(h, m, w_q, w_kv, w_o):
    B, S, _ = h.shape
    q = (h @ w_q).reshape(B, S, MEM_HEADS, MEM_HEAD_DIM)
    k, v = jnp.split(m @ w_kv, 2, axis=-1)
    k = k.reshape(B, -1, MEM_HEADS, MEM_HEAD_DIM)
    v = v.reshape(B, -1, MEM_HEADS, MEM_HEAD_DIM)
    s = jnp.einsum('bqhd,bmhd->bhqm', q, k, preferred_element_type=jnp.float32) * (MEM_HEAD_DIM ** -0.5)
    p = jax.nn.softmax(s, axis=-1).astype(v.dtype)
    o = jnp.einsum('bhqm,bmhd->bqhd', p, v).reshape(B, S, D_MODEL)
    return o @ w_o

def second_inputs(seed: int = 0) -> dict:
    key = jax.random.key(seed)
    ks = iter(jax.random.split(key, 40))

    def normal(shape, scale):
        return jax.random.normal(next(ks), shape, jnp.float32) * scale

    def gain(width):
        return 1.0 + normal((DEPTH_2, width), 0.02)

    L = DEPTH_2
    dt = jnp.exp(jax.random.uniform(next(ks), (L, GDN_HEADS), jnp.float32,
                                    minval=float(np.log(1e-3)), maxval=float(np.log(1e-1))))
    return {
        'x': normal((BATCH, SEQ, D_MODEL), 1.0),
        'mem': normal((BATCH, N_MEM, D_MODEL), 1.0),
        'ffn1_pre_norm': gain(D_MODEL),
        'ffn1_w_gate': normal((L, D_MODEL, D_FF), D_MODEL ** -0.5),
        'ffn1_w_up': normal((L, D_MODEL, D_FF), D_MODEL ** -0.5),
        'ffn1_w_down': normal((L, D_FF, D_MODEL), D_FF ** -0.5),
        'ffn1_post_norm': gain(D_MODEL),
        'mix_pre_norm': gain(D_MODEL),
        'w_in': normal((L, D_MODEL, IN_PROJ_WIDTH), D_MODEL ** -0.5),
        'fox_f_bias': jax.random.uniform(next(ks), (L, FOX_HEADS), jnp.float32, minval=1.0, maxval=4.0),
        'gdn_conv_w': normal((L, CONV_WIDTH, 3 * GDN_WIDTH), CONV_WIDTH ** -0.5),
        'gdn_a_log': jnp.log(jax.random.uniform(next(ks), (L, GDN_HEADS), jnp.float32, minval=1.0, maxval=16.0)),
        'gdn_dt_bias': dt + jnp.log(-jnp.expm1(-dt)),
        'gdn_out_norm': gain(GDN_HEAD_DIM),
        'w_out': normal((L, MIX_WIDTH, D_MODEL), MIX_WIDTH ** -0.5),
        'mix_post_norm': gain(D_MODEL),
        'mem_pre_norm': gain(D_MODEL),
        'mem_kv_norm': gain(D_MODEL),
        'mem_w_q': normal((L, D_MODEL, D_MODEL), D_MODEL ** -0.5),
        'mem_w_kv': normal((L, D_MODEL, 2 * D_MODEL), D_MODEL ** -0.5),
        'mem_w_o': normal((L, D_MODEL, D_MODEL), D_MODEL ** -0.5),
        'mem_post_norm': gain(D_MODEL),
        'ffn2_pre_norm': gain(D_MODEL),
        'ffn2_w_gate': normal((L, D_MODEL, D_FF), D_MODEL ** -0.5),
        'ffn2_w_up': normal((L, D_MODEL, D_FF), D_MODEL ** -0.5),
        'ffn2_w_down': normal((L, D_FF, D_MODEL), D_FF ** -0.5),
        'ffn2_post_norm': gain(D_MODEL),
    }

def second_block(x, mem, ffn1_pre_norm, ffn1_w_gate, ffn1_w_up, ffn1_w_down, ffn1_post_norm,
              mix_pre_norm, w_in, fox_f_bias, gdn_conv_w, gdn_a_log, gdn_dt_bias, gdn_out_norm,
              w_out, mix_post_norm, mem_pre_norm, mem_kv_norm, mem_w_q, mem_w_kv, mem_w_o,
              mem_post_norm, ffn2_pre_norm, ffn2_w_gate, ffn2_w_up, ffn2_w_down, ffn2_post_norm):
    h = x
    for l in range(DEPTH_2):
        f = swiglu(rms_norm_2(h, ffn1_pre_norm[l]), ffn1_w_gate[l], ffn1_w_up[l], ffn1_w_down[l])
        h = h + FFN_RESIDUAL_WEIGHT * rms_norm_2(f, ffn1_post_norm[l])
        mixed = hybrid_mixer(rms_norm_2(h, mix_pre_norm[l]), w_in[l], fox_f_bias[l], gdn_conv_w[l],
                             gdn_a_log[l], gdn_dt_bias[l], gdn_out_norm[l])
        h = h + rms_norm_2(mixed @ w_out[l], mix_post_norm[l])
        c = memory_cross_attention(rms_norm_2(h, mem_pre_norm[l]), rms_norm_2(mem, mem_kv_norm[l]),
                                   mem_w_q[l], mem_w_kv[l], mem_w_o[l])
        h = h + rms_norm_2(c, mem_post_norm[l])
        f = swiglu(rms_norm_2(h, ffn2_pre_norm[l]), ffn2_w_gate[l], ffn2_w_up[l], ffn2_w_down[l])
        h = h + FFN_RESIDUAL_WEIGHT * rms_norm_2(f, ffn2_post_norm[l])
    return h


def setup_inputs(seed=0):
    out = dict(first_inputs(seed))
    for name, value in second_inputs(seed + 1).items():
        if name != "x":
            out[name + "_2"] = value
    return out


def reference(
    x, norm_w, a_w_in, a_ln_w, a_ln_b, a_w_s, a_b_s, a_w_out, b_w_in, b_conv_w, b_conv_b,
    b_gate_a_w, b_gate_a_b, b_gate_x_w, b_gate_x_b, b_lambda, b_w_out, norm_f_w, mem_2,
    ffn1_pre_norm_2, ffn1_w_gate_2, ffn1_w_up_2, ffn1_w_down_2, ffn1_post_norm_2,
    mix_pre_norm_2, w_in_2, fox_f_bias_2, gdn_conv_w_2, gdn_a_log_2, gdn_dt_bias_2,
    gdn_out_norm_2, w_out_2, mix_post_norm_2, mem_pre_norm_2, mem_kv_norm_2, mem_w_q_2,
    mem_w_kv_2, mem_w_o_2, mem_post_norm_2, ffn2_pre_norm_2, ffn2_w_gate_2, ffn2_w_up_2,
    ffn2_w_down_2, ffn2_post_norm_2,
):
    x = first_block(
        x, norm_w, a_w_in, a_ln_w, a_ln_b, a_w_s, a_b_s, a_w_out, b_w_in, b_conv_w, b_conv_b,
        b_gate_a_w, b_gate_a_b, b_gate_x_w, b_gate_x_b, b_lambda, b_w_out, norm_f_w,
    )
    return second_block(
        x, mem_2, ffn1_pre_norm_2, ffn1_w_gate_2, ffn1_w_up_2, ffn1_w_down_2, ffn1_post_norm_2,
        mix_pre_norm_2, w_in_2, fox_f_bias_2, gdn_conv_w_2, gdn_a_log_2, gdn_dt_bias_2,
        gdn_out_norm_2, w_out_2, mix_post_norm_2, mem_pre_norm_2, mem_kv_norm_2, mem_w_q_2,
        mem_w_kv_2, mem_w_o_2, mem_post_norm_2, ffn2_pre_norm_2, ffn2_w_gate_2, ffn2_w_up_2,
        ffn2_w_down_2, ffn2_post_norm_2,
    )


_drawn_inputs = setup_inputs


def setup_inputs(seed=0):
    import zlib

    import numpy as np

    out = dict(_drawn_inputs(seed))
    spreads = {}
    factors = {'a_ln_w': 3.056,
     'a_ln_b': 7.842,
     'b_gate_a_b': 8.0,
     'b_gate_x_b': 8.0,
     'ffn1_pre_norm_2': 3.209,
     'ffn1_post_norm_2': 4.552,
     'gdn_out_norm_2': 5.106,
     'mix_post_norm_2': 4.205,
     'mem_pre_norm_2': 4.91,
     'mem_kv_norm_2': 3.409,
     'mem_post_norm_2': 17.773,
     'ffn2_pre_norm_2': 87.209,
     'ffn2_post_norm_2': 158.943}
    for name, (base, spread) in spreads.items():
        noise = np.random.default_rng([zlib.crc32(name.encode()), seed]).standard_normal(out[name].shape)
        drawn = base * np.exp(spread * noise) if base else spread * noise
        out[name] = __import__('jax').numpy.asarray(drawn.astype(out[name].dtype))
    for name, factor in factors.items():
        out[name] = (out[name] * factor).astype(out[name].dtype)
    return out
```

```python
from contextlib import ExitStack

import numpy as np

import concourse.bass as bass
from concourse import mybir

F32 = mybir.dt.float32
F32R = mybir.dt.float32r
I32 = mybir.dt.int32
ALU = mybir.AluOpType
ACT = mybir.ActivationFunctionType
AX = mybir.AxisListType

P = 128
SEQ = 512
TOK = SEQ // P
D = 1024
KD = D // P
AW = 2048
KA = AW // P
AG = 8
BW = 1536
KB = BW // P
FF = 2816
KF = FF // P
FOXH, FOXD = 8, 64
GH, GD = 4, 128
CH = 64
MEM = 256
KM = MEM // P
MH, MHD = 4, 256
RMS_EPS = 1e-6
LN_EPS = 1e-5
KIB = 1024

UNITS = {16: (4, 4, 4, 4), 12: (3, 3, 3, 3), 22: (6, 6, 5, 5), 4: (1, 1, 1, 1)}
SLOT = (0, 6, 12, 17)
RMAX = 22

VEC_SIZES = (
    ("norm0", KD), ("norm1", KD), ("normf", KD), ("a_ln_w", KA), ("a_ln_b", KA),
    ("conv", 4 * KB), ("conv_b", KB), ("gate_a_b", KB), ("gate_x_b", KB), ("lam", KB),
    ("ffn1_pre", KD), ("ffn1_post", KD), ("mix_pre", KD), ("mix_post", KD),
    ("gconv", 4 * 3 * GH), ("out_norm", 1), ("mem_pre", KD), ("mem_kv", KD), ("mem_post", KD),
    ("ffn2_pre", KD), ("ffn2_post", KD), ("small_bias", 1), ("a_log", 1),
)
VEC = {}
_at = 0
for _name, _n in VEC_SIZES:
    VEC[_name] = _at
    _at += _n
NVEC = _at


class Phase:

    def __init__(self, name, rounds, tiles):
        self.name, self.rounds, self.tiles = name, rounds, tiles
        self.units = UNITS[tiles]
        self.base = 0

    def used(self, r, j):
        return 4 * (self.base + r) + j + 1


PHASES = [
    Phase("a_v", 8, 16), Phase("a_ug", 16, 16), Phase("a_out", 8, 16),
    Phase("b_in", 12, 16), Phase("b_out", 8, 12),
    Phase("ffn1_up", 22, 16), Phase("ffn1_down", 8, 22),
    Phase("fox_v", 2, 16), Phase("fox_qk", 4, 16), Phase("small", 2, 4),
    Phase("gdn_qkv", 6, 16), Phase("gdn_z", 2, 16), Phase("mix_out", 4, 16),
    Phase("mem_k", 4, 16), Phase("mem_v", 4, 16), Phase("mem_q", 4, 16), Phase("mem_o", 4, 16),
    Phase("ffn2_up", 22, 16), Phase("ffn2_down", 8, 22),
]
PH = {ph.name: ph for ph in PHASES}


def number(phases):
    base = 0
    for ph in phases:
        ph.base = base
        base += ph.rounds
        assert ph.rounds % 2 == 0


def rounds(eng, ph, body, step=None):
    before = step.n if step else 0
    for parity in range(2):
        body(parity, parity, 0)
    if ph.rounds > 2:
        per_pair = step.n - before if step else 0
        with eng.Fori(1, ph.rounds // 2) as pair:
            if per_pair:
                step.at = pair * per_pair + before
            for parity in range(2):
                body(pair * 2 + parity, parity, pair)
        if step:
            assert step.n == before + 2 * per_pair, "a pair's steps differ from the peeled pair's"
            step.at = step.n = before + per_pair * (ph.rounds // 2)


def wait_alone(eng, sem, value, passed):
    eng.wait_ge(sem, value)
    if not isinstance(value, int):
        eng.sem_inc(passed, 1)


def _members(kind, *parts):
    return [(f"{name}_{kind}", n) for name, n in parts]


STATS = ("s0", 1), ("s1", 1), ("s2", 1), ("s2b", 1), ("f1", 1), ("s3", 1), ("mx", 1), ("m", 1), ("s4", 1), ("mo", 1), ("s5", 1), ("f2", 1)
SPLITS = ("s0", KD), ("s1", KD), ("s2", KD), ("s3", KD), ("m", KD), ("s4", KD), ("s5", KD)
SQUARES = ("s0", KD), ("s1", KD), ("s2", 2 * KD), ("s3", KD), ("m", KD), ("s4", KD), ("s5", KD)
BRANCHES = ("f1", KD), ("mx", KD), ("mo", KD), ("f2", KD)
FFNS = ("a", KA), ("ffn1", KF), ("ffn2", KF)
SHARED = [
    _members("sum", *(s for s in STATS if s[0] != "s2b")), _members("diag", *STATS), _members("rows", *STATS), _members("rb", *STATS),
    _members("hi", *SPLITS), _members("lo", *SPLITS), _members("sq", *SQUARES), _members("added", *SQUARES),
    *(_members(kind, *BRANCHES) for kind in ("f", "sq", "added", "x")),
    *(_members(kind, *FFNS) for kind in ("tg", "tu", "y", "yh", "yl")),
    _members("sg", *FFNS[1:]), _members("neg", ("lam", 1), ("rows", 1)), _members("exp", ("lam", 1), ("rows", 1)),
    *(_members(kind, ("gl", 2 * GH), ("go", GH)) for kind in ("sq", "sums", "diags", "spread", "scaled")),
    *([(f"b_{b}", n * KB), (f"g_{g}", n * 3 * GH)] for b, g, n in (("xb", "xb", 1), ("xc0", "c0", 1), ("taps", "taps", 2), ("xc", "conv", 1))),
    *(_members(kind, ("fx", FOXH * TOK), ("ma", MH * TOK)) for kind in ("s", "nm", "e", "p", "t", "pt")),
    [("fx_o", FOXH), ("ma_o", 2 * MH)], [("fx_hi", FOXH // 2), ("ma_hi", 2 * MH)], [("fx_lo", FOXH // 2), ("ma_lo", 2 * MH)],
]


class Sems:

    def __init__(self, nc, ctx):
        self.nc, self.ctx, self.made, self.key, self.start = nc, ctx, {}, {}, {}
        for members in SHARED:
            total = 0
            for name, n in members:
                self.key[name], self.start[name] = members[0][0], total
                total += n

    def __call__(self, name):
        key = self.key.get(name, name)
        if key not in self.made:
            self.made[key] = self.ctx.enter_context(self.nc.semaphore(key))
        return self.made[key]

    def due(self, name, value):
        return self(name), value + self.start.get(name, 0)


class Chain:

    def __init__(self, eng, sem):
        self.eng, self.sem, self.at, self.n = eng, sem, 0, 0

    def __call__(self, instruction):
        instruction.then_inc(self.sem, 1)
        self.at = self.at + 1
        self.n += 1
        self.eng.wait_ge(self.sem, self.at)


def first(r):
    return isinstance(r, int) and r == 0


def build(nc, dram, out, phases=PHASES, dump=None):
    number(phases)
    active = {ph.name for ph in phases}
    ctx = ExitStack()
    with ctx:
        base = 16640

        def place(name, at_kib, shape, dt=F32):
            return nc.alloc_sbuf_tensor_at(name, [P] + shape, dt, offset=base + int(at_kib * KIB))

        X = place("residual", 0, [KD, SEQ])
        XH = place("x_hi", 16, [KD, SEQ], F32R)
        XL = place("x_lo", 32, [KD, SEQ], F32R)
        F = place("branch_out", 32, [KD, SEQ])
        YAT = 48
        RAW = place("raw_weights", 144, [2, RMAX, P])
        WH = place("weights_hi", 166, [RMAX, P], F32R)
        WL = place("weights_lo", 177, [RMAX, P], F32R)
        T = place("temps", 188, [7, SEQ])
        RB = place("rms_rows", 202, [SEQ])
        IDENT = place("ident", 204, [P])
        ONES = place("ones", 204.5, [P])
        V_ = place("vecs", 205, [NVEC])
        SM = place("small_cols", 206.5, [64])
        SC = place("scratch_cols", 206.75, [128])
        assert NVEC * 4 <= 1536

        def vec(name, k=0):
            return V_[:, bass.ds(VEC[name] + k, 1)] if not isinstance(k, int) else V_[:, VEC[name] + k:VEC[name] + k + 1]

        PS = [ctx.enter_context(nc.psum_tensor(f"bank{i}", [P, SEQ], F32))[:, :] for i in range(8)]

        S = Sems(nc, ctx)
        due = S.due
        units_ready, units_used = S("units_ready"), S("units_used")

        def wait(eng, sem, value):
            wait_alone(eng, sem, value, S("scalar_passed") if eng is nc.scalar else S("gpsimd_passed"))

        A_X = place("a_x", YAT, [KD, SEQ])
        A_YH = place("a_y_hi", YAT, [KA, SEQ], F32R)
        A_YL = place("a_y_lo", YAT + 32, [KA, SEQ], F32R)
        A_V = place("a_v", YAT + 64, [TOK, AW])
        A_WS = place("a_w_s", 0, [AG, P])
        A_RS = place("a_row_sums", 4, [AG, P])
        A_BS = place("a_b_s", 8, [AG, P])
        A_VN = place("a_v_normed", 12, [2, TOK, P])
        B_YH = place("b_y_hi", YAT, [KB, SEQ], F32R)
        B_YL = place("b_y_lo", YAT + 24, [KB, SEQ], F32R)
        B_GW = place("b_gate_w", YAT + 48, [KB, 2, P])
        B_ST = place("b_gate_stage", YAT + 60, [2, 2, P])
        B_XB = place("b_xb", YAT + 62, [2, SEQ + 8])
        B_XC = place("b_xc", YAT + 66.5, [2, SEQ])
        B_TG = place("b_tg", YAT + 70.5, [2, SEQ])
        B_TMP = place("b_temps", YAT + 74.5, [10, SEQ])
        Y_H = place("ffn_y_hi", YAT, [KF, SEQ], F32R)
        Y_L = place("ffn_y_lo", YAT + 44, [KF, SEQ], F32R)

        def sp_loads(sp):
            for ph in phases:
                src = dram[ph.name]

                def body(r, parity, pair, ph=ph, src=src):
                    first_rounds = isinstance(r, int) and ph.base + r < 2
                    if not first_rounds:
                        sp.wait_ge(units_ready, 4 * (ph.base - 1) + 4 * r)
                    sp.dma_start(RAW[:, parity, 0:ph.tiles, :].rearrange("p t n -> p (t n)"), src[r]).then_inc(S(f"raw{parity}"), 16)
                rounds(sp, ph, body)

        def pool_split(pool):
            for ph in phases:
                if ph.name == "a_ug":
                    pool_causal_w_s(pool)
                elif ph.name == "fox_v":
                    pool_masks(pool)
                elif ph.name == "mix_out":
                    pool_levels(pool)

                def body(r, parity, pair, ph=ph):
                    pool.wait_ge(*due(f"raw{parity}", pair * 16 + (8 * ph.base + 16)))
                    at = 0
                    for j, n in enumerate(ph.units):
                        hi, lo = WH[:, SLOT[j]:SLOT[j] + n, :], WL[:, SLOT[j]:SLOT[j] + n, :]
                        raw = RAW[:, parity, at:at + n, :]
                        at += n
                        if not (isinstance(r, int) and ph.base + r == 0):
                            wait(pool, units_used, 4 * (ph.base - 1) + j + 1 + 4 * r)
                        nc.gpsimd.tensor_scalar(hi, raw, 1.0, 0.0, ALU.mult, ALU.add).then_inc(S("units_hi"), 1)
                        pool.wait_ge(*due("units_hi", 4 * ph.base + j + 1 + 4 * r))
                        nc.gpsimd.tensor_tensor(lo, raw, hi.bitcast(F32), ALU.subtract).then_inc(units_ready, 1)
                rounds(pool, ph, body)

        def feature_tile(pe, ph, r, js, ps, xh, xl, ready=None):
            k, last_k = 0, sum(ph.units[j] for j in js) - 1
            for j in js:
                pe.wait_ge(units_ready, ph.used(r, j))
                for t in range(ph.units[j]):
                    if ready:
                        ready(k)
                    wh, wl = WH[:, SLOT[j] + t, :], WL[:, SLOT[j] + t, :]
                    nc.tensor.matmul(ps, wh, xh[:, k, :], start=k == 0, stop=False)
                    nc.tensor.matmul(ps, wl, xh[:, k, :], start=False, stop=False)
                    last = nc.tensor.matmul(ps, wh, xl[:, k, :], start=False, stop=k == last_k)
                    k += 1
                last.then_inc(units_used, 1)

        def token_tiles(pe, ph, r, parity, banks, xh, xl, ready=None, free=None):
            for j in range(4):
                k = 4 * parity + j
                pe.wait_ge(units_ready, ph.used(r, j))
                if ready:
                    ready(k)
                wh = WH[:, SLOT[j]:SLOT[j] + 4, :].rearrange("p t n -> p (t n)")
                wl = WL[:, SLOT[j]:SLOT[j] + 4, :].rearrange("p t n -> p (t n)")
                for i, bank in enumerate(banks):
                    if k == 0 and free:
                        free(i)
                    tok = slice(i * P, (i + 1) * P)
                    nc.tensor.matmul(bank, xh[:, k, tok], wh, start=k == 0, stop=False)
                    nc.tensor.matmul(bank, xh[:, k, tok], wl, start=False, stop=False)
                    last = nc.tensor.matmul(bank, xl[:, k, tok], wh, start=False, stop=k == KD - 1)
                last.then_inc(units_used, 1)

        def bank_free(pe, name, r):
            if not (isinstance(r, int) and r < 2):
                pe.wait_ge(*due(name, r - 1))

        def pe_sum(pe, name, acc, ps, count=KD, ntok=TOK):
            pe.wait_ge(*due(f"{name}_added", count))
            for i in range(ntok):
                last = nc.tensor.matmul(ps[:, i:i + 1], acc[:, i * P:(i + 1) * P], ONES[:, 0:1], start=True, stop=True)
            last.then_inc(S(f"{name}_sum"), 1)

        def pe_spread(pe, name, diag, ps, n=SEQ):
            pe.wait_ge(*due(f"{name}_diag", 1))
            nc.tensor.matmul(ps[:, 0:n], ONES[:, :], diag, start=True, stop=True).then_inc(S(f"{name}_rows"), 1)

        def inverse_root(step, out_, x, scratch):
            y, z, w = scratch
            step(nc.vector.tensor_scalar(y.bitcast(I32), x.bitcast(I32), -0.5, float(0x5F3759DF), ALU.mult, ALU.add))
            step(nc.vector.tensor_scalar(w, x, -0.5, None, ALU.mult))
            for i in range(3):
                step(nc.vector.tensor_tensor(z, y, y, ALU.mult))
                step(nc.vector.tensor_tensor(z, z, w, ALU.mult))
                step(nc.vector.scalar_tensor_tensor(out=out_ if i == 2 else y, in0=z, scalar=1.5, in1=y, op0=ALU.add, op1=ALU.mult))

        def scratch(n, k=3):
            return [SC[:, i * 32:i * 32 + n] for i in range(k)]

        def dve_column(dve, step, name, ps, col, width, eps, n=TOK):
            dve.wait_ge(*due(f"{name}_sum", 1))
            x = SC[:, 96:96 + n]
            step(nc.vector.tensor_scalar(x, ps, 1.0 / width, eps, ALU.mult, ALU.add))
            inverse_root(step, col, x, scratch(n))

        def dve_diag(dve, step, name, col, diag, n=TOK):
            nc.vector.tensor_tensor(
                diag.rearrange("p (a b) -> p a b", b=P),
                IDENT[:, :].unsqueeze(1).to_broadcast([P, n, P]),
                col.unsqueeze(2).to_broadcast([P, n, P]), ALU.mult).then_inc(S(f"{name}_diag"), 1)

        def act_split(act, name, k, parity, src, gain, ready, sq_scales=(None,)):
            ready()
            n = len(sq_scales)
            nc.scalar.activation(XH[:, k, :], src, ACT.Copy, scale=gain).then_inc(S(f"{name}_hi"), 1)
            for q, sc in enumerate(sq_scales):
                if not (isinstance(k, int) and k < 2):
                    wait(act, *due(f"{name}_added", (k - 1) * n))
                kw = {} if sc is None else {"scale": sc}
                nc.scalar.activation(T[:, 2 * q + parity, :], src, ACT.Square, **kw).then_inc(S(f"{name}_sq"), 1)

        def dve_split(dve, name, k, parity, src, gain, accs):
            dve.wait_ge(*due(f"{name}_hi", k + 1))
            nc.vector.scalar_tensor_tensor(out=XL[:, k, :], in0=src, scalar=gain, in1=XH[:, k, :].bitcast(F32), op0=ALU.mult, op1=ALU.subtract).then_inc(S(f"{name}_lo"), 1)
            n = len(accs)
            for q, acc in enumerate(accs):
                dve.wait_ge(*due(f"{name}_sq", k * n + (q + 1)))
                sq = T[:, 2 * q + parity, :]
                if first(k):
                    nc.vector.tensor_copy(acc, sq).then_inc(S(f"{name}_added"), 1)
                else:
                    dve.wait_ge(*due(f"{name}_added", (k - 1) * n + q + 1))
                    nc.vector.tensor_tensor(acc, acc, sq, ALU.add).then_inc(S(f"{name}_added"), 1)

        def x_gate(pe, name, on=lambda r: first(r)):
            return lambda k: pe.wait_ge(*due(f"{name}_lo", k + 1))

        ACC, ACC2, DIAG = T[:, 4, :], T[:, 5, :], T[:, 6, :]

        def act_rows(act, name, ps, dst, n=SEQ):
            wait(act, *due(f"{name}_rows", 1))
            nc.scalar.activation(dst, ps[:, 0:n], ACT.Copy).then_inc(S(f"{name}_rb"), 1)

        PV, PU, PO = PH["a_v"], PH["a_ug"], PH["a_out"]
        COL = SM[:, 0:4]
        MV = SM[:, 8:16].rearrange("p (t c) -> p t c", c=2)
        RSTD = SM[:, 16:20]

        def act_setup(act):
            for i in range(4):
                act.dma_start(A_X[:, 2 * i:2 * i + 2, :], dram["x"][:, 2 * i:2 * i + 2, :]).then_inc(S(f"x_in{i}"), 16)
                if i == 0:
                    act.dma_start(V_[:, :], dram["vecs"]).then_inc(S("vecs_in"), 16)
            act.dma_start(A_WS[:, :, :], dram["a_w_s"]).then_inc(S("ws_in"), 16)
            act.dma_start(A_BS[:, :, :].rearrange("p g t -> p (g t)"), dram["a_b_s"].partition_broadcast(P)).then_inc(S("bs_in"), 16)
            wait(act, *due("vecs_in", 16))
            for k in range(KD):
                act_split(act, "s0", k, k % 2, A_X[:, k, :], vec("norm0", k), lambda: wait(act, *due(f"x_in{k // 2}", 16)))

        def dve_setup(dve, step):
            nc.vector.memset(ONES[:, :], 1.0).then_inc(S("ones"), 1)
            dve.wait_ge(*due("vecs_in", 16))
            for k in range(KD):
                dve.wait_ge(*due(f"x_in{k // 2}", 16))
                dve_split(dve, "s0", k, k % 2, A_X[:, k, :], vec("norm0", k), [ACC])
            dve.wait_ge(*due("ident", 2))
            dve_column(dve, step, "s0", PS[7][:, 0:4], COL, D, RMS_EPS)
            dve_diag(dve, step, "s0", COL, DIAG)

        def pool_setup(pool):
            nc.gpsimd.memset(IDENT[:, :], 0.0).then_inc(S("ident"), 1)
            pool.wait_ge(*due("ident", 1))
            nc.gpsimd.affine_select(out=IDENT[:, :], in_=IDENT[:, :], compare_op=ALU.not_equal, fill=1.0, base=0,
                                    pattern=[[-1, P]], channel_multiplier=1).then_inc(S("ident"), 1)

        def pool_causal_w_s(pool):
            pool.wait_ge(*due("ws_in", 16))
            nc.gpsimd.affine_select(out=A_WS[:, :, :], in_=A_WS[:, :, :], compare_op=ALU.is_ge, fill=0.0, base=0,
                                    pattern=[[0, AG], [1, P]], channel_multiplier=-1).then_inc(S("ws_causal"), 1)

        def pe_a_v(pe):
            def body(r, parity, pair):
                def ready(k):
                    if isinstance(r, int) and r < 2:
                        pe.wait_ge(*due("s0_lo", k + 1))

                def free(i):
                    if not isinstance(r, int):
                        pe.wait_ge(*due("a_v_free", pair * 4 + (i - 3)))
                token_tiles(pe, PV, r, parity, PS[0:4], XH, XL, ready, free)
                if first(r):
                    pe.wait_ge(*due("ones", 1))
                    pe_sum(pe, "s0", ACC, PS[7])
                elif isinstance(r, int):
                    pe_spread(pe, "s0", DIAG, PS[6])
            rounds(pe, PV, body)

        def act_a_v(act):
            def body(r, parity, pair):
                if parity:
                    if isinstance(r, int):
                        wait(act, *due("s0_diag", 1))
                    wait(act, units_used, PV.used(r, 3))
                    for i in range(TOK):
                        nc.scalar.activation(A_V[:, i, bass.ds(pair * SEQ, SEQ)], PS[i], ACT.Gelu_apprx_tanh, scale=COL[:, i:i + 1]).then_inc(S("a_v_free"), 1)
                    if isinstance(r, int):
                        act_rows(act, "s0", PS[6], RB[:, :])
            rounds(act, PV, body)

        def dve_a_v(dve, step):
            BN = T[:, 5, 0:96].rearrange("p (t b s) -> p t b s", t=TOK, s=6)

            def body(r, parity, pair):
                if parity:
                    for i in range(TOK):
                        dve.wait_ge(*due("a_v_free", pair * 4 + (i + 1)))
                        step(nc.vector.bn_stats(BN[:, i, pair, :], A_V[:, i, bass.ds(pair * SEQ, SEQ)]))
            rounds(dve, PV, body, step)
            for i in range(TOK):
                step(nc.vector.bn_aggr(MV[:, i, :], BN[:, i, :, :].rearrange("p b s -> p (b s)")))
            x = SC[:, 96:100]
            step(nc.vector.tensor_scalar(x, MV[:, :, 1], LN_EPS, None, ALU.add))
            inverse_root(step, RSTD, x, scratch(TOK))

        def pe_a_ug(pe):
            for half in range(2):
                if half == 0:
                    pe.wait_ge(*due("ws_causal", 1))
                    pe.wait_ge(*due("a_v_free", TOK * PV.rounds // 2))
                nc.tensor.matmul(PS[4 + half], ONES[:, :], A_WS[:, 4 * half:4 * half + 4, :].rearrange("p g t -> p (g t)"), start=True, stop=True).then_inc(S("ws_sums"), 1)

            def body(r, parity, pair):
                for i, read in enumerate(("a_tu", "a_tg")):
                    bank_free(pe, read, r)
                    feature_tile(pe, PU, r, (2 * i, 2 * i + 1), PS[2 * parity + i], XH, XL)
                pe.wait_ge(*due("a_vn", r + 1))
                if not (isinstance(r, int) and r < 2):
                    pe.wait_ge(*due("a_s_read", r - 1))
                elif first(r):
                    pe.wait_ge(*due("ws_sums_copied", 2))
                for n in range(TOK):
                    last = nc.tensor.matmul(PS[4 + parity][:, n * P:(n + 1) * P], A_VN[:, parity, n, :], A_WS[:, pair, :], start=True, stop=True)
                last.then_inc(S("a_spatial"), 1)
            rounds(pe, PU, body)

        def act_a_ug(act):
            for half in range(2):
                wait(act, *due("ws_sums", half + 1))
                nc.scalar.activation(A_RS[:, 4 * half:4 * half + 4, :].rearrange("p g t -> p (g t)"), PS[4 + half], ACT.Copy).then_inc(S("ws_sums_copied"), 1)

            def body(r, parity, pair):
                wait(act, *due("a_tu", r + 1))
                nc.scalar.activation(T[:, 3, :], T[:, 0, :], ACT.Gelu_apprx_tanh).then_inc(S("a_gu"), 1)
                wait(act, *due("a_tg", r + 1))
                nc.scalar.activation(T[:, 4, :], T[:, 1, :], ACT.Tanh, scale=0.5).then_inc(S("a_th"), 1)
                wait(act, *due("a_y", r + 1))
                nc.scalar.activation(A_YH[:, r, :], T[:, 5, :], ACT.Copy).then_inc(S("a_yh"), 1)
            rounds(act, PU, body)

        def dve_a_ug(dve, step):
            dve.wait_ge(*due("s0_rb", 1))
            dve.wait_ge(*due("ws_sums_copied", 2))
            dve.wait_ge(*due("bs_in", 16))

            def body(r, parity, pair):
                if not (isinstance(r, int) and r < 2):
                    dve.wait_ge(*due("a_spatial", r - 1))
                for n in range(TOK):
                    last = nc.vector.tensor_scalar(A_VN[:, parity, n, :], A_V[:, n, bass.ds(r * P, P)], MV[:, n, 0:1], RSTD[:, n:n + 1], ALU.subtract, ALU.mult)
                last.then_inc(S("a_vn"), 1)
                dve.wait_ge(units_used, PU.used(r, 1))
                nc.vector.tensor_tensor(T[:, 0, :], PS[2 * parity], RB[:, :], ALU.mult).then_inc(S("a_tu"), 1)
                dve.wait_ge(units_used, PU.used(r, 3))
                nc.vector.tensor_tensor(T[:, 1, :], PS[2 * parity + 1], RB[:, :], ALU.mult).then_inc(S("a_tg"), 1)
                step(nc.vector.scalar_tensor_tensor(out=T[:, 6, 0:P], in0=A_RS[:, pair, :], scalar=vec("a_ln_b", r), in1=A_BS[:, pair, :], op0=ALU.mult, op1=ALU.add))
                dve.wait_ge(*due("a_spatial", r + 1))
                nc.vector.scalar_tensor_tensor(
                    out=T[:, 2, :].rearrange("p (n t) -> p n t", n=TOK), in0=PS[4 + parity].rearrange("p (n t) -> p n t", n=TOK),
                    scalar=vec("a_ln_w", r), in1=T[:, 6, 0:P].unsqueeze(1).to_broadcast([P, TOK, P]), op0=ALU.mult, op1=ALU.add).then_inc(S("a_s_read"), 1)
                dve.wait_ge(*due("a_s_read", r + 1))
                dve.wait_ge(*due("a_gu", r + 1))
                step(nc.vector.tensor_tensor(T[:, 2, :], T[:, 2, :], T[:, 3, :], ALU.mult))
                dve.wait_ge(*due("a_th", r + 1))
                dve.wait_ge(*due("a_tg", r + 1))
                step(nc.vector.scalar_tensor_tensor(out=T[:, 4, :], in0=T[:, 4, :], scalar=1.0, in1=T[:, 1, :], op0=ALU.add, op1=ALU.mult))
                nc.vector.scalar_tensor_tensor(out=T[:, 5, :], in0=T[:, 4, :], scalar=0.5, in1=T[:, 2, :], op0=ALU.mult, op1=ALU.mult).then_inc(S("a_y"), 1)
                dve.wait_ge(*due("a_yh", r + 1))
                nc.vector.tensor_tensor(A_YL[:, r, :], T[:, 5, :], A_YH[:, r, :].bitcast(F32), ALU.subtract).then_inc(S("a_yl"), 1)
            rounds(dve, PU, body, step)

        def pe_a_out(pe):
            pe.wait_ge(*due("a_tg", PU.rounds))

            def body(r, parity, pair):
                bank_free(pe, "a_x", r)
                feature_tile(pe, PO, r, range(4), PS[parity], A_YH, A_YL,
                             (lambda k: pe.wait_ge(*due("a_yl", k + 1))) if first(r) else None)
            rounds(pe, PO, body)

        def act_a_out(act):
            wait(act, *due("a_yl", KA))
            act.dma_start(X[:, :, :], dram["x"]).then_inc(S("x_again"), 16)
            rounds(act, PO, lambda r, parity, pair: act_split(
                act, "s1", r, parity, X[:, r, :], vec("norm1", r), lambda: wait(act, *due("a_x", r + 1))))

        def dve_a_out(dve, step):
            dve.wait_ge(*due("x_again", 16))

            def body(r, parity, pair):
                dve.wait_ge(units_used, PO.used(r, 3))
                nc.vector.tensor_tensor(X[:, r, :], PS[parity], X[:, r, :], ALU.add).then_inc(S("a_x"), 1)
                dve_split(dve, "s1", r, parity, X[:, r, :], vec("norm1", r), [ACC])
            rounds(dve, PO, body)

        PB, PBO = PH["b_in"], PH["b_out"]
        LC = place("lru_cols", 207.25, [4, KB])
        N4, P4, HBA, HBX = (LC[:, i, :] for i in range(4))
        NG = SM[:, 24:32]

        def log1p_exp_neg_abs(dve, step, name, out_, x, e, s2):
            step(nc.vector.tensor_scalar(e, x, -1.0, None, ALU.mult))
            nc.vector.tensor_tensor(e, e, x, ALU.min).then_inc(S(f"{name}_neg"), 1)
            dve.wait_ge(*due(f"{name}_exp", 1))
            step(nc.vector.tensor_scalar(s2, e, 2.0, None, ALU.add))
            step(nc.vector.reciprocal(s2, s2))
            step(nc.vector.tensor_tensor(e, e, s2, ALU.mult))
            step(nc.vector.tensor_tensor(s2, e, e, ALU.mult))
            step(nc.vector.tensor_scalar(out_, s2, 1.0 / 17, None, ALU.mult))
            for n in (15, 13, 11, 9, 7, 5, 3):
                step(nc.vector.scalar_tensor_tensor(out=out_, in0=out_, scalar=1.0 / n, in1=s2, op0=ALU.add, op1=ALU.mult))
            step(nc.vector.scalar_tensor_tensor(out=out_, in0=out_, scalar=1.0, in1=e, op0=ALU.add, op1=ALU.mult))
            step(nc.vector.tensor_scalar(out_, out_, 2.0, None, ALU.mult))

        def act_exp_neg(act, name, e):
            wait(act, *due(f"{name}_neg", 1))
            nc.scalar.activation(e, e, ACT.Exp).then_inc(S(f"{name}_exp"), 1)

        def act_lru_cols(act):
            act_exp_neg(act, "lam", SC[:, 0:KB])

        def dve_lru_cols(dve, step):
            lam = V_[:, VEC["lam"]:VEC["lam"] + KB]
            log1p_exp_neg_abs(dve, step, "lam", P4, lam, SC[:, 0:KB], SC[:, 32:32 + KB])
            t = SC[:, 64:64 + KB]
            step(nc.vector.tensor_scalar(t, lam, -1.0, 0.0, ALU.mult, ALU.max))
            step(nc.vector.tensor_tensor(P4, P4, t, ALU.add))
            step(nc.vector.tensor_scalar(P4, P4, 4.0, None, ALU.mult))
            step(nc.vector.tensor_scalar(N4, P4, -1.0, None, ALU.mult))
            step(nc.vector.tensor_scalar(HBA, V_[:, VEC["gate_a_b"]:VEC["gate_a_b"] + KB], 0.5, None, ALU.mult))
            step(nc.vector.tensor_scalar(HBX, V_[:, VEC["gate_x_b"]:VEC["gate_x_b"] + KB], 0.5, None, ALU.mult))
            nc.vector.tensor_tensor(NG, V_[:, VEC["normf"]:VEC["normf"] + KD], V_[:, VEC["ffn1_pre"]:VEC["ffn1_pre"] + KD], ALU.mult).then_inc(S("lru_cols"), 1)

        def act_b_loads(act):
            wait(act, units_used, PO.used(PO.rounds - 1, 3))
            act.dma_start(B_GW[:, :, :, :].rearrange("p h g n -> p (h g n)"), dram["b_gates"]).then_inc(S("gates_in"), 16)

        XB0 = 8

        def pe_b_in(pe):
            def gates(r, parity):
                pe.wait_ge(*due("b_xc", r + 1))
                pe.wait_ge(*due("b_stage", r + 1))
                if not (isinstance(r, int) and r < 2):
                    pe.wait_ge(*due("b_thi", r - 1))
                for g in range(2):
                    nc.tensor.matmul(PS[4 + 2 * parity + g], B_ST[:, parity, g, :], B_XC[:, parity, :], start=True, stop=True).then_inc(S("b_gates"), 1)

            def body(r, parity, pair):
                if first(r):
                    pe.wait_ge(*due("a_x", PO.rounds))
                bank_free(pe, "b_xb", r)
                feature_tile(pe, PB, r, (0, 1), PS[2 * parity], XH, XL,
                             (lambda k: pe.wait_ge(*due("s1_lo", k + 1))) if first(r) else None)
                if first(r):
                    pe_sum(pe, "s1", ACC, PS[7])
                else:
                    gates(r - 1, 1 - parity)
                bank_free(pe, "b_tg", r)
                feature_tile(pe, PB, r, (2, 3), PS[2 * parity + 1], XH, XL)
                if first(r):
                    pe_spread(pe, "s1", DIAG, PS[6])
            rounds(pe, PB, body)
            gates(PB.rounds - 1, 1)

        def act_b_in(act):
            def post(r, parity):
                TR, A_, TL, A2, TI, SQ, TG_ = (B_TMP[:, i, :] for i in (0, 1, 2, 3, 4, 5, 6))
                wait(act, *due("b_gates", 2 * r + 1))
                if not first(r):
                    wait(act, *due("b_scan", r))
                step_a = nc.scalar.activation(TR, PS[4 + 2 * parity], ACT.Tanh, scale=0.5, bias=HBA[:, bass.ds(r, 1)])
                step_a.then_inc(S("b_thr"), 1)
                wait(act, *due("b_gates", 2 * r + 2))
                nc.scalar.activation(TI, PS[5 + 2 * parity], ACT.Tanh, scale=0.5, bias=HBX[:, bass.ds(r, 1)]).then_inc(S("b_thi"), 1)
                wait(act, *due("b_thr", r + 1))
                nc.scalar.activation(A_, TR, ACT.Exp, scale=N4[:, bass.ds(r, 1)], bias=N4[:, bass.ds(r, 1)]).then_inc(S("b_a"), 1)
                nc.scalar.activation(TL, TR, ACT.Tanh, scale=P4[:, bass.ds(r, 1)], bias=P4[:, bass.ds(r, 1)]).then_inc(S("b_tl"), 1)
                wait(act, *due("b_a", r + 1))
                nc.scalar.activation(A2, A_, ACT.Square).then_inc(S("b_a2"), 1)
                wait(act, *due("b_tg", r + 1))
                nc.scalar.activation(TG_, B_TG[:, parity, :], ACT.Tanh, scale=0.5).then_inc(S("b_thg"), 1)
                wait(act, *due("b_m2", r + 1))
                nc.scalar.activation(SQ, A2, ACT.Sqrt).then_inc(S("b_mult"), 1)
                wait(act, *due("b_y", r + 1))
                nc.scalar.activation(B_YH[:, r, :], B_TMP[:, 7, :], ACT.Copy).then_inc(S("b_yh"), 1)

            def body(r, parity, pair):
                if first(r):
                    wait(act, *due("gates_in", 16))
                    act_rows(act, "s1", PS[6], RB[:, :])
                wait(act, *due("b_xb", r + 1))
                nc.scalar.activation(B_XC[:, parity, :], B_XB[:, parity, XB0:XB0 + SEQ], ACT.Identity,
                                     scale=V_[:, bass.ds(VEC["conv"] + 3 * KB + r, 1)], bias=V_[:, bass.ds(VEC["conv_b"] + r, 1)]).then_inc(S("b_xc0"), 1)
                if not (isinstance(r, int) and r < 2):
                    wait(act, *due("b_gates", 2 * r - 2))
                nc.scalar.activation(B_ST[:, parity, :, :], B_GW[:, r, :, :], ACT.Copy).then_inc(S("b_stage"), 1)
                if not first(r):
                    post(r - 1, 1 - parity)
            rounds(act, PB, body)
            post(PB.rounds - 1, 1)

        def dve_b_in(dve, step):
            dve_column(dve, step, "s1", PS[7][:, 0:4], COL, D, RMS_EPS)
            dve_diag(dve, step, "s1", COL, DIAG)

            def post(r, parity):
                A_, TL, A2, TI, SQ, TG_, Y_ = (B_TMP[:, i, :] for i in (1, 2, 3, 4, 5, 6, 7))
                BT, H_ = B_TMP[:, 8, :], B_TMP[:, 9, :]
                dve.wait_ge(*due("b_a2", r + 1))
                nc.vector.scalar_tensor_tensor(out=A2, in0=A2, scalar=1.0, in1=TL, op0=ALU.add, op1=ALU.mult).then_inc(S("b_m2"), 1)
                nc.vector.scalar_tensor_tensor(out=BT, in0=TI, scalar=1.0, in1=B_XC[:, parity, :], op0=ALU.add, op1=ALU.mult).then_inc(S("b_ix"), 1)
                dve.wait_ge(*due("b_thg", r + 1))
                nc.vector.scalar_tensor_tensor(out=Y_, in0=TG_, scalar=1.0, in1=B_TG[:, parity, :], op0=ALU.add, op1=ALU.mult).then_inc(S("b_sg"), 1)
                dve.wait_ge(*due("b_ix", r + 1))
                dve.wait_ge(*due("b_mult", r + 1))
                nc.vector.scalar_tensor_tensor(out=BT, in0=SQ, scalar=0.5, in1=BT, op0=ALU.mult, op1=ALU.mult).then_inc(S("b_bterm"), 1)
                dve.wait_ge(*due("b_bterm", r + 1))
                nc.vector.tensor_tensor_scan(H_, A_, BT, 0.0, ALU.mult, ALU.add).then_inc(S("b_scan"), 1)
                dve.wait_ge(*due("b_scan", r + 1))
                nc.vector.scalar_tensor_tensor(out=Y_, in0=Y_, scalar=0.5, in1=H_, op0=ALU.mult, op1=ALU.mult).then_inc(S("b_y"), 1)
                dve.wait_ge(*due("b_yh", r + 1))
                nc.vector.tensor_tensor(B_YL[:, r, :], Y_, B_YH[:, r, :].bitcast(F32), ALU.subtract).then_inc(S("b_yl"), 1)

            def body(r, parity, pair):
                if first(r):
                    dve.wait_ge(*due("s1_rb", 1))
                dve.wait_ge(units_used, PB.used(r, 1))
                nc.vector.tensor_tensor(B_XB[:, parity, XB0:XB0 + SEQ], PS[2 * parity], RB[:, :], ALU.mult).then_inc(S("b_xb"), 1)
                dve.wait_ge(*due("b_xc0", r + 1))
                for tap in range(3):
                    conv = nc.vector.scalar_tensor_tensor(
                        out=B_XC[:, parity, :], in0=B_XB[:, parity, XB0 - 3 + tap:XB0 - 3 + tap + SEQ],
                        scalar=V_[:, bass.ds(VEC["conv"] + tap * KB + r, 1)], in1=B_XC[:, parity, :], op0=ALU.mult, op1=ALU.add)
                    if tap < 2:
                        conv.then_inc(S("b_taps"), 1)
                        dve.wait_ge(*due("b_taps", 2 * r + (tap + 1)))
                conv.then_inc(S("b_xc"), 1)
                dve.wait_ge(*due("b_xc", r + 1))
                if not first(r):
                    post(r - 1, 1 - parity)
                dve.wait_ge(units_used, PB.used(r, 3))
                nc.vector.tensor_tensor(B_TG[:, parity, :], PS[2 * parity + 1], RB[:, :], ALU.mult).then_inc(S("b_tg"), 1)

            nc.vector.memset(B_XB[:, :, 0:8], 0.0).then_inc(S("b_pad"), 1)
            rounds(dve, PB, body)
            dve.wait_ge(*due("b_tg", PB.rounds))
            post(PB.rounds - 1, 1)

        def pe_b_out(pe):
            def body(r, parity, pair):
                if first(r):
                    pe.wait_ge(*due("b_tg", PB.rounds))
                bank_free(pe, "b_x", r)
                feature_tile(pe, PBO, r, range(4), PS[parity], B_YH, B_YL,
                             (lambda k: pe.wait_ge(*due("b_yl", k + 1))) if first(r) else None)
            rounds(pe, PBO, body)

        def act_b_out(act):
            rounds(act, PBO, lambda r, parity, pair: act_split(
                act, "s2", r, parity, X[:, r, :], NG[:, bass.ds(r, 1)], lambda: wait(act, *due("b_x", r + 1)),
                (None, vec("normf", r))))

        def dve_b_out(dve, step):
            def body(r, parity, pair):
                dve.wait_ge(units_used, PBO.used(r, 3))
                nc.vector.tensor_tensor(X[:, r, :], PS[parity], X[:, r, :], ALU.add).then_inc(S("b_x"), 1)
                dve.wait_ge(*due("b_x", r + 1))
                dve_split(dve, "s2", r, parity, X[:, r, :], NG[:, bass.ds(r, 1)], [ACC, ACC2])
            rounds(dve, PBO, body)

        def pe_ffn_up(pe, f, stat, before_bank, after_sum):
            ph = PH[f"{f}_up"]

            def body(r, parity, pair):
                if first(r):
                    pe.wait_ge(*due(before_bank[0], before_bank[1]))
                for i, read in enumerate((f"{f}_tg", f"{f}_tu")):
                    bank_free(pe, read, r)
                    feature_tile(pe, ph, r, (2 * i, 2 * i + 1), PS[2 * parity + i], XH, XL,
                                 (lambda k: pe.wait_ge(*due(f"{stat}_lo", k + 1))) if first(r) and i == 0 else None)
                    if first(r):
                        after_sum(i)
            rounds(pe, ph, body)

        def act_ffn_up(act, f):
            ph = PH[f"{f}_up"]

            def body(r, parity, pair):
                wait(act, *due(f"{f}_tg", r + 1))
                nc.scalar.activation(T[:, 2, :], T[:, 0, :], ACT.Silu).then_inc(S(f"{f}_sg"), 1)
                wait(act, *due(f"{f}_y", r + 1))
                nc.scalar.activation(Y_H[:, r, :], T[:, 3, :], ACT.Copy).then_inc(S(f"{f}_yh"), 1)
            rounds(act, ph, body)

        def dve_ffn_up(dve, step, f):
            ph = PH[f"{f}_up"]

            def body(r, parity, pair):
                dve.wait_ge(units_used, ph.used(r, 1))
                nc.vector.tensor_tensor(T[:, 0, :], PS[2 * parity], RB[:, :], ALU.mult).then_inc(S(f"{f}_tg"), 1)
                dve.wait_ge(units_used, ph.used(r, 3))
                nc.vector.tensor_tensor(T[:, 1, :], PS[2 * parity + 1], RB[:, :], ALU.mult).then_inc(S(f"{f}_tu"), 1)
                dve.wait_ge(*due(f"{f}_tu", r + 1))
                dve.wait_ge(*due(f"{f}_sg", r + 1))
                nc.vector.tensor_tensor(T[:, 3, :], T[:, 1, :], T[:, 2, :], ALU.mult).then_inc(S(f"{f}_y"), 1)
                dve.wait_ge(*due(f"{f}_yh", r + 1))
                nc.vector.tensor_tensor(Y_L[:, r, :], T[:, 3, :], Y_H[:, r, :].bitcast(F32), ALU.subtract).then_inc(S(f"{f}_yl"), 1)
            rounds(dve, ph, body)

        def act_branch_tile(act, n, k, parity, src, to=F):
            nc.scalar.activation(to[:, k, :], src, ACT.Copy).then_inc(S(f"{n}_f"), 1)
            if not (isinstance(k, int) and k < 2):
                wait(act, *due(f"{n}_added", k - 1))
            nc.scalar.activation(T[:, parity, :], src, ACT.Square).then_inc(S(f"{n}_sq"), 1)

        def dve_branch_tile(dve, n, k, parity):
            dve.wait_ge(*due(f"{n}_sq", k + 1))
            if first(k):
                nc.vector.tensor_copy(ACC, T[:, parity, :]).then_inc(S(f"{n}_added"), 1)
            else:
                dve.wait_ge(*due(f"{n}_added", k))
                nc.vector.tensor_tensor(ACC, ACC, T[:, parity, :], ALU.add).then_inc(S(f"{n}_added"), 1)

        def pe_ffn_down(pe, f, n):
            ph = PH[f"{f}_down"]

            def body(r, parity, pair):
                if first(r):
                    pe.wait_ge(*due(f"{f}_tu", PH[f"{f}_up"].rounds))
                bank_free(pe, f"{n}_sq", r)
                feature_tile(pe, ph, r, range(4), PS[parity], Y_H, Y_L,
                             (lambda k: pe.wait_ge(*due(f"{f}_yl", k + 1))) if first(r) else None)
            rounds(pe, ph, body)
            pe_sum(pe, n, ACC, PS[7])
            pe_spread(pe, n, DIAG, PS[6])

        def act_ffn_down(act, f, n):
            ph = PH[f"{f}_down"]

            def body(r, parity, pair):
                wait(act, units_used, ph.used(r, 3))
                act_branch_tile(act, n, r, parity, PS[parity])
            rounds(act, ph, body)
            act_rows(act, n, PS[6], RB[:, :])

        def dve_ffn_down(dve, step, f, n):
            rounds(dve, PH[f"{f}_down"], lambda r, parity, pair: dve_branch_tile(dve, n, r, parity))
            dve_column(dve, step, n, PS[7][:, 0:4], COL, D, RMS_EPS)
            dve_diag(dve, step, n, COL, DIAG)

        def dve_residual(dve, step, n, k, gain, weight, f):
            t = T[:, 5, :]
            step(nc.vector.scalar_tensor_tensor(out=t, in0=f[:, k, :], scalar=vec(gain, k), in1=RB[:, :], op0=ALU.mult, op1=ALU.mult))
            nc.vector.scalar_tensor_tensor(out=X[:, k, :], in0=t, scalar=weight, in1=X[:, k, :], op0=ALU.mult, op1=ALU.add).then_inc(S(f"{n}_x"), 1)
            dve.wait_ge(*due(f"{n}_x", k + 1))

        def dve_join(dve, step, n, gain, weight, nxt, next_gain, f=F, between=None):
            dve.wait_ge(*due(f"{n}_rb", 1))
            for k in range(KD):
                dve_residual(dve, step, n, k, gain, weight, f)
                dve_split(dve, nxt, k, k % 2, X[:, k, :], vec(next_gain, k), [ACC])
                if between:
                    between(k)

        def act_join(act, n, nxt, next_gain):
            for k in range(KD):
                act_split(act, nxt, k, k % 2, X[:, k, :], vec(next_gain, k), lambda: wait(act, *due(f"{n}_x", k + 1)))

        C2, CF = SM[:, 4:8], SM[:, 20:24]
        RB1 = T[:, 6, :]

        def pe_between(pe, i):
            if i == 0:
                pe.wait_ge(*due("s2_added", 2 * KD))
                for q, acc in enumerate((ACC, ACC2)):
                    for t in range(TOK):
                        last = nc.tensor.matmul(PS[7][:, 4 * q + t:4 * q + t + 1], acc[:, t * P:(t + 1) * P], ONES[:, 0:1], start=True, stop=True)
                last.then_inc(S("s2_sum"), 1)
            else:
                pe_spread(pe, "s2", T[:, 0, :], PS[6])
                pe_spread(pe, "s2b", T[:, 1, :], PS[5])

        def dve_between(dve, step):
            dve_column(dve, step, "s2", PS[7][:, 0:4], C2, D, RMS_EPS)
            x = SC[:, 96:100]
            step(nc.vector.tensor_tensor(x, C2, C2, ALU.mult))
            step(nc.vector.tensor_tensor(x, x, PS[7][:, 4:8], ALU.mult))
            step(nc.vector.tensor_scalar(x, x, 1.0 / D, RMS_EPS, ALU.mult, ALU.add))
            inverse_root(step, CF, x, scratch(TOK))
            step(nc.vector.tensor_tensor(CF, CF, C2, ALU.mult))
            dve_diag(dve, step, "s2", C2, T[:, 0, :])
            dve_diag(dve, step, "s2b", CF, T[:, 1, :])
            dve.wait_ge(*due("s2_rb", 1))
            for k in range(KD):
                last = nc.vector.scalar_tensor_tensor(out=X[:, k, :], in0=X[:, k, :], scalar=vec("normf", k), in1=RB1, op0=ALU.mult, op1=ALU.mult)
            last.then_inc(S("x2"), 1)
            dve.wait_ge(*due("s2b_rb", 1))

        def act_between(act):
            act_rows(act, "s2", PS[6], RB1)
            act_rows(act, "s2b", PS[5], RB[:, :])

        PFV, PFQ, PSM, PGQ, PGZ, PMO = (PH[n] for n in ("fox_v", "fox_qk", "small", "gdn_qkv", "gdn_z", "mix_out"))
        FQ = place("fox_q", YAT, [4, SEQ])
        FK = place("fox_k", YAT + 8, [4, SEQ])
        FV = place("fox_v_rows", YAT + 16, [TOK, SEQ])
        GQKV = place("gdn_qkv_t", YAT + 24, [12, SEQ])
        GZ = place("gdn_z_t", YAT + 48, [GH, SEQ])
        R_ = place("token_rows", YAT + 56, [SEQ])
        COLS = place("token_cols", YAT + 58, [TOK, P])
        G_XB = place("gdn_xb", YAT + 60, [2, SEQ + 8])
        FS = place("fox_s", YAT + 64, [2, SEQ])
        FP = place("fox_p", YAT + 68, [2, SEQ])
        FPT = place("fox_pt", YAT + 72, [2, TOK, SEQ])
        MASKS = place("masks", YAT + 88, [9, P])
        CM, INC, STRICT = MASKS[:, 0, :], MASKS[:, 1, :], MASKS[:, 2, :]
        LEVELS = (1, 2, 4, 8, 16, 32)
        F_ROWS, B_ROWS, G_ROWS, E_ROWS = 0, 32, 64, 96

        def pool_masks(pool):
            n = [0]

            def done(instruction):
                n[0] += 1
                instruction.then_inc(S("masks"), 1)
                pool.wait_ge(*due("masks", n[0]))

            def keep(m, op, pattern, base, cm, fill=0.0):
                done(nc.gpsimd.affine_select(out=m, in_=m, compare_op=op, fill=fill, base=base, pattern=pattern, channel_multiplier=cm))
            pool.wait_ge(units_used, PH["ffn1_down"].used(7, 3))
            done(nc.gpsimd.memset(CM, 0.0))
            keep(CM, ALU.is_ge, [[-1, P]], 0, 1, -1e30)
            for i, b in enumerate(LEVELS):
                m = MASKS[:, 3 + i, :]
                done(nc.gpsimd.memset(m, 1.0))
                v = m.rearrange("p (n c) -> p n c", c=2 * b)
                keep(v, ALU.is_ge, [[-2 * b, P // (2 * b)], [0, 2 * b]], 0, 1)
                keep(v, ALU.is_ge, [[2 * b, P // (2 * b)], [0, 2 * b]], b - 1, -1)
                keep(v, ALU.is_ge, [[0, P // (2 * b)], [1, 2 * b]], -b, 0)
            for m, base in ((INC, 0), (STRICT, -1)):
                done(nc.gpsimd.memset(m, 1.0))
                v = m.rearrange("p (n c) -> p n c", c=CH)
                keep(v, ALU.is_ge, [[-CH, P // CH], [0, CH]], 0, 1)
                keep(v, ALU.is_ge, [[CH, P // CH], [0, CH]], CH - 1, -1)
                keep(m, ALU.is_ge, [[1, P]], base, -1)

        N_MASKS = 2 + 4 * 6 + 2 * 4

        def pe_mix_in(pe):
            def fox_v(r, parity, pair):
                if first(r):
                    pe.wait_ge(*due("f1_sq", KD))
                token_tiles(pe, PFV, r, parity, PS[0:4], XH, XL, lambda k: pe.wait_ge(*due("s3_lo", k + 1)))
                if first(r):
                    pe_sum(pe, "s3", ACC, PS[7])
                else:
                    pe_spread(pe, "s3", DIAG, PS[6])
            rounds(pe, PFV, fox_v)

            def fox_qk(r, parity, pair):
                if first(r):
                    pe.wait_ge(*due("fv", TOK))
                for i, read in enumerate(("fq", "fk")):
                    bank_free(pe, read, r)
                    feature_tile(pe, PFQ, r, (2 * i, 2 * i + 1), PS[2 * parity + i], XH, XL)
            rounds(pe, PFQ, fox_qk)
            for r in range(2):
                for j in range(4):
                    k = 4 * r + j
                    pe.wait_ge(units_ready, PSM.used(r, j))
                    wh, wl = WH[:, SLOT[j], :], WL[:, SLOT[j], :]
                    nc.tensor.matmul(PS[4], wh, XH[:, k, :], start=k == 0, stop=False)
                    nc.tensor.matmul(PS[4], wl, XH[:, k, :], start=False, stop=False)
                    nc.tensor.matmul(PS[4], wh, XL[:, k, :], start=False, stop=k == KD - 1).then_inc(units_used, 1)

            def qkv(r, parity, pair):
                if first(r):
                    pe.wait_ge(*due("fk", PFQ.rounds))
                for i in range(2):
                    if not (isinstance(r, int) and r < 2):
                        pe.wait_ge(*due("g_xb", (r - 2) * 2 + (i + 1)))
                    feature_tile(pe, PGQ, r, (2 * i, 2 * i + 1), PS[2 * parity + i], XH, XL)
            rounds(pe, PGQ, qkv)

            def z(r, parity, pair):
                if first(r):
                    pe.wait_ge(*due("g_xb", 2 * PGQ.rounds))
                for i in range(2):
                    feature_tile(pe, PGZ, r, (2 * i, 2 * i + 1), PS[2 * parity + i], XH, XL)
            rounds(pe, PGZ, z)

        def act_mix_in(act):
            act.wait_ge(*due("s3_diag", 1))
            act.wait_ge(units_used, PFV.used(1, 3))
            for i in range(TOK):
                nc.scalar.activation(FV[:, i, :], PS[i], ACT.Copy, scale=COL[:, i:i + 1]).then_inc(S("fv"), 1)
            act_rows(act, "s3", PS[6], RB[:, :])
            act.wait_ge(*due("rows_x", 1))
            nc.scalar.activation(T[B_ROWS:B_ROWS + GH, 3, :], T[B_ROWS:B_ROWS + GH, 2, :], ACT.Tanh, scale=0.5).then_inc(S("beta_tanh"), 1)
            nc.scalar.activation(SM[64:68, 21:22], V_[64:68, VEC["a_log"]:VEC["a_log"] + 1], ACT.Exp).then_inc(S("a_exp"), 1)
            act_exp_neg(act, "rows", T[:, 4, :])

            def qkv(r, parity, pair):
                for i in range(2):
                    wait(act, *due("g_xb", r * 2 + (i + 1)))
                    nc.scalar.activation(T[:, i, :], G_XB[:, i, 8:8 + SEQ], ACT.Copy, scale=V_[:, bass.ds(VEC["gconv"] + 36 + r * 2 + i, 1)]).then_inc(S("g_c0"), 1)
                    wait(act, *due("g_conv", r * 2 + (i + 1)))
                    nc.scalar.activation(GQKV[:, r * 2 + i, :], T[:, i, :], ACT.Silu).then_inc(S("g_qkv"), 1)
            rounds(act, PGQ, qkv)

            def z(r, parity, pair):
                for i in range(2):
                    act.wait_ge(*due("g_z", r * 2 + (i + 1)))
                    nc.scalar.activation(GZ[:, r * 2 + i, :], T[:, 2 + i, :], ACT.Silu).then_inc(S("g_zs"), 1)
            rounds(act, PGZ, z)
            act.wait_ge(*due("cols_t", 1))
            nc.scalar.activation(COLS[:, :, 0:100], PS[5].rearrange("p (t c) -> p t c", t=TOK)[:, :, 0:100], ACT.Copy).then_inc(S("cols"), 1)

        def pe_cols(pe):
            pe.wait_ge(*due("rows", 1))
            for i in range(TOK):
                last = nc.tensor.transpose(PS[5][:, i * P:i * P + 100], R_[0:100, i * P:(i + 1) * P], IDENT[0:100, 0:100])
            last.then_inc(S("cols_t"), 1)

        def dve_mix_in(dve, step):
            dve_column(dve, step, "s3", PS[7][:, 0:4], COL, D, RMS_EPS)
            dve_diag(dve, step, "s3", COL, DIAG)
            dve.wait_ge(*due("s3_rb", 1))

            def fox_qk(r, parity, pair):
                dve.wait_ge(units_used, PFQ.used(r, 1))
                nc.vector.scalar_tensor_tensor(out=FQ[:, r, :], in0=PS[2 * parity], scalar=FOXD ** -0.5, in1=RB[:, :], op0=ALU.mult, op1=ALU.mult).then_inc(S("fq"), 1)
                dve.wait_ge(units_used, PFQ.used(r, 3))
                nc.vector.tensor_tensor(FK[:, r, :], PS[2 * parity + 1], RB[:, :], ALU.mult).then_inc(S("fk"), 1)
            rounds(dve, PFQ, fox_qk)
            X_, LP, E_, S2_ = T[:, 2, :], T[:, 6, :], T[:, 4, :], T[:, 5, :]
            dve.wait_ge(units_used, PSM.used(1, 3))
            step(nc.vector.tensor_tensor(X_, PS[4], RB[:, :], ALU.mult))
            nc.vector.tensor_scalar(X_, X_, vec("small_bias"), None, ALU.add).then_inc(S("rows_x"), 1)
            dve.wait_ge(*due("rows_x", 1))
            step(nc.vector.memset(R_[:, :], 0.0))
            step(nc.vector.memset(G_XB[:, :, 0:8], 0.0))
            log1p_exp_neg_abs(dve, step, "rows", LP, X_, E_, S2_)
            f, b, g, e = (slice(n, n + 8 if n == 0 else n + GH) for n in (F_ROWS, B_ROWS, G_ROWS, E_ROWS))
            step(nc.vector.scalar_tensor_tensor(out=E_[f, :], in0=X_[f, :], scalar=0.0, in1=LP[f, :], op0=ALU.min, op1=ALU.subtract))
            step(nc.vector.tensor_tensor_scan(R_[f, :], ONES[f, 0:1].to_broadcast([8, SEQ]), E_[f, :], 0.0, ALU.mult, ALU.add))
            dve.wait_ge(*due("beta_tanh", 1))
            step(nc.vector.tensor_scalar(R_[b, :], T[b, 3, :], 0.5, 0.5, ALU.mult, ALU.add))
            dve.wait_ge(*due("a_exp", 1))
            step(nc.vector.scalar_tensor_tensor(out=E_[g, :], in0=X_[g, :], scalar=0.0, in1=LP[g, :], op0=ALU.max, op1=ALU.add))
            step(nc.vector.tensor_scalar(E_[g, :], E_[g, :], SM[g, 21:22], -1.0, ALU.mult, ALU.mult))
            step(nc.vector.memset(S2_[g, :], 1.0))
            step(nc.vector.memset(S2_[g, :].rearrange("p (n c) -> p n c", c=CH)[:, :, 0:1], 0.0))
            step(nc.vector.tensor_tensor_scan(R_[g, :], S2_[g, :], E_[g, :], 0.0, ALU.mult, ALU.add))
            chunks = R_[g, :].rearrange("p (n c) -> p n c", c=CH)
            nc.vector.tensor_tensor(R_[e, :].rearrange("p (n c) -> p n c", c=CH), chunks[:, :, CH - 1:CH].to_broadcast([GH, SEQ // CH, CH]), chunks, ALU.subtract).then_inc(S("rows"), 1)

            def qkv(r, parity, pair):
                for i in range(2):
                    dve.wait_ge(units_used, PGQ.used(r, 2 * i + 1))
                    if not first(r):
                        dve.wait_ge(*due("g_conv", 2 * r - 1 + i))
                    nc.vector.tensor_tensor(G_XB[:, i, 8:8 + SEQ], PS[2 * parity + i], RB[:, :], ALU.mult).then_inc(S("g_xb"), 1)
                    dve.wait_ge(*due("g_c0", r * 2 + (i + 1)))
                    for tap in range(3):
                        conv = nc.vector.scalar_tensor_tensor(
                            out=T[:, i, :], in0=G_XB[:, i, 5 + tap:5 + tap + SEQ], scalar=V_[:, bass.ds(VEC["gconv"] + 12 * tap + r * 2 + i, 1)],
                            in1=T[:, i, :], op0=ALU.mult, op1=ALU.add)
                        if tap < 2:
                            conv.then_inc(S("g_taps"), 1)
                            dve.wait_ge(*due("g_taps", r * 4 + (2 * i + tap + 1)))
                    conv.then_inc(S("g_conv"), 1)
            rounds(dve, PGQ, qkv)

            def z(r, parity, pair):
                for i in range(2):
                    dve.wait_ge(units_used, PGZ.used(r, 2 * i + 1))
                    if not first(r):
                        dve.wait_ge(*due("g_zs", 2 * r - 1 + i))
                    nc.vector.tensor_tensor(T[:, 2 + i, :], PS[2 * parity + i], RB[:, :], ALU.mult).then_inc(S("g_z"), 1)
            rounds(dve, PGZ, z)

        STEPS = FOXH * TOK

        def row_of(pe, at, n, i, ps):
            sel = IDENT[at:at + n, at + i:at + i + 1].to_broadcast([n, P])
            return nc.tensor.matmul(ps, sel, R_[at:at + n, :], start=True, stop=True)

        def pe_fox(pe):
            pe.wait_ge(*due("g_z", 4))
            for i in range(STEPS + 5):
                h, qt = divmod(i, TOK)
                if i < STEPS:
                    if qt == 0:
                        if h >= 2:
                            pe.wait_ge(*due("fx_rowc", h - 1))
                        row_of(pe, F_ROWS, 8, h, PS[6 + h % 2]).then_inc(S("fx_row"), 1)
                    n, rows = (qt + 1) * P, slice(64 * (h % 2), 64 * (h % 2) + 64)
                    if i >= 2:
                        pe.wait_ge(*due("fx_sv", i - 1))
                    nc.tensor.matmul(PS[i % 2][:, 0:n], FQ[rows, h // 2, qt * P:(qt + 1) * P], FK[rows, h // 2, 0:n], start=True, stop=True).then_inc(S("fx_s"), 1)
                j = i - 2
                if 0 <= j < STEPS:
                    pe.wait_ge(*due("fx_p", j + 1))
                    if j >= 2:
                        pe.wait_ge(*due("fx_pt", j - 1))
                    for kt in range(j % TOK + 1):
                        last = nc.tensor.transpose(PS[2 + j % 2][:, kt * P:(kt + 1) * P], FP[:, j % 2, kt * P:(kt + 1) * P], IDENT[:, :])
                    last.then_inc(S("fx_t"), 1)
                if i >= 8 and qt == 0:
                    fox_out(pe, h - 2)

        def fox_out(pe, h):
            pe.wait_ge(*due("fx_pt", TOK * (h + 1)))
            if h >= 4 and h % 2 == 0:
                pe.wait_ge(*due("fx_lo", h // 2 - 1))
            half = slice(64 * (h % 2), 64 * (h % 2) + 64)
            for kt in range(TOK):
                last = nc.tensor.matmul(PS[4 + (h // 2) % 2][half, kt * P:SEQ], FV[:, kt, h * FOXD:(h + 1) * FOXD], FPT[:, h % 2, kt, kt * P:SEQ],
                                        start=kt == 0, stop=kt == TOK - 1)
            last.then_inc(S("fx_o"), 1)

        def dve_fox(dve, step):
            MXC, SUMC = SC[:, 0:32], SC[:, 32:64]
            dve.wait_ge(*due("masks", N_MASKS))
            dve.wait_ge(*due("cols", 1))
            for i in range(STEPS + 1):
                h, qt = divmod(i, TOK)
                if i < STEPS:
                    n = (qt + 1) * P
                    s = FS[:, i % 2, :]
                    dve.wait_ge(*due("fx_rowc", h + 1))
                    dve.wait_ge(*due("fx_s", i + 1))
                    if i >= 2:
                        dve.wait_ge(*due("fx_e", i - 1))
                    nc.vector.scalar_tensor_tensor(out=s[:, 0:n], in0=PS[i % 2][:, 0:n], scalar=COLS[:, qt, F_ROWS + h:F_ROWS + h + 1], in1=T[:, h % 2, 0:n], op0=ALU.add, op1=ALU.subtract).then_inc(S("fx_sv"), 1)
                    dve.wait_ge(*due("fx_sv", i + 1))
                    step(nc.vector.tensor_tensor(s[:, n - P:n], s[:, n - P:n], CM, ALU.add))
                    step(nc.vector.reduce_max(MXC[:, i:i + 1], s[:, 0:n], axis=AX.X))
                    nc.vector.tensor_scalar(MXC[:, i:i + 1], MXC[:, i:i + 1], -1.0, None, ALU.mult).then_inc(S("fx_nm"), 1)
                if i >= 1:
                    j = i - 1
                    n = (j % TOK + 1) * P
                    dve.wait_ge(*due("fx_e", j + 1))
                    step(nc.vector.reciprocal(SUMC[:, j:j + 1], SUMC[:, j:j + 1]))
                    nc.vector.tensor_scalar(FP[:, j % 2, 0:n], FP[:, j % 2, 0:n], SUMC[:, j:j + 1], None, ALU.mult).then_inc(S("fx_p"), 1)
                if i >= 8 and qt == 3 and h % 2 == 1:
                    dve_fox_out(dve, (h - 3) // 2)
            dve_fox_out(dve, FOXH // 2 - 1)

        def dve_fox_out(dve, m):
            dve.wait_ge(*due("fx_hi", m + 1))
            nc.vector.tensor_tensor(XL[:, m, :], PS[4 + m % 2], XH[:, m, :].bitcast(F32), ALU.subtract).then_inc(S("fx_lo"), 1)

        def act_fox(act):
            MXC, SUMC = SC[:, 0:32], SC[:, 32:64]
            for i in range(STEPS + 3):
                h, qt = divmod(i, TOK)
                if i < STEPS:
                    if qt == 0:
                        act.wait_ge(*due("fx_row", h + 1))
                        if h >= 2:
                            act.wait_ge(*due("fx_sv", TOK * (h - 1)))
                        nc.scalar.activation(T[:, h % 2, :], PS[6 + h % 2], ACT.Copy).then_inc(S("fx_rowc"), 1)
                    n = (qt + 1) * P
                    act.wait_ge(*due("fx_nm", i + 1))
                    if i >= 2:
                        act.wait_ge(*due("fx_t", i - 1))
                    nc.scalar.activation(FP[:, i % 2, 0:n], FS[:, i % 2, 0:n], ACT.Exp, bias=MXC[:, i:i + 1], accum_out=SUMC[:, i:i + 1]).then_inc(S("fx_e"), 1)
                j = i - 3
                if 0 <= j < STEPS:
                    jh, jq = divmod(j, TOK)
                    act.wait_ge(*due("fx_t", j + 1))
                    if jh >= 2 and jq == 0:
                        act.wait_ge(*due("fx_o", jh - 1))
                    nc.scalar.activation(FPT[:, jh % 2, 0:jq + 1, jq * P:(jq + 1) * P], PS[2 + j % 2][:, 0:(jq + 1) * P].rearrange("p (k q) -> p k q", q=P), ACT.Copy).then_inc(S("fx_pt"), 1)
                if i >= 8 and qt == 3 and h % 2 == 1 and i < STEPS:
                    act_fox_out(act, (h - 3) // 2)
            act_fox_out(act, FOXH // 2 - 1)

        def act_fox_out(act, m):
            act.wait_ge(*due("fx_o", 2 * m + 2))
            act.wait_ge(units_used, PGZ.used(1, 3))
            nc.scalar.activation(XH[:, m, :], PS[4 + m % 2], ACT.Copy).then_inc(S("fx_hi"), 1)

        GS = place("gdn_inv_t", YAT, [TOK, SEQ])
        GT = place("gdn_inv", YAT + 8, [TOK, SEQ])
        GLT = place("gdn_l_t", YAT + 16, [TOK, SEQ])
        GU_ = place("gdn_u", YAT + 8, [TOK, SEQ])
        GWN = place("gdn_w_t_neg", YAT + 16, [TOK, SEQ])
        GST = place("gdn_state", YAT + 32, [2, SEQ])
        GVN = place("gdn_v_new", YAT + 36, [2, SEQ])
        GAT = place("gdn_attn_t", YAT + 40, [TOK, SEQ])
        GR = place("gdn_g_rows", YAT + 64, [GH, SEQ])
        GC = place("gdn_level", YAT + 64, [TOK, SEQ])
        GO = place("gdn_o_t", YAT + 64, [GH, SEQ])
        EG = place("gdn_exp_g", YAT + 72, [GH, SEQ])
        GKB = place("gdn_k_beta", YAT + 80, [GH, SEQ])
        GKT = place("gdn_k_tail", YAT + 80, [TOK, SEQ])
        GVB = place("gdn_v_beta", 40, [TOK, SEQ])
        GKE = place("gdn_k_beta_eg", 24, [TOK, SEQ])
        NC = SM[:, 32:64]
        CE = COLS[:, :, 104:124].rearrange("p t (a h) -> p t a h", h=GH)
        heads = lambda ap: ap.rearrange("p (h c) -> p h c", h=GH)
        across = lambda col: col.unsqueeze(2).to_broadcast([P, GH, P])
        every = lambda mask: mask.unsqueeze(1).to_broadcast([P, GH, P])
        tile_of = lambda p: slice(p * P, (p + 1) * P)

        def pe_norms(pe, name, src_ready, count, n_cols):
            for j in range(count):
                pe.wait_ge(*due(src_ready, j + 1))
                for i in range(TOK):
                    last = nc.tensor.matmul(PS[7][:, 4 * j + i:4 * j + i + 1], T[:, j % 2, tile_of(i)], ONES[:, 0:1], start=True, stop=True)
                last.then_inc(S(f"{name}_sums"), 1)

        def pe_spreads(pe, name, count):
            for j in range(count):
                pe.wait_ge(*due(f"{name}_diags", j + 1))
                if j >= 2:
                    pe.wait_ge(*due(f"{name}_scaled", j - 1))
                nc.tensor.matmul(PS[4 + j % 2], ONES[:, :], T[:, 2 + j % 2, :], start=True, stop=True).then_inc(S(f"{name}_spread"), 1)

        def act_squares(act, name, tiles):
            for j, tile in enumerate(tiles):
                if j >= 2:
                    act.wait_ge(*due(f"{name}_sums", j - 1))
                nc.scalar.activation(T[:, j % 2, :], tile, ACT.Square).then_inc(S(f"{name}_sq"), 1)

        def dve_diags(dve, name, cols, j):
            if j >= 2:
                dve.wait_ge(*due(f"{name}_spread", j - 1))
            nc.vector.tensor_tensor(
                heads(T[:, 2 + j % 2, :]), every(IDENT[:, :]),
                cols[:, 4 * j:4 * j + 4].unsqueeze(2).to_broadcast([P, TOK, P]), ALU.mult).then_inc(S(f"{name}_diags"), 1)

        def pe_gdn_products(pe):
            pe.wait_ge(*due("fx_e", STEPS))
            pe_norms(pe, "gl", "gl_sq", 8, 32)
            pe_spreads(pe, "gl", 8)
            for h in range(GH):
                if h >= 2:
                    pe.wait_ge(*due("g_er", h - 1))
                elif h == 0:
                    pe.wait_ge(*due("fx_lo", 4))
                row_of(pe, G_ROWS, GH, h, PS[h % 2]).then_inc(S("g_row"), 1)
                if h >= 2:
                    pe.wait_ge(*due("g_kb", h - 1))
                row_of(pe, B_ROWS, GH, h, PS[2 + h % 2]).then_inc(S("g_brow"), 1)
            for p in range(TOK):
                if p < 2:
                    pe.wait_ge(*due("gl_scaled", 8))
                else:
                    pe.wait_ge(*due("g_vb", p - 1))
                for h in range(GH):
                    last = nc.tensor.transpose(PS[4 + p % 2][:, h * P:(h + 1) * P], GQKV[:, 8 + h, tile_of(p)], IDENT[:, :])
                last.then_inc(S("g_vt"), 1)
            pe.wait_ge(*due("g_er", GH))
            pe.wait_ge(*due("g_kb", GH))
            for p in range(TOK):
                if p >= 2:
                    pe.wait_ge(*due("g_lt1", p - 1))
                for h in range(GH):
                    last = nc.tensor.matmul(PS[p % 2][:, h * P:(h + 1) * P], GQKV[:, 4 + h, tile_of(p)], GKB[:, h, tile_of(p)], start=True, stop=True)
                last.then_inc(S("g_kk"), 1)
                if p >= 2:
                    pe.wait_ge(*due("g_at", p - 1))
                for h in range(GH):
                    last = nc.tensor.matmul(PS[2 + p % 2][:, h * P:(h + 1) * P], GQKV[:, 4 + h, tile_of(p)], GQKV[:, h, tile_of(p)], start=True, stop=True)
                last.then_inc(S("g_qk"), 1)
            for p in range(TOK):
                if p < 2:
                    pe.wait_ge(*due("g_vb", TOK))
                else:
                    pe.wait_ge(*due("g_kt", p - 1))
                for h in range(GH):
                    last = nc.tensor.transpose(PS[4 + p % 2][:, h * P:(h + 1) * P], GQKV[:, 4 + h, tile_of(p)], IDENT[:, :])
                last.then_inc(S("g_ktt"), 1)

        def act_gdn_products(act):
            act_squares(act, "gl", [GQKV[:, j, :] for j in range(8)])
            nc.scalar.activation(CE[:, :, 0, :], COLS[:, :, G_ROWS:G_ROWS + GH], ACT.Exp).then_inc(S("g_ce"), 1)
            nc.scalar.activation(CE[:, :, 2, :], COLS[:, :, E_ROWS:E_ROWS + GH], ACT.Exp).then_inc(S("g_ce"), 1)
            for h in range(GH):
                act.wait_ge(*due("g_row", h + 1))
                nc.scalar.activation(GR[:, h, :], PS[h % 2], ACT.Copy).then_inc(S("g_gr"), 1)
                nc.scalar.activation(EG[:, h, :], PS[h % 2], ACT.Exp).then_inc(S("g_er"), 1)
            for p in range(TOK):
                act.wait_ge(*due("g_dec", p + 1))
                nc.scalar.activation(T[:, 1, :], T[:, 0, :], ACT.Exp).then_inc(S("g_dexp"), 1)

        def dve_gdn_products(dve, step):
            x = SC[:, 96:128]
            dve.wait_ge(*due("gl_sums", 8))
            step(nc.vector.tensor_scalar(x, PS[7][:, 0:32], RMS_EPS, None, ALU.add))
            inverse_root(step, NC, x, scratch(32))
            step(nc.vector.tensor_scalar(NC[:, 0:16], NC[:, 0:16], GD ** -0.5, None, ALU.mult))
            dve_diags(dve, "gl", NC, 0)
            for j in range(8):
                if j < 7:
                    dve_diags(dve, "gl", NC, j + 1)
                dve.wait_ge(*due("gl_spread", j + 1))
                nc.vector.tensor_tensor(GQKV[:, j, :], GQKV[:, j, :], PS[4 + j % 2], ALU.mult).then_inc(S("gl_scaled"), 1)
            dve.wait_ge(*due("gl_scaled", 8))
            dve.wait_ge(*due("g_ce", 2))
            step(nc.vector.tensor_tensor(CE[:, :, 1, :], CE[:, :, 0, :], COLS[:, :, B_ROWS:B_ROWS + GH], ALU.mult))
            for h in range(GH):
                dve.wait_ge(*due("g_brow", h + 1))
                nc.vector.tensor_tensor(GKB[:, h, :], GQKV[:, 4 + h, :], PS[2 + h % 2], ALU.mult).then_inc(S("g_kb"), 1)
            for p in range(TOK):
                dve.wait_ge(*due("g_vt", p + 1))
                nc.vector.tensor_tensor(heads(GVB[:, p, :]), heads(PS[4 + p % 2]), across(COLS[:, p, B_ROWS:B_ROWS + GH]), ALU.mult).then_inc(S("g_vb"), 1)
            dve.wait_ge(*due("g_er", GH))
            for p in range(TOK):
                for h in range(GH):
                    last = nc.vector.tensor_scalar(T[:, 0, h * P:(h + 1) * P], GR[:, h, tile_of(p)], COLS[:, p, G_ROWS + h:G_ROWS + h + 1], 0.0, ALU.subtract, ALU.min)
                last.then_inc(S("g_dec"), 1)
                dve.wait_ge(*due("g_dexp", p + 1))
                step(nc.vector.tensor_tensor(heads(T[:, 1, :]), heads(T[:, 1, :]), every(INC), ALU.mult))
                dve.wait_ge(*due("g_kk", p + 1))
                nc.vector.tensor_tensor(GLT[:, p, :], PS[p % 2], T[:, 1, :], ALU.mult).then_inc(S("g_lt1"), 1)
                dve.wait_ge(*due("g_qk", p + 1))
                nc.vector.tensor_tensor(GAT[:, p, :], PS[2 + p % 2], T[:, 1, :], ALU.mult).then_inc(S("g_at"), 1)
                dve.wait_ge(*due("g_lt1", p + 1))
                nc.vector.tensor_tensor(heads(GLT[:, p, :]), heads(GLT[:, p, :]), every(STRICT), ALU.mult).then_inc(S("g_lt"), 1)
                dve.wait_ge(*due("g_at", p + 1))
            for h in range(GH):
                dve.wait_ge(*due("g_qk", TOK))
                step(nc.vector.tensor_tensor(GQKV[:, h, :], GQKV[:, h, :], EG[:, h, :], ALU.mult))
            for p in range(TOK):
                dve.wait_ge(*due("g_ktt", p + 1))
                nc.vector.tensor_tensor(heads(GKE[:, p, :]), heads(PS[4 + p % 2]), across(CE[:, p, 1, :]), ALU.mult).then_inc(S("g_ke"), 1)
                nc.vector.tensor_tensor(heads(GKT[:, p, :]), heads(PS[4 + p % 2]), across(CE[:, p, 2, :]), ALU.mult).then_inc(S("g_kt"), 1)

        def pool_levels(pool):
            for n, b in enumerate(LEVELS):
                for p in range(TOK):
                    if n == 0:
                        pool.wait_ge(*due("g_lt", p + 1))
                        if p == 0:
                            pool.wait_ge(*due("g_dec", TOK))
                    else:
                        pool.wait_ge(*due("g_u", (n - 1) * TOK + p + 1))
                        if n == 1:
                            pool.wait_ge(*due("g_s", p + 1))
                    nc.gpsimd.tensor_tensor(heads(GC[:, p, :]), heads(GLT[:, p, :]), every(MASKS[:, 3 + n, :]), ALU.mult).then_inc(S("g_c"), 1)

        def pe_levels(pe):
            for n, b in enumerate(LEVELS):
                for p in range(TOK):
                    m = n * TOK + p
                    pe.wait_ge(*due("g_c", m + 1))
                    if m >= TOK + 2:
                        pe.wait_ge(*due("g_uc", m - TOK - 1))
                    elif m >= 2:
                        pe.wait_ge(*due("g_t", m - 1))
                    else:
                        pe.wait_ge(*due("g_at", TOK))
                    if n:
                        pe.wait_ge(*due("g_t", (n - 1) * TOK + p + 1))
                    for h in range(GH):
                        c, o = GC[:, p, h * P:(h + 1) * P], PS[m % 2][:, h * P:(h + 1) * P]
                        if n == 0:
                            last = nc.tensor.transpose(o, c, IDENT[:, :])
                        else:
                            last = nc.tensor.matmul(o, c, GT[:, p, h * P:(h + 1) * P], start=True, stop=True)
                    last.then_inc(S("g_u"), 1)
                if n == 0:
                    continue
                for p in range(TOK):
                    m = n * TOK + p
                    pe.wait_ge(*due("g_uc", m - TOK + 1))
                    if m - TOK >= 2:
                        pe.wait_ge(*due("g_t", m - 1))
                        pe.wait_ge(*due("g_s", m - 1))
                    elif m - TOK == 0:
                        pe.wait_ge(*due("g_kt", TOK))
                    for h in range(GH):
                        hh = slice(h * P, (h + 1) * P)
                        last = nc.tensor.matmul(PS[2 + p % 2][:, hh], GS[:, p, hh], T[:, p, hh], start=True, stop=True)
                    last.then_inc(S("g_tu"), 1)
                    for h in range(GH):
                        hh = slice(h * P, (h + 1) * P)
                        last = nc.tensor.matmul(PS[4 + p % 2][:, hh], T[:, p, hh], GS[:, p, hh], start=True, stop=True)
                    last.then_inc(S("g_us"), 1)

        def act_levels(act):
            for m in range(TOK, TOK * len(LEVELS)):
                act.wait_ge(*due("g_u", m + 1))
                if m >= 2 * TOK:
                    act.wait_ge(*due("g_us", m - 2 * TOK + 1))
                nc.scalar.activation(T[:, m % TOK, :], PS[m % 2], ACT.Copy).then_inc(S("g_uc"), 1)

        def dve_levels(dve, step):
            for n in range(len(LEVELS)):
                for p in range(TOK):
                    m = n * TOK + p
                    if n == 0:
                        dve.wait_ge(*due("g_u", m + 1))
                        nc.vector.scalar_tensor_tensor(out=heads(GT[:, p, :]), in0=heads(PS[m % 2]), scalar=-1.0, in1=every(IDENT[:, :]), op0=ALU.mult, op1=ALU.add).then_inc(S("g_t"), 1)
                        nc.vector.scalar_tensor_tensor(out=heads(GS[:, p, :]), in0=heads(GC[:, p, :]), scalar=-1.0, in1=every(IDENT[:, :]), op0=ALU.mult, op1=ALU.add).then_inc(S("g_s"), 1)
                    else:
                        dve.wait_ge(*due("g_us", m - TOK + 1))
                        dve.wait_ge(*due("g_t", m - TOK + 1))
                        dve.wait_ge(*due("g_s", m - TOK + 1))
                        nc.vector.tensor_tensor(GT[:, p, :], GT[:, p, :], PS[2 + p % 2], ALU.subtract).then_inc(S("g_t"), 1)
                        nc.vector.tensor_tensor(GS[:, p, :], GS[:, p, :], PS[4 + p % 2], ALU.subtract).then_inc(S("g_s"), 1)

        NL = TOK * len(LEVELS)
        NCHUNK = SEQ // CH

        def pe_chunks(pe):
            for p in range(TOK):
                if p == 0:
                    pe.wait_ge(*due("g_s", NL))
                    pe.wait_ge(*due("g_ke", TOK))
                    pe.wait_ge(*due("g_uc", NL - TOK))
                if p >= 2:
                    pe.wait_ge(*due("g_wn", p - 1))
                for h in range(GH):
                    hh = slice(h * P, (h + 1) * P)
                    last = nc.tensor.matmul(PS[p % 2][:, hh], GKE[:, p, hh], GS[:, p, hh], start=True, stop=True)
                last.then_inc(S("g_w"), 1)
                if p >= 2:
                    pe.wait_ge(*due("g_uu", p - 1))
                for h in range(GH):
                    hh = slice(h * P, (h + 1) * P)
                    last = nc.tensor.matmul(PS[2 + p % 2][:, hh], GS[:, p, hh], GVB[:, p, hh], start=True, stop=True)
                last.then_inc(S("g_uraw"), 1)
            for i in range(NCHUNK):
                p, half = i // 2, slice(CH * (i % 2), CH * (i % 2) + CH)
                pe.wait_ge(*due("c_st", i + 1))
                if i == 0:
                    pe.wait_ge(*due("g_wn", TOK))
                    pe.wait_ge(*due("g_uu", TOK))
                for h in range(GH):
                    last = nc.tensor.matmul(PS[i % 2][half, h * P:(h + 1) * P], GWN[:, p, h * P + CH * (i % 2):h * P + CH * (i % 2) + CH], GST[:, i % 2, h * P:(h + 1) * P], start=True, stop=True)
                last.then_inc(S("c_ws"), 1)
                pe.wait_ge(*due("c_vn", i + 1))
                for h in range(GH):
                    hh = slice(h * P, (h + 1) * P)
                    last = nc.tensor.matmul(PS[4 + i % 2][:, hh], GKT[half, p, hh], GVN[half, i % 2, hh], start=True, stop=True)
                last.then_inc(S("c_kv"), 1)
                if i >= 2:
                    pe.wait_ge(*due("c_oc", i - 1))
                for h in range(GH):
                    hh = slice(h * P, (h + 1) * P)
                    o = PS[2 + i % 2][:, h * CH:(h + 1) * CH]
                    nc.tensor.matmul(o, GST[:, i % 2, hh], GQKV[:, h, i * CH:(i + 1) * CH], start=True, stop=False)
                    last = nc.tensor.matmul(o, GVN[half, i % 2, hh], GAT[half, p, h * P + CH * (i % 2):h * P + CH * (i % 2) + CH], start=False, stop=True)
                last.then_inc(S("c_o"), 1)
            pe_norms(pe, "go", "go_sq", GH, 16)
            pe_spreads(pe, "go", GH)

        def act_chunks(act):
            for p in range(TOK):
                act.wait_ge(*due("g_w", p + 1))
                nc.scalar.activation(GWN[:, p, :], PS[p % 2], ACT.Copy, scale=-1.0).then_inc(S("g_wn"), 1)
                act.wait_ge(*due("g_uraw", p + 1))
                nc.scalar.activation(GU_[:, p, :], PS[2 + p % 2], ACT.Copy).then_inc(S("g_uu"), 1)
            for i in range(NCHUNK):
                act.wait_ge(*due("c_o", i + 1))
                nc.scalar.activation(GO[:, :, i * CH:(i + 1) * CH], PS[2 + i % 2][:, 0:GH * CH].rearrange("p (h c) -> p h c", h=GH), ACT.Copy).then_inc(S("c_oc"), 1)
            act.wait_ge(*due("c_oc", NCHUNK))
            act_squares(act, "go", [GO[:, h, :] for h in range(GH)])
            for h in range(GH):
                act.wait_ge(*due("go_y", h + 1))
                nc.scalar.activation(XH[:, 4 + h, :], T[:, 5, :], ACT.Copy).then_inc(S("mx_hi"), 1)

        def dve_chunks(dve, step):
            dve.wait_ge(*due("g_kk", TOK))
            dve.wait_ge(*due("g_ktt", TOK))
            nc.vector.memset(GST[:, 0, :], 0.0).then_inc(S("c_st"), 1)
            dve.wait_ge(*due("g_uu", TOK))
            for i in range(NCHUNK):
                p, half, nxt = i // 2, slice(CH * (i % 2), CH * (i % 2) + CH), (i + 1) % 2
                dve.wait_ge(*due("c_st", i + 1))
                if i >= 1:
                    dve.wait_ge(*due("c_o", i))
                end = EG[:, :, i * CH + CH - 1:i * CH + CH].to_broadcast([P, GH, P])
                step(nc.vector.tensor_tensor(heads(GST[:, nxt, :]), heads(GST[:, i % 2, :]), end, ALU.mult))
                dve.wait_ge(*due("c_ws", i + 1))
                nc.vector.tensor_tensor(GVN[half, i % 2, :], GU_[half, p, :], PS[i % 2][half, :], ALU.add).then_inc(S("c_vn"), 1)
                dve.wait_ge(*due("c_kv", i + 1))
                nc.vector.tensor_tensor(GST[:, nxt, :], GST[:, nxt, :], PS[4 + i % 2], ALU.add).then_inc(S("c_st"), 1)
            x, cols = SC[:, 96:112], SM[:, 32:48]
            dve.wait_ge(*due("go_sums", GH))
            step(nc.vector.tensor_scalar(x, PS[7][:, 0:16], 1.0 / GD, RMS_EPS, ALU.mult, ALU.add))
            inverse_root(step, cols, x, scratch(16))
            dve_diags(dve, "go", cols, 0)
            for h in range(GH):
                if h < GH - 1:
                    dve_diags(dve, "go", cols, h + 1)
                dve.wait_ge(*due("go_spread", h + 1))
                nc.vector.scalar_tensor_tensor(out=T[:, 4, :], in0=GO[:, h, :], scalar=vec("out_norm"), in1=PS[4 + h % 2], op0=ALU.mult, op1=ALU.mult).then_inc(S("go_scaled"), 1)
                dve.wait_ge(*due("go_scaled", h + 1))
                nc.vector.tensor_tensor(T[:, 5, :], T[:, 4, :], GZ[:, h, :], ALU.mult).then_inc(S("go_y"), 1)
                dve.wait_ge(*due("mx_hi", h + 1))
                nc.vector.tensor_tensor(XL[:, 4 + h, :], T[:, 5, :], XH[:, 4 + h, :].bitcast(F32), ALU.subtract).then_inc(S("mx_lo"), 1)

        PMK, PMV, PMQ, PMEMO = (PH[n] for n in ("mem_k", "mem_v", "mem_q", "mem_o"))
        F2 = place("branch_out_2", YAT, [KD, SEQ])
        MRAW = place("mem_raw", YAT + 16, [KD, MEM])
        MXH = place("mem_hi", YAT + 24, [KD, MEM], F32R)
        MXL = place("mem_lo", YAT + 32, [KD, MEM], F32R)
        MKT = place("mem_k_t", YAT + 40, [KD, MEM])
        MVR = place("mem_v_rows", YAT + 48, [KM, D])
        MQ = place("mem_q_t", YAT + 56, [KD, SEQ])
        MP = place("mem_p", YAT + 72, [2, MEM])
        MPT = place("mem_pt", YAT + 74, [2, KM, SEQ])
        MCOL = SM[:, 20:22]
        MROW = place("mem_rows", YAT + 82, [MEM])
        MSQ = place("mem_sq", YAT + 83, [2, MEM])
        MACC = place("mem_acc", YAT + 85, [MEM])
        MDIAG = place("mem_diag", YAT + 86, [MEM])

        def pe_branch(pe, ph, n, ready=None):
            def body(r, parity, pair):
                for i in range(2):
                    if not (isinstance(r, int) and r < 2):
                        pe.wait_ge(*due(f"{n}_sq", r * 2 + (i - 3)))
                    feature_tile(pe, ph, r, (2 * i, 2 * i + 1), PS[2 * parity + i], XH, XL, ready if first(r) and i == 0 else None)
            rounds(pe, ph, body)

        def act_branch(act, ph, n, to):
            def body(r, parity, pair):
                for i in range(2):
                    wait(act, units_used, ph.used(r, 2 * i + 1))
                    if not (isinstance(r, int) and r == 0):
                        wait(act, *due(f"{n}_added", r * 2 + (i - 1)))
                    nc.scalar.activation(to[:, r * 2 + i, :], PS[2 * parity + i], ACT.Copy).then_inc(S(f"{n}_f"), 1)
                    nc.scalar.activation(T[:, i, :], PS[2 * parity + i], ACT.Square).then_inc(S(f"{n}_sq"), 1)
            rounds(act, ph, body)

        def dve_branch(dve, ph, n):
            def body(r, parity, pair):
                for i in range(2):
                    dve.wait_ge(*due(f"{n}_sq", r * 2 + (i + 1)))
                    if first(r) and i == 0:
                        nc.vector.tensor_copy(ACC, T[:, i, :]).then_inc(S(f"{n}_added"), 1)
                    else:
                        dve.wait_ge(*due(f"{n}_added", r * 2 + i))
                        nc.vector.tensor_tensor(ACC, ACC, T[:, i, :], ALU.add).then_inc(S(f"{n}_added"), 1)
            rounds(dve, ph, body)

        def act_mem_prepare(act):
            act.wait_ge(units_used, PMO.used(0, 0))
            act.dma_start(MRAW[:, :, :], dram["mem"]).then_inc(S("mem_in"), 16)
            act.wait_ge(*due("mem_in", 16))
            for k in range(KD):
                nc.scalar.activation(MXH[:, k, :], MRAW[:, k, :], ACT.Copy, scale=vec("mem_kv", k)).then_inc(S("m_hi"), 1)
                if k >= 2:
                    act.wait_ge(*due("m_added", k - 1))
                nc.scalar.activation(MSQ[:, k % 2, :], MRAW[:, k, :], ACT.Square).then_inc(S("m_sq"), 1)

        def dve_mem_prepare(dve):
            dve.wait_ge(*due("mem_in", 16))
            for k in range(KD):
                dve.wait_ge(*due("m_hi", k + 1))
                nc.vector.scalar_tensor_tensor(out=MXL[:, k, :], in0=MRAW[:, k, :], scalar=vec("mem_kv", k), in1=MXH[:, k, :].bitcast(F32), op0=ALU.mult, op1=ALU.subtract).then_inc(S("m_lo"), 1)
                dve.wait_ge(*due("m_sq", k + 1))
                if k == 0:
                    nc.vector.tensor_copy(MACC[:, :], MSQ[:, 0, :]).then_inc(S("m_added"), 1)
                else:
                    dve.wait_ge(*due("m_added", k))
                    nc.vector.tensor_tensor(MACC[:, :], MACC[:, :], MSQ[:, k % 2, :], ALU.add).then_inc(S("m_added"), 1)

        def pe_mem_kv(pe):
            pe_sum(pe, "mx", ACC, PS[7])
            pe_sum(pe, "m", MACC[:, :], PS[4], ntok=KM)
            pe.wait_ge(*due("m_lo", KD))
            pe_spread(pe, "mx", DIAG, PS[6])

            def keys(r, parity, pair):
                if first(r):
                    pe.wait_ge(*due("mx_sq", KD))
                for i in range(2):
                    if not (isinstance(r, int) and r < 2):
                        pe.wait_ge(*due("mk", r * 2 + (i - 3)))
                    feature_tile(pe, PMK, r, (2 * i, 2 * i + 1), PS[2 * parity + i][:, 0:MEM], MXH, MXL)
                if first(r):
                    pe_spread(pe, "m", MDIAG[:, :], PS[5], n=MEM)
            rounds(pe, PMK, keys)

            def values(r, parity, pair):
                if first(r):
                    pe.wait_ge(*due("mk", KD))

                def free(i):
                    if not (isinstance(r, int) and r < 2):
                        pe.wait_ge(*due("mv", pair * 2 + (i - 1)))
                token_tiles(pe, PMV, r, parity, PS[0:2], MXH, MXL, None, free)
            rounds(pe, PMV, values)

            def queries(r, parity, pair):
                if first(r):
                    pe.wait_ge(*due("mv", 4))
                for i in range(2):
                    if not (isinstance(r, int) and r < 2):
                        pe.wait_ge(*due("mq", r * 2 + (i - 3)))
                    feature_tile(pe, PMQ, r, (2 * i, 2 * i + 1), PS[2 * parity + i], XH, XL,
                                 (lambda k: pe.wait_ge(*due("s4_lo", k + 1))) if first(r) and i == 0 else None)
                    if first(r):
                        if i == 0:
                            pe_sum(pe, "s4", ACC, PS[7])
                        else:
                            pe_spread(pe, "s4", DIAG, PS[6])
            rounds(pe, PMQ, queries)

        def act_mem_kv(act):
            act_rows(act, "mx", PS[6], RB[:, :])
            act_rows(act, "m", PS[5], MROW[:, :], n=MEM)
            act_join(act, "mx", "s4", "mem_pre")

            def values(r, parity, pair):
                if parity:
                    wait(act, units_used, PMV.used(r, 3))
                    for i in range(KM):
                        nc.scalar.activation(MVR[:, i, bass.ds(pair * SEQ, SEQ)], PS[i], ACT.Copy, scale=MCOL[:, i:i + 1]).then_inc(S("mv"), 1)
            rounds(act, PMV, values)
            act_rows(act, "s4", PS[6], RB[:, :])

        def dve_mem_kv(dve, step):
            dve_column(dve, step, "mx", PS[7][:, 0:4], COL, D, RMS_EPS)
            dve_diag(dve, step, "mx", COL, DIAG)
            dve_column(dve, step, "m", PS[4][:, 0:2], MCOL, D, RMS_EPS, n=KM)
            dve_diag(dve, step, "m", MCOL, MDIAG[:, :], n=KM)
            dve.wait_ge(*due("m_rb", 1))

            def key_tile(k):
                dve.wait_ge(units_used, PMK.used(k // 2, 2 * (k % 2) + 1))
                nc.vector.tensor_tensor(MKT[:, k, :], PS[k % 4][:, 0:MEM], MROW[:, :], ALU.mult).then_inc(S("mk"), 1)
            dve_join(dve, step, "mx", "mix_post", 1.0, "s4", "mem_pre", f=F2, between=key_tile)
            dve_column(dve, step, "s4", PS[7][:, 0:4], COL, D, RMS_EPS)
            dve_diag(dve, step, "s4", COL, DIAG)
            dve.wait_ge(*due("s4_rb", 1))

            def queries(r, parity, pair):
                for i in range(2):
                    dve.wait_ge(units_used, PMQ.used(r, 2 * i + 1))
                    nc.vector.scalar_tensor_tensor(out=MQ[:, r * 2 + i, :], in0=PS[2 * parity + i], scalar=MHD ** -0.5, in1=RB[:, :], op0=ALU.mult, op1=ALU.mult).then_inc(S("mq"), 1)
            rounds(dve, PMQ, queries)

        MSTEPS = MH * TOK

        def pe_mem_attention(pe):
            pe.wait_ge(*due("mq", KD))
            for i in range(MSTEPS + 5):
                h, qt = divmod(i, TOK)
                if i < MSTEPS:
                    if i >= 2:
                        pe.wait_ge(*due("ma_e", i - 1))
                    for d in range(2):
                        last = nc.tensor.matmul(PS[i % 2][:, 0:MEM], MQ[:, 2 * h + d, tile_of(qt)], MKT[:, 2 * h + d, :], start=d == 0, stop=d == 1)
                    last.then_inc(S("ma_s"), 1)
                j = i - 2
                if 0 <= j < MSTEPS:
                    pe.wait_ge(*due("ma_p", j + 1))
                    if j >= 2:
                        pe.wait_ge(*due("ma_pt", j - 1))
                    for kt in range(KM):
                        last = nc.tensor.transpose(PS[2 + j % 2][:, kt * P:(kt + 1) * P], MP[:, j % 2, kt * P:(kt + 1) * P], IDENT[:, :])
                    last.then_inc(S("ma_t"), 1)
                if i >= 8 and qt == 0:
                    g = h - 2
                    pe.wait_ge(*due("ma_pt", TOK * (g + 1)))
                    for d in range(2):
                        if g >= 1:
                            pe.wait_ge(*due("ma_lo", 2 * (g - 1) + d + 1))
                        for kt in range(KM):
                            last = nc.tensor.matmul(PS[4 + d], MVR[:, kt, (2 * g + d) * P:(2 * g + d + 1) * P], MPT[:, g % 2, kt, :], start=kt == 0, stop=kt == KM - 1)
                        last.then_inc(S("ma_o"), 1)

        def act_mem_attention(act):
            MXC, SUMC = SC[:, 0:32], SC[:, 32:64]
            for i in range(MSTEPS + 4):
                h, qt = divmod(i, TOK)
                if i < MSTEPS:
                    act.wait_ge(*due("ma_nm", i + 1))
                    if i >= 2:
                        act.wait_ge(*due("ma_t", i - 1))
                    nc.scalar.activation(MP[:, i % 2, :], PS[i % 2][:, 0:MEM], ACT.Exp, bias=MXC[:, i:i + 1], accum_out=SUMC[:, i:i + 1]).then_inc(S("ma_e"), 1)
                j = i - 3
                if 0 <= j < MSTEPS:
                    jh, jq = divmod(j, TOK)
                    act.wait_ge(*due("ma_t", j + 1))
                    if jh >= 2 and jq == 0:
                        act.wait_ge(*due("ma_o", 2 * (jh - 1)))
                    nc.scalar.activation(MPT[:, jh % 2, :, tile_of(jq)], PS[2 + j % 2][:, 0:MEM].rearrange("p (k q) -> p k q", q=P), ACT.Copy).then_inc(S("ma_pt"), 1)
                if i >= 8 and qt == 3:
                    for d in range(2):
                        act_mem_hi(act, 2 * (h - 2) + d)
            for d in range(2):
                act_mem_hi(act, 2 * (MH - 1) + d)

        def act_mem_hi(act, t):
            act.wait_ge(*due("ma_o", t + 1))
            nc.scalar.activation(XH[:, t, :], PS[4 + t % 2], ACT.Copy).then_inc(S("ma_hi"), 1)

        def dve_mem_attention(dve, step):
            MXC, SUMC = SC[:, 0:32], SC[:, 32:64]

            def lo(t):
                dve.wait_ge(*due("ma_hi", t + 1))
                nc.vector.tensor_tensor(XL[:, t, :], PS[4 + t % 2], XH[:, t, :].bitcast(F32), ALU.subtract).then_inc(S("ma_lo"), 1)
            for i in range(MSTEPS + 4):
                h, qt = divmod(i, TOK)
                if i < MSTEPS:
                    dve.wait_ge(*due("ma_s", i + 1))
                    step(nc.vector.reduce_max(MXC[:, i:i + 1], PS[i % 2][:, 0:MEM], axis=AX.X))
                    nc.vector.tensor_scalar(MXC[:, i:i + 1], MXC[:, i:i + 1], -1.0, None, ALU.mult).then_inc(S("ma_nm"), 1)
                if 1 <= i <= MSTEPS:
                    j = i - 1
                    dve.wait_ge(*due("ma_e", j + 1))
                    step(nc.vector.reciprocal(SUMC[:, j:j + 1], SUMC[:, j:j + 1]))
                    nc.vector.tensor_scalar(MP[:, j % 2, :], MP[:, j % 2, :], SUMC[:, j:j + 1], None, ALU.mult).then_inc(S("ma_p"), 1)
                if i >= 8 and qt == 3:
                    for d in range(2):
                        lo(2 * (h - 2) + d)
            for d in range(2):
                lo(2 * (MH - 1) + d)

        block = ctx.enter_context(nc.Block())
        end = phases[-1].name
        reached = lambda name: name in active

        @block.sync
        def _(sp):
            sp_loads(sp)
            last = {"a_out": "a_x", "b_out": "b_x", "ffn1_down": "f1_x", "mix_out": "mx_x", "mem_o": "mo_x", "ffn2_down": "f2_x"}[end]
            for k in range(KD):
                sp.wait_ge(*due(last, k + 1))
                sp.dma_start(out[:, k, :], X[:, k, :]).then_inc(S("stored"), 16)
            sp.wait_ge(*due("stored", 16 * KD))

        @block.gpsimd
        def _(pool):
            pool_setup(pool)
            pool_split(pool)

        @block.tensor
        def _(pe):
            pe_a_v(pe)
            pe_a_ug(pe)
            pe_a_out(pe)
            if reached("b_out"):
                pe_b_in(pe)
                pe_b_out(pe)
            if reached("ffn1_down"):
                pe_ffn_up(pe, "ffn1", "s2", ("b_x", KD), lambda i: pe_between(pe, i))
                pe_ffn_down(pe, "ffn1", "f1")
            if reached("mix_out"):
                pe_mix_in(pe)
                pe_cols(pe)
                pe_fox(pe)
                pe_gdn_products(pe)
                pe_levels(pe)
                pe_chunks(pe)
                pe_branch(pe, PMO, "mx", lambda k: pe.wait_ge(*due("mx_lo", max(k - 3, 1))))
            if reached("mem_o"):
                pe_mem_kv(pe)
                pe_mem_attention(pe)
                pe_branch(pe, PMEMO, "mo", lambda k: pe.wait_ge(*due("ma_lo", k + 1)))
                pe_sum(pe, "mo", ACC, PS[7])
                pe_spread(pe, "mo", DIAG, PS[6])
            if reached("ffn2_down"):
                def between(i):
                    if i == 0:
                        pe_sum(pe, "s5", ACC, PS[7])
                    else:
                        pe_spread(pe, "s5", DIAG, PS[6])
                pe_ffn_up(pe, "ffn2", "s5", ("mo_sq", KD), between)
                pe_ffn_down(pe, "ffn2", "f2")

        @block.scalar
        def _(act):
            act_setup(act)
            act_lru_cols(act)
            act_a_v(act)
            act_a_ug(act)
            act_a_out(act)
            if reached("b_out"):
                act_b_loads(act)
                act_b_in(act)
                act_b_out(act)
            if reached("ffn1_down"):
                act_between(act)
                act_ffn_up(act, "ffn1")
                act_ffn_down(act, "ffn1", "f1")
                act_join(act, "f1", "s3", "mix_pre")
            if reached("mix_out"):
                act_mix_in(act)
                act_fox(act)
                act_gdn_products(act)
                act_levels(act)
                act_chunks(act)
                act_mem_prepare(act)
                act_branch(act, PMO, "mx", F2)
            if reached("mem_o"):
                act_mem_kv(act)
                act_mem_attention(act)
                act_branch(act, PMEMO, "mo", F2)
                act_rows(act, "mo", PS[6], RB[:, :])
                act_join(act, "mo", "s5", "ffn2_pre")
            if reached("ffn2_down"):
                act_rows(act, "s5", PS[6], RB[:, :])
                act_ffn_up(act, "ffn2")
                act_ffn_down(act, "ffn2", "f2")

        @block.vector
        def _(dve):
            step = Chain(dve, S("vector_steps"))
            dve_setup(dve, step)
            dve_lru_cols(dve, step)
            dve_a_v(dve, step)
            dve_a_ug(dve, step)
            dve_a_out(dve, step)
            if reached("b_out"):
                dve_b_in(dve, step)
                dve_b_out(dve, step)
            if reached("ffn1_down"):
                dve_between(dve, step)
                dve_ffn_up(dve, step, "ffn1")
                dve_ffn_down(dve, step, "ffn1", "f1")
                dve_join(dve, step, "f1", "ffn1_post", 0.5, "s3", "mix_pre")
            if reached("mix_out"):
                dve_mix_in(dve, step)
                dve_fox(dve, step)
                dve_gdn_products(dve, step)
                dve_levels(dve, step)
                dve_chunks(dve, step)
                dve_mem_prepare(dve)
                dve_branch(dve, PMO, "mx")
            if reached("mem_o"):
                dve_mem_kv(dve, step)
                dve_mem_attention(dve, step)
                dve_branch(dve, PMEMO, "mo")
                dve_column(dve, step, "mo", PS[7][:, 0:4], COL, D, RMS_EPS)
                dve_diag(dve, step, "mo", COL, DIAG)
                dve_join(dve, step, "mo", "mem_post", 1.0, "s5", "ffn2_pre", f=F2)
            if reached("ffn2_down"):
                dve_column(dve, step, "s5", PS[7][:, 0:4], COL, D, RMS_EPS)
                dve_diag(dve, step, "s5", COL, DIAG)
                dve.wait_ge(*due("s5_rb", 1))
                dve_ffn_up(dve, step, "ffn2")
                dve_ffn_down(dve, step, "ffn2", "f2")
                dve.wait_ge(*due("f2_rb", 1))
                for k in range(KD):
                    dve_residual(dve, step, "f2", k, "ffn2_post", 0.5, F)
    return nc



def _cols(w, m):
    k = w.shape[0] // P
    return w[:, m * P:(m + 1) * P].reshape(k, P, P).transpose(1, 0, 2)


def _tiles(w, order):
    return np.stack([np.concatenate([_cols(w, a), _cols(w, b)], 1).reshape(P, -1) for a, b in order])


def _singles(w):
    return np.stack([_cols(w, m).reshape(P, -1) for m in range(w.shape[1] // P)])


def _moving(w):
    n = w.shape[1] // 512
    return w.reshape(2, 4, P, n, 512).transpose(3, 0, 2, 1, 4).reshape(2 * n, P, 4 * 512)


def _vec(v):
    return v.reshape(-1, P).T


def layout(i):
    a = {}
    a["x"] = i["x"][0].T.reshape(KD, P, SEQ).transpose(1, 0, 2)
    w = i["a_w_in"][0]
    a["a_v"] = _moving(w[:, AW:2 * AW])
    a["a_ug"] = _tiles(w, [(m, 2 * KA + m) for m in range(KA)])
    a["a_out"] = _singles(i["a_w_out"][0])
    a["a_w_s"] = i["a_w_s"][0].transpose(2, 0, 1)
    a["a_b_s"] = i["a_b_s"][0].reshape(-1)
    w = i["b_w_in"][0]
    a["b_in"] = _tiles(w, [(m, KB + m) for m in range(KB)])
    a["b_gates"] = np.stack([i["b_gate_a_w"][0], i["b_gate_x_w"][0]], 1).transpose(2, 0, 1, 3).reshape(P, -1)
    a["b_out"] = _singles(i["b_w_out"][0])
    for f in ("ffn1", "ffn2"):
        both = np.concatenate([i[f"{f}_w_gate_2"][0], i[f"{f}_w_up_2"][0]], 1)
        a[f"{f}_up"] = _tiles(both, [(m, KF + m) for m in range(KF)])
        a[f"{f}_down"] = _singles(i[f"{f}_w_down_2"][0])
    w = i["w_in_2"][0]
    FOX, GDN = FOXH * FOXD, GH * GD
    at = np.cumsum([0, FOX, FOX, FOX, FOXH, GDN, GDN, GDN, GDN, GH, GH])
    part = [w[:, at[n]:at[n + 1]] for n in range(10)]
    a["fox_v"] = _moving(part[2])
    a["fox_qk"] = _tiles(np.concatenate(part[0:2], 1), [(m, 4 + m) for m in range(4)])
    small = np.zeros((D, P), w.dtype)
    small[:, 0:FOXH], small[:, 32:32 + GH], small[:, 64:64 + GH] = part[3], part[8], part[9]
    a["small"] = _cols(small, 0).reshape(P, 2, 4 * P).transpose(1, 0, 2)
    qkv = np.concatenate(part[4:7], 1)
    a["gdn_qkv"] = _tiles(qkv, [(m, m + 1) for m in range(0, 12, 2)])
    a["gdn_z"] = _tiles(part[7], [(0, 1), (2, 3)])
    a["mix_out"] = _tiles(i["w_out_2"][0], [(m, m + 1) for m in range(0, 8, 2)])
    pairs = [(m, m + 1) for m in range(0, 8, 2)]
    kv = i["mem_w_kv_2"][0]
    a["mem_k"], a["mem_v"] = _tiles(kv[:, :D], pairs), _moving(kv[:, D:])
    a["mem_q"], a["mem_o"] = _tiles(i["mem_w_q_2"][0], pairs), _tiles(i["mem_w_o_2"][0], pairs)
    a["mem"] = i["mem_2"][0].T.reshape(KD, P, MEM).transpose(1, 0, 2)
    column = lambda n, v: np.concatenate([np.zeros(n, v.dtype), v, np.zeros(P - n - len(v), v.dtype)])
    small_bias = np.zeros(P, w.dtype)
    small_bias[0:FOXH], small_bias[64:64 + GH] = i["fox_f_bias_2"][0], i["gdn_dt_bias_2"][0]
    vecs = {
        "norm0": i["norm_w"][0], "norm1": i["norm_w"][1], "normf": i["norm_f_w"],
        "a_ln_w": i["a_ln_w"][0], "a_ln_b": i["a_ln_b"][0], "conv": i["b_conv_w"][0].reshape(-1),
        "conv_b": i["b_conv_b"][0], "gate_a_b": i["b_gate_a_b"][0], "gate_x_b": i["b_gate_x_b"][0],
        "lam": i["b_lambda"][0], "ffn1_pre": i["ffn1_pre_norm_2"][0], "ffn1_post": i["ffn1_post_norm_2"][0],
        "mix_pre": i["mix_pre_norm_2"][0], "mix_post": i["mix_post_norm_2"][0],
        "gconv": i["gdn_conv_w_2"][0].reshape(-1), "out_norm": i["gdn_out_norm_2"][0],
        "mem_pre": i["mem_pre_norm_2"][0], "mem_kv": i["mem_kv_norm_2"][0], "mem_post": i["mem_post_norm_2"][0],
        "ffn2_pre": i["ffn2_pre_norm_2"][0], "ffn2_post": i["ffn2_post_norm_2"][0],
        "small_bias": small_bias, "a_log": column(64, i["gdn_a_log_2"][0]),
    }
    a["vecs"] = np.concatenate([_vec(vecs[name]) for name, _ in VEC_SIZES], 1)
    return a


def kernel(**inputs):
    import concourse.bacc as bacc
    from concourse.bass_utils import run_bass_kernel_spmd

    arrays = {f"in_{n}": np.ascontiguousarray(a) for n, a in layout({n: np.asarray(v) for n, v in inputs.items()}).items()}
    nc = bacc.Bacc("TRN2", target_bir_lowering=False, num_devices=1)
    dram = {n[3:]: nc.dram_tensor(n, a.shape, mybir.dt.from_np(a.dtype), kind="ExternalInput").ap() for n, a in arrays.items()}
    out = nc.dram_tensor("out", (P, KD, SEQ), F32, kind="ExternalOutput").ap()
    build(nc, dram, out)
    r = run_bass_kernel_spmd(nc, [arrays], core_ids=[0]).results[0]["out"]
    return r.transpose(1, 0, 2).reshape(D, SEQ).T.reshape(1, SEQ, D)
```

```python
from contextlib import ExitStack

import numpy as np

import concourse.bass as bass
from concourse import mybir

F32 = mybir.dt.float32
F32R = mybir.dt.float32r
I32 = mybir.dt.int32
ALU = mybir.AluOpType
ACT = mybir.ActivationFunctionType
AX = mybir.AxisListType

P = 128
SEQ = 512
TOK = SEQ // P
D = 1024
KD = D // P
AW = 2048
KA = AW // P
AG = 8
BW = 1536
KB = BW // P
FF = 2816
KF = FF // P
FOXH, FOXD = 8, 64
GH, GD = 4, 128
CH = 64
MEM = 256
KM = MEM // P
MH, MHD = 4, 256
RMS_EPS = 1e-6
LN_EPS = 1e-5
KIB = 1024

UNITS = {16: (4, 4, 4, 4), 12: (3, 3, 3, 3), 22: (6, 6, 5, 5), 4: (1, 1, 1, 1)}
SLOT = (0, 6, 12, 17)
RMAX = 22

VEC_SIZES = (
    ("norm0", KD), ("norm1", KD), ("normf", KD), ("a_ln_w", KA), ("a_ln_b", KA),
    ("conv", 4 * KB), ("conv_b", KB), ("gate_a_b", KB), ("gate_x_b", KB), ("lam", KB),
    ("ffn1_pre", KD), ("ffn1_post", KD), ("mix_pre", KD), ("mix_post", KD),
    ("gconv", 4 * 3 * GH), ("out_norm", 1), ("mem_pre", KD), ("mem_kv", KD), ("mem_post", KD),
    ("ffn2_pre", KD), ("ffn2_post", KD), ("small_bias", 1), ("a_log", 1),
)
VEC = {}
_at = 0
for _name, _n in VEC_SIZES:
    VEC[_name] = _at
    _at += _n
NVEC = _at


class Phase:

    def __init__(self, name, rounds, tiles):
        self.name, self.rounds, self.tiles = name, rounds, tiles
        self.units = UNITS[tiles]
        self.base = 0

    def used(self, r, j):
        return 4 * (self.base + r) + j + 1


PHASES = [
    Phase("a_v", 8, 16), Phase("a_ug", 16, 16), Phase("a_out", 8, 16),
    Phase("b_in", 12, 16), Phase("b_out", 8, 12),
    Phase("ffn1_up", 22, 16), Phase("ffn1_down", 8, 22),
    Phase("mem_k", 4, 16), Phase("fox_v", 2, 16), Phase("small", 2, 4), Phase("fox_qk", 4, 16),
    Phase("gdn_qkv", 6, 16), Phase("gdn_z", 2, 16), Phase("mix_out", 4, 16), Phase("mem_v", 4, 16), Phase("mem_q", 4, 16), Phase("mem_o", 4, 16),
    Phase("ffn2_up", 22, 16), Phase("ffn2_down", 8, 22),
]
PH = {ph.name: ph for ph in PHASES}


def number(phases):
    base = 0
    for ph in phases:
        ph.base = base
        base += ph.rounds
        assert ph.rounds % 2 == 0


def rounds(eng, ph, body, step=None):
    before = step.n if step else 0
    for parity in range(2):
        body(parity, parity, 0)
    if ph.rounds > 2:
        per_pair = step.n - before if step else 0
        with eng.Fori(1, ph.rounds // 2) as pair:
            if per_pair:
                step.at = pair * per_pair + before
            for parity in range(2):
                body(pair * 2 + parity, parity, pair)
        if step:
            assert step.n == before + 2 * per_pair, "a pair's steps differ from the peeled pair's"
            step.at = step.n = before + per_pair * (ph.rounds // 2)


def wait_alone(eng, sem, value, passed):
    eng.wait_ge(sem, value)
    if not isinstance(value, int):
        eng.sem_inc(passed, 1)


def _members(kind, *parts):
    return [(f"{name}_{kind}", n) for name, n in parts]


STATS = ("s0", 1), ("s1", 1), ("s2", 1), ("s2b", 1), ("m", 1), ("f1", 1), ("s3", 1), ("mx", 1), ("s4", 1), ("mo", 1), ("s5", 1), ("f2", 1)
SPLITS = ("s0", KD), ("s1", KD), ("s2", KD), ("m", KD), ("s3", KD), ("m2", KD), ("s4", KD), ("s5", KD)
SQUARES = ("s0", KD), ("s1", KD), ("s2", 2 * KD), ("m", KD), ("s3", KD), ("s4", KD), ("s5", KD)
BRANCHES = ("f1", KD), ("mx", KD), ("mo", KD), ("f2", KD)
FFNS = ("a", KA), ("ffn1", KF), ("ffn2", KF)
SHARED = [
    _members("sum", *(s for s in STATS if s[0] != "s2b")), _members("diag", *STATS), _members("rows", *STATS), _members("rb", *STATS),
    _members("hi", *SPLITS), _members("lo", *SPLITS), _members("sq", *SQUARES), _members("added", *SQUARES),
    *(_members(kind, *BRANCHES) for kind in ("f", "sq", "added")),
    _members("x", ("f1", KD), ("mx", KD), ("mo", KD - 3), ("f2", KD - 3)),
    *(_members(kind, *FFNS) for kind in ("tg", "tu", "y", "yh", "yl")),
    _members("sg", *FFNS[1:]), _members("neg", ("lam", 1), ("rows", 1)), _members("exp", ("lam", 1), ("rows", 1)),
    *(_members(kind, ("gl", 2 * GH), ("go", GH)) for kind in ("sq", "sums", "diags", "spread", "scaled")),
    *([(f"b_{b}", n * KB), (f"g_{g}", n * 3 * GH)] for b, g, n in (("xb", "xb", 1), ("xc0", "c0", 1), ("taps", "taps", 2), ("xc", "conv", 1))),
    *(_members(kind, ("fx", FOXH * TOK), ("ma", MH * TOK)) for kind in ("s", "nm", "e", "p", "t", "pt")),
    [("fx_o", FOXH), ("ma_o", 2 * MH)], [("fx_hi", FOXH // 2), ("ma_hi", 2 * MH)], [("fx_lo", FOXH // 2), ("ma_lo", 2 * MH)],
]


class Sems:

    def __init__(self, nc, ctx):
        self.nc, self.ctx, self.made, self.key, self.start = nc, ctx, {}, {}, {}
        for members in SHARED:
            total = 0
            for name, n in members:
                self.key[name], self.start[name] = members[0][0], total
                total += n

    def __call__(self, name):
        key = self.key.get(name, name)
        if key not in self.made:
            self.made[key] = self.ctx.enter_context(self.nc.semaphore(key))
        return self.made[key]

    def due(self, name, value):
        return self(name), value + self.start.get(name, 0)


class Chain:

    def __init__(self, eng, sem):
        self.eng, self.sem, self.at, self.n = eng, sem, 0, 0

    def __call__(self, instruction):
        instruction.then_inc(self.sem, 1)
        self.at = self.at + 1
        self.n += 1
        self.eng.wait_ge(self.sem, self.at)


def first(r):
    return isinstance(r, int) and r == 0


def build(nc, dram, out, phases=PHASES, dump=None):
    number(phases)
    active = {ph.name for ph in phases}
    ctx = ExitStack()
    with ctx:
        base = 16640

        def place(name, at_kib, shape, dt=F32):
            return nc.alloc_sbuf_tensor_at(name, [P] + shape, dt, offset=base + int(at_kib * KIB))

        X = place("residual", 0, [KD, SEQ])
        XH = place("x_hi", 16, [KD, SEQ], F32R)
        XL = place("x_lo", 32, [KD, SEQ], F32R)
        F = place("branch_out", 32, [KD, SEQ])
        YAT = 48
        RAW = place("raw_weights", 144, [2, RMAX, P])
        WH = place("weights_hi", 166, [RMAX, P], F32R)
        WL = place("weights_lo", 177, [RMAX, P], F32R)
        T = place("temps", 188, [7, SEQ])
        RB = place("rms_rows", 202, [SEQ])
        IDENT = place("ident", 204, [P])
        ONES = place("ones", 204.5, [P])
        V_ = place("vecs", 205, [NVEC])
        SM = place("small_cols", 206.5, [64])
        SC = place("scratch_cols", 206.75, [128])
        assert NVEC * 4 <= 1536

        def vec(name, k=0):
            return V_[:, bass.ds(VEC[name] + k, 1)] if not isinstance(k, int) else V_[:, VEC[name] + k:VEC[name] + k + 1]

        PS = [ctx.enter_context(nc.psum_tensor(f"bank{i}", [P, SEQ], F32))[:, :] for i in range(8)]

        S = Sems(nc, ctx)
        due = S.due
        units_ready, units_used = S("units_ready"), S("units_used")

        def wait(eng, sem, value):
            wait_alone(eng, sem, value, S("scalar_passed") if eng is nc.scalar else S("gpsimd_passed"))

        A_X = place("a_x", YAT, [KD, SEQ])
        A_YH = place("a_y_hi", YAT, [KA, SEQ], F32R)
        A_YL = place("a_y_lo", YAT + 32, [KA, SEQ], F32R)
        A_V = place("a_v", YAT + 64, [TOK, AW])
        A_WS = place("a_w_s", 0, [AG, P])
        A_RS = place("a_row_sums", 4, [AG, P])
        A_BS = place("a_b_s", 8, [AG, P])
        A_VN = place("a_v_normed", 12, [2, TOK, P])
        B_YH = place("b_y_hi", YAT, [KB, SEQ], F32R)
        B_YL = place("b_y_lo", YAT + 24, [KB, SEQ], F32R)
        B_GW = place("b_gate_w", YAT + 48, [KB, 2, P])
        B_ST = place("b_gate_stage", YAT + 60, [2, 2, P])
        B_XB = place("b_xb", YAT + 62, [2, SEQ + 8])
        B_XC = place("b_xc", YAT + 66.5, [2, SEQ])
        B_TG = place("b_tg", YAT + 70.5, [2, SEQ])
        B_TMP = place("b_temps", YAT + 74.5, [10, SEQ])
        Y_H = place("ffn_y_hi", YAT, [KF, SEQ], F32R)
        Y_L = place("ffn_y_lo", YAT + 44, [KF, SEQ], F32R)

        def sp_loads(sp):
            for ph in phases:
                src = dram[ph.name]

                def body(r, parity, pair, ph=ph, src=src):
                    if isinstance(r, int) and ph.base + r == 0:
                        at = 0
                        for j, n in enumerate(ph.units):
                            sp.dma_start(RAW[:, 0, at:at + n, :].rearrange("p t n -> p (t n)"), src[0][:, at * P:(at + n) * P]).then_inc(S(f"raw_first{j}"), 16)
                            at += n
                        return
                    if not (isinstance(r, int) and ph.base + r < 2):
                        sp.wait_ge(units_ready, 4 * (ph.base - 1) + 4 * r)
                    sp.dma_start(RAW[:, parity, 0:ph.tiles, :].rearrange("p t n -> p (t n)"), src[r]).then_inc(S(f"raw{parity}"), 16)
                rounds(sp, ph, body)

        def pool_split(pool):
            for ph in phases:
                after_first = None
                if ph.name == "a_ug":
                    pool_causal_w_s(pool)
                elif ph.name == "fox_qk":
                    pool_causal_mask(pool)
                elif ph.name == "gdn_z":
                    pool_masks(pool)
                elif ph.name == "mix_out":
                    pool_fox_lo(pool)
                    pool_levels(pool)
                    pool_gates(pool)
                elif ph.name == "ffn2_up":
                    after_first = lambda: pool_residuals(pool, "mo", "mem_post", 1.0, F2)

                def body(r, parity, pair, ph=ph, after_first=after_first):
                    very_first = isinstance(r, int) and ph.base + r == 0
                    if not very_first:
                        pool.wait_ge(*due(f"raw{parity}", pair * 16 + (8 * ph.base + 16 * parity)))
                    at = 0
                    for j, n in enumerate(ph.units):
                        if very_first:
                            pool.wait_ge(*due(f"raw_first{j}", 16))
                        hi, lo = WH[:, SLOT[j]:SLOT[j] + n, :], WL[:, SLOT[j]:SLOT[j] + n, :]
                        raw = RAW[:, parity, at:at + n, :]
                        at += n
                        if not (isinstance(r, int) and ph.base + r == 0):
                            wait(pool, units_used, 4 * (ph.base - 1) + j + 1 + 4 * r)
                        nc.gpsimd.tensor_scalar(hi, raw, 1.0, 0.0, ALU.mult, ALU.add).then_inc(S("units_hi"), 1)
                        pool.wait_ge(*due("units_hi", 4 * ph.base + j + 1 + 4 * r))
                        nc.gpsimd.tensor_tensor(lo, raw, hi.bitcast(F32), ALU.subtract).then_inc(units_ready, 1)
                    if first(r) and after_first:
                        after_first()
                rounds(pool, ph, body)

        def feature_tile(pe, ph, r, js, ps, xh, xl, ready=None):
            k, last_k = 0, sum(ph.units[j] for j in js) - 1
            for j in js:
                pe.wait_ge(units_ready, ph.used(r, j))
                for t in range(ph.units[j]):
                    if ready:
                        ready(k)
                    wh, wl = WH[:, SLOT[j] + t, :], WL[:, SLOT[j] + t, :]
                    nc.tensor.matmul(ps, wh, xh[:, k, :], start=k == 0, stop=False)
                    nc.tensor.matmul(ps, wl, xh[:, k, :], start=False, stop=False)
                    last = nc.tensor.matmul(ps, wh, xl[:, k, :], start=False, stop=k == last_k)
                    k += 1
                last.then_inc(units_used, 1)

        def token_tiles(pe, ph, r, parity, banks, xh, xl, ready=None, free=None):
            for j in range(4):
                k = 4 * parity + j
                pe.wait_ge(units_ready, ph.used(r, j))
                if ready:
                    ready(k)
                wh = WH[:, SLOT[j]:SLOT[j] + 4, :].rearrange("p t n -> p (t n)")
                wl = WL[:, SLOT[j]:SLOT[j] + 4, :].rearrange("p t n -> p (t n)")
                for i, bank in enumerate(banks):
                    if k == 0 and free:
                        free(i)
                    tok = slice(i * P, (i + 1) * P)
                    nc.tensor.matmul(bank, xh[:, k, tok], wh, start=k == 0, stop=False)
                    nc.tensor.matmul(bank, xh[:, k, tok], wl, start=False, stop=False)
                    last = nc.tensor.matmul(bank, xl[:, k, tok], wh, start=False, stop=k == KD - 1)
                last.then_inc(units_used, 1)

        def bank_free(pe, name, r):
            if not (isinstance(r, int) and r < 2):
                pe.wait_ge(*due(name, r - 1))

        def pe_sum(pe, name, acc, ps, count=KD, ntok=TOK):
            pe.wait_ge(*due(f"{name}_added", count))
            for i in range(ntok):
                last = nc.tensor.matmul(ps[:, i:i + 1], acc[:, i * P:(i + 1) * P], ONES[:, 0:1], start=True, stop=True)
            last.then_inc(S(f"{name}_sum"), 1)

        def pe_spread(pe, name, diag, ps, n=SEQ):
            pe.wait_ge(*due(f"{name}_diag", 1))
            nc.tensor.matmul(ps[:, 0:n], ONES[:, :], diag, start=True, stop=True).then_inc(S(f"{name}_rows"), 1)

        def inverse_root(step, out_, x, scratch):
            y, z, w = scratch
            step(nc.vector.tensor_scalar(y.bitcast(I32), x.bitcast(I32), -0.5, float(0x5F3759DF), ALU.mult, ALU.add))
            step(nc.vector.tensor_scalar(w, x, -0.5, None, ALU.mult))
            for i in range(3):
                step(nc.vector.tensor_tensor(z, y, y, ALU.mult))
                step(nc.vector.tensor_tensor(z, z, w, ALU.mult))
                step(nc.vector.scalar_tensor_tensor(out=out_ if i == 2 else y, in0=z, scalar=1.5, in1=y, op0=ALU.add, op1=ALU.mult))

        def scratch(n, k=3):
            return [SC[:, i * 32:i * 32 + n] for i in range(k)]

        def dve_column(dve, step, name, ps, col, width, eps, n=TOK):
            dve.wait_ge(*due(f"{name}_sum", 1))
            x = SC[:, 96:96 + n]
            step(nc.vector.tensor_scalar(x, ps, 1.0 / width, eps, ALU.mult, ALU.add))
            inverse_root(step, col, x, scratch(n))

        def dve_diag(dve, step, name, col, diag, n=TOK):
            nc.vector.tensor_tensor(
                diag.rearrange("p (a b) -> p a b", b=P),
                IDENT[:, :].unsqueeze(1).to_broadcast([P, n, P]),
                col.unsqueeze(2).to_broadcast([P, n, P]), ALU.mult).then_inc(S(f"{name}_diag"), 1)

        def act_split(act, name, k, parity, src, gain, ready, sq_scales=(None,)):
            ready()
            n = len(sq_scales)
            nc.scalar.activation(XH[:, k, :], src, ACT.Copy, scale=gain).then_inc(S(f"{name}_hi"), 1)
            for q, sc in enumerate(sq_scales):
                if not (isinstance(k, int) and k < 2):
                    wait(act, *due(f"{name}_added", (k - 1) * n))
                kw = {} if sc is None else {"scale": sc}
                nc.scalar.activation(T[:, 2 * q + parity, :], src, ACT.Square, **kw).then_inc(S(f"{name}_sq"), 1)

        def dve_split(dve, name, k, parity, src, gain, accs):
            dve.wait_ge(*due(f"{name}_hi", k + 1))
            nc.vector.scalar_tensor_tensor(out=XL[:, k, :], in0=src, scalar=gain, in1=XH[:, k, :].bitcast(F32), op0=ALU.mult, op1=ALU.subtract).then_inc(S(f"{name}_lo"), 1)
            n = len(accs)
            for q, acc in enumerate(accs):
                dve.wait_ge(*due(f"{name}_sq", k * n + (q + 1)))
                sq = T[:, 2 * q + parity, :]
                if first(k):
                    nc.vector.tensor_copy(acc, sq).then_inc(S(f"{name}_added"), 1)
                else:
                    dve.wait_ge(*due(f"{name}_added", (k - 1) * n + q + 1))
                    nc.vector.tensor_tensor(acc, acc, sq, ALU.add).then_inc(S(f"{name}_added"), 1)

        def x_gate(pe, name, on=lambda r: first(r)):
            return lambda k: pe.wait_ge(*due(f"{name}_lo", k + 1))

        ACC, ACC2, DIAG = T[:, 4, :], T[:, 5, :], T[:, 6, :]

        def act_rows(act, name, ps, dst, n=SEQ):
            wait(act, *due(f"{name}_rows", 1))
            nc.scalar.activation(dst, ps[:, 0:n], ACT.Copy).then_inc(S(f"{name}_rb"), 1)

        PV, PU, PO = PH["a_v"], PH["a_ug"], PH["a_out"]
        COL = SM[:, 0:4]
        MV = SM[:, 8:16].rearrange("p (t c) -> p t c", c=2)
        RSTD = SM[:, 16:20]

        def act_setup(act):
            for i in range(4):
                act.dma_start(A_X[:, 2 * i:2 * i + 2, :], dram["x"][:, 2 * i:2 * i + 2, :]).then_inc(S(f"x_in{i}"), 16)
                if i == 0:
                    act.dma_start(V_[:, :], dram["vecs"]).then_inc(S("vecs_in"), 16)
            act.dma_start(A_WS[:, :, :], dram["a_w_s"]).then_inc(S("ws_in"), 16)
            act.dma_start(A_BS[:, :, :].rearrange("p g t -> p (g t)"), dram["a_b_s"].partition_broadcast(P)).then_inc(S("bs_in"), 16)
            wait(act, *due("vecs_in", 16))
            for k in range(KD):
                act_split(act, "s0", k, k % 2, A_X[:, k, :], vec("norm0", k), lambda: wait(act, *due(f"x_in{k // 2}", 16)))

        def dve_setup(dve, step):
            nc.vector.memset(ONES[:, :], 1.0).then_inc(S("ones"), 1)
            dve.wait_ge(*due("vecs_in", 16))
            for k in range(KD):
                dve.wait_ge(*due(f"x_in{k // 2}", 16))
                dve_split(dve, "s0", k, k % 2, A_X[:, k, :], vec("norm0", k), [ACC])
            dve.wait_ge(*due("ident", 2))
            dve_column(dve, step, "s0", PS[7][:, 0:4], COL, D, RMS_EPS)
            dve_diag(dve, step, "s0", COL, DIAG)

        def pool_setup(pool):
            nc.gpsimd.memset(IDENT[:, :], 0.0).then_inc(S("ident"), 1)
            pool.wait_ge(*due("ident", 1))
            nc.gpsimd.affine_select(out=IDENT[:, :], in_=IDENT[:, :], compare_op=ALU.not_equal, fill=1.0, base=0,
                                    pattern=[[-1, P]], channel_multiplier=1).then_inc(S("ident"), 1)

        def pool_causal_w_s(pool):
            pool.wait_ge(*due("ws_in", 16))
            nc.gpsimd.affine_select(out=A_WS[:, :, :], in_=A_WS[:, :, :], compare_op=ALU.is_ge, fill=0.0, base=0,
                                    pattern=[[0, AG], [1, P]], channel_multiplier=-1).then_inc(S("ws_causal"), 1)

        def pe_a_v(pe):
            def body(r, parity, pair):
                def ready(k):
                    if isinstance(r, int) and r < 2:
                        pe.wait_ge(*due("s0_lo", k + 1))

                def free(i):
                    if not isinstance(r, int):
                        pe.wait_ge(*due("a_v_free", pair * 4 + (i - 3)))
                token_tiles(pe, PV, r, parity, PS[0:4], XH, XL, ready, free)
                if first(r):
                    pe.wait_ge(*due("ones", 1))
                    pe_sum(pe, "s0", ACC, PS[7])
                elif isinstance(r, int):
                    pe_spread(pe, "s0", DIAG, PS[6])
            rounds(pe, PV, body)

        def act_a_v(act):
            def body(r, parity, pair):
                if parity:
                    if isinstance(r, int):
                        wait(act, *due("s0_diag", 1))
                    wait(act, units_used, PV.used(r, 3))
                    for i in range(TOK):
                        nc.scalar.activation(A_V[:, i, bass.ds(pair * SEQ, SEQ)], PS[i], ACT.Gelu_apprx_tanh, scale=COL[:, i:i + 1]).then_inc(S("a_v_free"), 1)
                    if isinstance(r, int):
                        act_rows(act, "s0", PS[6], RB[:, :])
            rounds(act, PV, body)

        def dve_a_v(dve, step):
            BN = T[:, 5, 0:96].rearrange("p (t b s) -> p t b s", t=TOK, s=6)

            def body(r, parity, pair):
                if parity:
                    for i in range(TOK):
                        dve.wait_ge(*due("a_v_free", pair * 4 + (i + 1)))
                        step(nc.vector.bn_stats(BN[:, i, pair, :], A_V[:, i, bass.ds(pair * SEQ, SEQ)]))
            rounds(dve, PV, body, step)
            for i in range(TOK):
                step(nc.vector.bn_aggr(MV[:, i, :], BN[:, i, :, :].rearrange("p b s -> p (b s)")))
            x = SC[:, 96:100]
            step(nc.vector.tensor_scalar(x, MV[:, :, 1], LN_EPS, None, ALU.add))
            inverse_root(step, RSTD, x, scratch(TOK))

        def pe_a_ug(pe):
            for half in range(2):
                if half == 0:
                    pe.wait_ge(*due("ws_causal", 1))
                    pe.wait_ge(*due("a_v_free", TOK * PV.rounds // 2))
                nc.tensor.matmul(PS[4 + half], ONES[:, :], A_WS[:, 4 * half:4 * half + 4, :].rearrange("p g t -> p (g t)"), start=True, stop=True).then_inc(S("ws_sums"), 1)

            def body(r, parity, pair):
                for i, read in enumerate(("a_tu", "a_tg")):
                    bank_free(pe, read, r)
                    feature_tile(pe, PU, r, (2 * i, 2 * i + 1), PS[2 * parity + i], XH, XL)
                pe.wait_ge(*due("a_vn", r + 1))
                if not (isinstance(r, int) and r < 2):
                    pe.wait_ge(*due("a_s_read", r - 1))
                elif first(r):
                    pe.wait_ge(*due("ws_sums_copied", 2))
                for n in range(TOK):
                    last = nc.tensor.matmul(PS[4 + parity][:, n * P:(n + 1) * P], A_VN[:, parity, n, :], A_WS[:, pair, :], start=True, stop=True)
                last.then_inc(S("a_spatial"), 1)
            rounds(pe, PU, body)

        def act_a_ug(act):
            for half in range(2):
                wait(act, *due("ws_sums", half + 1))
                nc.scalar.activation(A_RS[:, 4 * half:4 * half + 4, :].rearrange("p g t -> p (g t)"), PS[4 + half], ACT.Copy).then_inc(S("ws_sums_copied"), 1)

            def body(r, parity, pair):
                wait(act, *due("a_tu", r + 1))
                nc.scalar.activation(T[:, 3, :], T[:, 0, :], ACT.Gelu_apprx_tanh).then_inc(S("a_gu"), 1)
                wait(act, *due("a_tg", r + 1))
                nc.scalar.activation(T[:, 4, :], T[:, 1, :], ACT.Tanh, scale=0.5).then_inc(S("a_th"), 1)
                wait(act, *due("a_y", r + 1))
                nc.scalar.activation(A_YH[:, r, :], T[:, 5, :], ACT.Copy).then_inc(S("a_yh"), 1)
            rounds(act, PU, body)

        def dve_a_ug(dve, step):
            dve.wait_ge(*due("s0_rb", 1))
            dve.wait_ge(*due("ws_sums_copied", 2))
            dve.wait_ge(*due("bs_in", 16))

            def body(r, parity, pair):
                if not (isinstance(r, int) and r < 2):
                    dve.wait_ge(*due("a_spatial", r - 1))
                for n in range(TOK):
                    last = nc.vector.tensor_scalar(A_VN[:, parity, n, :], A_V[:, n, bass.ds(r * P, P)], MV[:, n, 0:1], RSTD[:, n:n + 1], ALU.subtract, ALU.mult)
                last.then_inc(S("a_vn"), 1)
                dve.wait_ge(units_used, PU.used(r, 1))
                nc.vector.tensor_tensor(T[:, 0, :], PS[2 * parity], RB[:, :], ALU.mult).then_inc(S("a_tu"), 1)
                dve.wait_ge(units_used, PU.used(r, 3))
                nc.vector.tensor_tensor(T[:, 1, :], PS[2 * parity + 1], RB[:, :], ALU.mult).then_inc(S("a_tg"), 1)
                step(nc.vector.scalar_tensor_tensor(out=T[:, 6, 0:P], in0=A_RS[:, pair, :], scalar=vec("a_ln_b", r), in1=A_BS[:, pair, :], op0=ALU.mult, op1=ALU.add))
                dve.wait_ge(*due("a_spatial", r + 1))
                nc.vector.scalar_tensor_tensor(
                    out=T[:, 2, :].rearrange("p (n t) -> p n t", n=TOK), in0=PS[4 + parity].rearrange("p (n t) -> p n t", n=TOK),
                    scalar=vec("a_ln_w", r), in1=T[:, 6, 0:P].unsqueeze(1).to_broadcast([P, TOK, P]), op0=ALU.mult, op1=ALU.add).then_inc(S("a_s_read"), 1)
                dve.wait_ge(*due("a_s_read", r + 1))
                dve.wait_ge(*due("a_gu", r + 1))
                step(nc.vector.tensor_tensor(T[:, 2, :], T[:, 2, :], T[:, 3, :], ALU.mult))
                dve.wait_ge(*due("a_th", r + 1))
                dve.wait_ge(*due("a_tg", r + 1))
                step(nc.vector.scalar_tensor_tensor(out=T[:, 4, :], in0=T[:, 4, :], scalar=1.0, in1=T[:, 1, :], op0=ALU.add, op1=ALU.mult))
                nc.vector.scalar_tensor_tensor(out=T[:, 5, :], in0=T[:, 4, :], scalar=0.5, in1=T[:, 2, :], op0=ALU.mult, op1=ALU.mult).then_inc(S("a_y"), 1)
                dve.wait_ge(*due("a_yh", r + 1))
                nc.vector.tensor_tensor(A_YL[:, r, :], T[:, 5, :], A_YH[:, r, :].bitcast(F32), ALU.subtract).then_inc(S("a_yl"), 1)
            rounds(dve, PU, body, step)

        def pe_a_out(pe):
            pe.wait_ge(*due("a_tg", PU.rounds))

            def body(r, parity, pair):
                bank_free(pe, "a_x", r)
                feature_tile(pe, PO, r, range(4), PS[parity], A_YH, A_YL,
                             (lambda k: pe.wait_ge(*due("a_yl", k + 1))) if first(r) else None)
            rounds(pe, PO, body)

        def act_a_out(act):
            wait(act, *due("a_yl", KA))
            act.dma_start(X[:, :, :], dram["x"]).then_inc(S("x_again"), 16)
            rounds(act, PO, lambda r, parity, pair: act_split(
                act, "s1", r, parity, X[:, r, :], vec("norm1", r), lambda: wait(act, *due("a_x", r + 1))))

        def dve_a_out(dve, step):
            dve.wait_ge(*due("x_again", 16))

            def body(r, parity, pair):
                dve.wait_ge(units_used, PO.used(r, 3))
                nc.vector.tensor_tensor(X[:, r, :], PS[parity], X[:, r, :], ALU.add).then_inc(S("a_x"), 1)
                dve_split(dve, "s1", r, parity, X[:, r, :], vec("norm1", r), [ACC])
            rounds(dve, PO, body)

        PB, PBO = PH["b_in"], PH["b_out"]
        LC = place("lru_cols", 207.25, [4, KB])
        N4, P4, HBA, HBX = (LC[:, i, :] for i in range(4))
        NG = SM[:, 24:32]

        def log1p_exp_neg_abs(dve, step, name, out_, x, e, s2):
            step(nc.vector.tensor_scalar(e, x, -1.0, None, ALU.mult))
            nc.vector.tensor_tensor(e, e, x, ALU.min).then_inc(S(f"{name}_neg"), 1)
            dve.wait_ge(*due(f"{name}_exp", 1))
            step(nc.vector.tensor_scalar(s2, e, 2.0, None, ALU.add))
            step(nc.vector.reciprocal(s2, s2))
            step(nc.vector.tensor_tensor(e, e, s2, ALU.mult))
            step(nc.vector.tensor_tensor(s2, e, e, ALU.mult))
            step(nc.vector.tensor_scalar(out_, s2, 1.0 / 17, None, ALU.mult))
            for n in (15, 13, 11, 9, 7, 5, 3):
                step(nc.vector.scalar_tensor_tensor(out=out_, in0=out_, scalar=1.0 / n, in1=s2, op0=ALU.add, op1=ALU.mult))
            step(nc.vector.scalar_tensor_tensor(out=out_, in0=out_, scalar=1.0, in1=e, op0=ALU.add, op1=ALU.mult))
            step(nc.vector.tensor_scalar(out_, out_, 2.0, None, ALU.mult))

        def act_exp_neg(act, name, e):
            wait(act, *due(f"{name}_neg", 1))
            nc.scalar.activation(e, e, ACT.Exp).then_inc(S(f"{name}_exp"), 1)

        def act_lru_cols(act):
            act_exp_neg(act, "lam", SC[:, 0:KB])

        def dve_lru_cols(dve, step):
            lam = V_[:, VEC["lam"]:VEC["lam"] + KB]
            log1p_exp_neg_abs(dve, step, "lam", P4, lam, SC[:, 0:KB], SC[:, 32:32 + KB])
            t = SC[:, 64:64 + KB]
            step(nc.vector.tensor_scalar(t, lam, -1.0, 0.0, ALU.mult, ALU.max))
            step(nc.vector.tensor_tensor(P4, P4, t, ALU.add))
            step(nc.vector.tensor_scalar(P4, P4, 4.0, None, ALU.mult))
            step(nc.vector.tensor_scalar(N4, P4, -1.0, None, ALU.mult))
            step(nc.vector.tensor_scalar(HBA, V_[:, VEC["gate_a_b"]:VEC["gate_a_b"] + KB], 0.5, None, ALU.mult))
            step(nc.vector.tensor_scalar(HBX, V_[:, VEC["gate_x_b"]:VEC["gate_x_b"] + KB], 0.5, None, ALU.mult))
            nc.vector.tensor_tensor(NG, V_[:, VEC["normf"]:VEC["normf"] + KD], V_[:, VEC["ffn1_pre"]:VEC["ffn1_pre"] + KD], ALU.mult).then_inc(S("lru_cols"), 1)

        def act_b_loads(act):
            wait(act, units_used, PO.used(PO.rounds - 1, 3))
            act.dma_start(B_GW[:, :, :, :].rearrange("p h g n -> p (h g n)"), dram["b_gates"]).then_inc(S("gates_in"), 16)

        XB0 = 8

        def pe_b_in(pe):
            def gates(r, parity):
                pe.wait_ge(*due("b_xc", r + 1))
                pe.wait_ge(*due("b_stage", r + 1))
                if not (isinstance(r, int) and r < 2):
                    pe.wait_ge(*due("b_thi", r - 1))
                for g in range(2):
                    nc.tensor.matmul(PS[4 + 2 * parity + g], B_ST[:, parity, g, :], B_XC[:, parity, :], start=True, stop=True).then_inc(S("b_gates"), 1)

            def body(r, parity, pair):
                if first(r):
                    pe.wait_ge(*due("a_x", PO.rounds))
                bank_free(pe, "b_xb", r)
                feature_tile(pe, PB, r, (0, 1), PS[2 * parity], XH, XL,
                             (lambda k: pe.wait_ge(*due("s1_lo", k + 1))) if first(r) else None)
                if first(r):
                    pe_sum(pe, "s1", ACC, PS[7])
                else:
                    gates(r - 1, 1 - parity)
                bank_free(pe, "b_tg", r)
                feature_tile(pe, PB, r, (2, 3), PS[2 * parity + 1], XH, XL)
                if first(r):
                    pe_spread(pe, "s1", DIAG, PS[6])
            rounds(pe, PB, body)
            gates(PB.rounds - 1, 1)

        def act_b_in(act):
            def post(r, parity):
                TR, A_, TL, A2, TI, SQ, TG_ = (B_TMP[:, i, :] for i in (0, 1, 2, 3, 4, 5, 6))
                wait(act, *due("b_gates", 2 * r + 1))
                if not first(r):
                    wait(act, *due("b_scan", r))
                step_a = nc.scalar.activation(TR, PS[4 + 2 * parity], ACT.Tanh, scale=0.5, bias=HBA[:, bass.ds(r, 1)])
                step_a.then_inc(S("b_thr"), 1)
                wait(act, *due("b_gates", 2 * r + 2))
                nc.scalar.activation(TI, PS[5 + 2 * parity], ACT.Tanh, scale=0.5, bias=HBX[:, bass.ds(r, 1)]).then_inc(S("b_thi"), 1)
                wait(act, *due("b_thr", r + 1))
                nc.scalar.activation(A_, TR, ACT.Exp, scale=N4[:, bass.ds(r, 1)], bias=N4[:, bass.ds(r, 1)]).then_inc(S("b_a"), 1)
                nc.scalar.activation(TL, TR, ACT.Tanh, scale=P4[:, bass.ds(r, 1)], bias=P4[:, bass.ds(r, 1)]).then_inc(S("b_tl"), 1)
                wait(act, *due("b_a", r + 1))
                nc.scalar.activation(A2, A_, ACT.Square).then_inc(S("b_a2"), 1)
                wait(act, *due("b_tg", r + 1))
                nc.scalar.activation(TG_, B_TG[:, parity, :], ACT.Tanh, scale=0.5).then_inc(S("b_thg"), 1)
                wait(act, *due("b_m2", r + 1))
                nc.scalar.activation(SQ, A2, ACT.Sqrt).then_inc(S("b_mult"), 1)
                wait(act, *due("b_y", r + 1))
                nc.scalar.activation(B_YH[:, r, :], B_TMP[:, 7, :], ACT.Copy).then_inc(S("b_yh"), 1)

            def body(r, parity, pair):
                if first(r):
                    wait(act, *due("gates_in", 16))
                    act_rows(act, "s1", PS[6], RB[:, :])
                wait(act, *due("b_xb", r + 1))
                nc.scalar.activation(B_XC[:, parity, :], B_XB[:, parity, XB0:XB0 + SEQ], ACT.Identity,
                                     scale=V_[:, bass.ds(VEC["conv"] + 3 * KB + r, 1)], bias=V_[:, bass.ds(VEC["conv_b"] + r, 1)]).then_inc(S("b_xc0"), 1)
                if not (isinstance(r, int) and r < 2):
                    wait(act, *due("b_gates", 2 * r - 2))
                nc.scalar.activation(B_ST[:, parity, :, :], B_GW[:, r, :, :], ACT.Copy).then_inc(S("b_stage"), 1)
                if not first(r):
                    post(r - 1, 1 - parity)
            rounds(act, PB, body)
            post(PB.rounds - 1, 1)

        def dve_b_in(dve, step):
            dve_column(dve, step, "s1", PS[7][:, 0:4], COL, D, RMS_EPS)
            dve_diag(dve, step, "s1", COL, DIAG)

            def post(r, parity):
                A_, TL, A2, TI, SQ, TG_, Y_ = (B_TMP[:, i, :] for i in (1, 2, 3, 4, 5, 6, 7))
                BT, H_ = B_TMP[:, 8, :], B_TMP[:, 9, :]
                dve.wait_ge(*due("b_a2", r + 1))
                nc.vector.scalar_tensor_tensor(out=A2, in0=A2, scalar=1.0, in1=TL, op0=ALU.add, op1=ALU.mult).then_inc(S("b_m2"), 1)
                nc.vector.scalar_tensor_tensor(out=BT, in0=TI, scalar=1.0, in1=B_XC[:, parity, :], op0=ALU.add, op1=ALU.mult).then_inc(S("b_ix"), 1)
                dve.wait_ge(*due("b_thg", r + 1))
                nc.vector.scalar_tensor_tensor(out=Y_, in0=TG_, scalar=1.0, in1=B_TG[:, parity, :], op0=ALU.add, op1=ALU.mult).then_inc(S("b_sg"), 1)
                dve.wait_ge(*due("b_ix", r + 1))
                dve.wait_ge(*due("b_mult", r + 1))
                nc.vector.scalar_tensor_tensor(out=BT, in0=SQ, scalar=0.5, in1=BT, op0=ALU.mult, op1=ALU.mult).then_inc(S("b_bterm"), 1)
                dve.wait_ge(*due("b_bterm", r + 1))
                nc.vector.tensor_tensor_scan(H_, A_, BT, 0.0, ALU.mult, ALU.add).then_inc(S("b_scan"), 1)
                dve.wait_ge(*due("b_scan", r + 1))
                nc.vector.scalar_tensor_tensor(out=Y_, in0=Y_, scalar=0.5, in1=H_, op0=ALU.mult, op1=ALU.mult).then_inc(S("b_y"), 1)
                dve.wait_ge(*due("b_yh", r + 1))
                nc.vector.tensor_tensor(B_YL[:, r, :], Y_, B_YH[:, r, :].bitcast(F32), ALU.subtract).then_inc(S("b_yl"), 1)

            def body(r, parity, pair):
                if first(r):
                    dve.wait_ge(*due("s1_rb", 1))
                dve.wait_ge(units_used, PB.used(r, 1))
                nc.vector.tensor_tensor(B_XB[:, parity, XB0:XB0 + SEQ], PS[2 * parity], RB[:, :], ALU.mult).then_inc(S("b_xb"), 1)
                dve.wait_ge(*due("b_xc0", r + 1))
                for tap in range(3):
                    conv = nc.vector.scalar_tensor_tensor(
                        out=B_XC[:, parity, :], in0=B_XB[:, parity, XB0 - 3 + tap:XB0 - 3 + tap + SEQ],
                        scalar=V_[:, bass.ds(VEC["conv"] + tap * KB + r, 1)], in1=B_XC[:, parity, :], op0=ALU.mult, op1=ALU.add)
                    if tap < 2:
                        conv.then_inc(S("b_taps"), 1)
                        dve.wait_ge(*due("b_taps", 2 * r + (tap + 1)))
                conv.then_inc(S("b_xc"), 1)
                dve.wait_ge(*due("b_xc", r + 1))
                if not first(r):
                    post(r - 1, 1 - parity)
                dve.wait_ge(units_used, PB.used(r, 3))
                nc.vector.tensor_tensor(B_TG[:, parity, :], PS[2 * parity + 1], RB[:, :], ALU.mult).then_inc(S("b_tg"), 1)

            nc.vector.memset(B_XB[:, :, 0:8], 0.0).then_inc(S("b_pad"), 1)
            rounds(dve, PB, body)
            dve.wait_ge(*due("b_tg", PB.rounds))
            post(PB.rounds - 1, 1)

        def pe_b_out(pe):
            def body(r, parity, pair):
                if first(r):
                    pe.wait_ge(*due("b_tg", PB.rounds))
                bank_free(pe, "b_x", r)
                feature_tile(pe, PBO, r, range(4), PS[parity], B_YH, B_YL,
                             (lambda k: pe.wait_ge(*due("b_yl", k + 1))) if first(r) else None)
            rounds(pe, PBO, body)

        def act_b_out(act):
            rounds(act, PBO, lambda r, parity, pair: act_split(
                act, "s2", r, parity, X[:, r, :], NG[:, bass.ds(r, 1)], lambda: wait(act, *due("b_x", r + 1)),
                (None, vec("normf", r))))

        def dve_b_out(dve, step):
            def body(r, parity, pair):
                dve.wait_ge(units_used, PBO.used(r, 3))
                nc.vector.tensor_tensor(X[:, r, :], PS[parity], X[:, r, :], ALU.add).then_inc(S("b_x"), 1)
                dve.wait_ge(*due("b_x", r + 1))
                dve_split(dve, "s2", r, parity, X[:, r, :], NG[:, bass.ds(r, 1)], [ACC, ACC2])
            rounds(dve, PBO, body)

        def pe_ffn_up(pe, f, stat, before_bank, after_sum):
            ph = PH[f"{f}_up"]

            def body(r, parity, pair):
                if first(r):
                    pe.wait_ge(*due(before_bank[0], before_bank[1]))
                for i, read in enumerate((f"{f}_tg", f"{f}_tu")):
                    bank_free(pe, read, r)
                    feature_tile(pe, ph, r, (2 * i, 2 * i + 1), PS[2 * parity + i], XH, XL,
                                 (lambda k: pe.wait_ge(*due(f"{stat}_lo", k + 1))) if first(r) and i == 0 else None)
                    if first(r):
                        after_sum(i)
            rounds(pe, ph, body)

        def act_ffn_up(act, f):
            ph = PH[f"{f}_up"]

            def body(r, parity, pair):
                wait(act, *due(f"{f}_tg", r + 1))
                nc.scalar.activation(T[:, 2, :], T[:, 0, :], ACT.Silu).then_inc(S(f"{f}_sg"), 1)
                wait(act, *due(f"{f}_y", r + 1))
                nc.scalar.activation(Y_H[:, r, :], T[:, 3, :], ACT.Copy).then_inc(S(f"{f}_yh"), 1)
            rounds(act, ph, body)

        def dve_ffn_up(dve, step, f):
            ph = PH[f"{f}_up"]

            def body(r, parity, pair):
                dve.wait_ge(units_used, ph.used(r, 1))
                nc.vector.tensor_tensor(T[:, 0, :], PS[2 * parity], RB[:, :], ALU.mult).then_inc(S(f"{f}_tg"), 1)
                dve.wait_ge(units_used, ph.used(r, 3))
                nc.vector.tensor_tensor(T[:, 1, :], PS[2 * parity + 1], RB[:, :], ALU.mult).then_inc(S(f"{f}_tu"), 1)
                dve.wait_ge(*due(f"{f}_tu", r + 1))
                dve.wait_ge(*due(f"{f}_sg", r + 1))
                nc.vector.tensor_tensor(T[:, 3, :], T[:, 1, :], T[:, 2, :], ALU.mult).then_inc(S(f"{f}_y"), 1)
                dve.wait_ge(*due(f"{f}_yh", r + 1))
                nc.vector.tensor_tensor(Y_L[:, r, :], T[:, 3, :], Y_H[:, r, :].bitcast(F32), ALU.subtract).then_inc(S(f"{f}_yl"), 1)
            rounds(dve, ph, body)

        def act_branch_tile(act, n, k, parity, src, to=F):
            nc.scalar.activation(to[:, k, :], src, ACT.Copy).then_inc(S(f"{n}_f"), 1)
            if not (isinstance(k, int) and k < 2):
                wait(act, *due(f"{n}_added", k - 1))
            nc.scalar.activation(T[:, parity, :], src, ACT.Square).then_inc(S(f"{n}_sq"), 1)

        def dve_branch_tile(dve, n, k, parity):
            dve.wait_ge(*due(f"{n}_sq", k + 1))
            if first(k):
                nc.vector.tensor_copy(ACC, T[:, parity, :]).then_inc(S(f"{n}_added"), 1)
            else:
                dve.wait_ge(*due(f"{n}_added", k))
                nc.vector.tensor_tensor(ACC, ACC, T[:, parity, :], ALU.add).then_inc(S(f"{n}_added"), 1)

        def pe_ffn_down(pe, f, n, after=None):
            ph = PH[f"{f}_down"]

            def body(r, parity, pair):
                if first(r):
                    pe.wait_ge(*due(f"{f}_tu", PH[f"{f}_up"].rounds))
                bank_free(pe, f"{n}_sq", r)
                feature_tile(pe, ph, r, range(4), PS[parity], Y_H, Y_L,
                             (lambda k: pe.wait_ge(*due(f"{f}_yl", k + 1))) if first(r) else None)
                if after and isinstance(r, int):
                    after(r)
            rounds(pe, ph, body)

        def act_ffn_down(act, f, n, after=None):
            ph = PH[f"{f}_down"]

            def body(r, parity, pair):
                wait(act, units_used, ph.used(r, 3))
                act_branch_tile(act, n, r, parity, PS[parity])
                if after and isinstance(r, int):
                    after(r)
            rounds(act, ph, body)

        def dve_ffn_down(dve, step, f, n, after=None):
            def body(r, parity, pair):
                dve_branch_tile(dve, n, r, parity)
                if after and isinstance(r, int):
                    after(r)
            rounds(dve, PH[f"{f}_down"], body)
            dve_column(dve, step, n, PS[7][:, 0:4], COL, D, RMS_EPS)
            dve_diag(dve, step, n, COL, DIAG)

        def dve_residual(dve, step, n, k, gain, weight, f, pooled=False):
            t = T[:, 5, :]
            step(nc.vector.scalar_tensor_tensor(out=t, in0=f[:, k, :], scalar=vec(gain, k), in1=RB[:, :], op0=ALU.mult, op1=ALU.mult))
            nc.vector.scalar_tensor_tensor(out=X[:, k, :], in0=t, scalar=weight, in1=X[:, k, :], op0=ALU.mult, op1=ALU.add).then_inc(S(f"{n}_x"), 1)
            dve.wait_ge(*x_ready(n, k, pooled))

        POOL_TILES = (2, 4, 7)

        def pool_residuals(pool, n, gain, weight, f):
            for k in POOL_TILES:
                pool.wait_ge(*due(f"{n}_f", k + 1))
                nc.gpsimd.tensor_scalar(f[:, k, :], f[:, k, :], vec(gain, k), weight, ALU.mult, ALU.mult).then_inc(S("pool_scaled"), 1)
            pool.wait_ge(*due(f"{n}_rb", 1))
            pool.wait_ge(*due("pool_scaled", base_of[n] + len(POOL_TILES)))
            for i, k in enumerate(POOL_TILES):
                nc.gpsimd.tensor_tensor(f[:, k, :], f[:, k, :], RB[:, :], ALU.mult).then_inc(S("pool_scaled"), 1)
                pool.wait_ge(*due("pool_scaled", base_of[n] + len(POOL_TILES) + i + 1))
                nc.gpsimd.tensor_tensor(X[:, k, :], f[:, k, :], X[:, k, :], ALU.add).then_inc(S("pool_x"), 1)

        base_of = {"mo": 0, "f2": 2 * len(POOL_TILES)}

        def x_ready(n, k, pooled):
            if not pooled:
                return due(f"{n}_x", k + 1)
            if k in POOL_TILES:
                return due("pool_x", base_of[n] // 2 + POOL_TILES.index(k) + 1)
            return due(f"{n}_x", k + 1 - sum(q < k for q in POOL_TILES))

        def dve_join(dve, step, n, gain, weight, nxt, next_gain, f=F, pooled=False):
            dve.wait_ge(*due(f"{n}_rb", 1))
            for k in range(KD):
                if not (pooled and k in POOL_TILES):
                    dve_residual(dve, step, n, k, gain, weight, f, pooled)
                dve.wait_ge(*x_ready(n, k, pooled))
                dve_split(dve, nxt, k, k % 2, X[:, k, :], vec(next_gain, k), [ACC])

        def act_join(act, n, nxt, next_gain, before=None, pooled=False):
            for k in range(KD):
                if before:
                    before(k)
                act_split(act, nxt, k, k % 2, X[:, k, :], vec(next_gain, k), lambda: wait(act, *x_ready(n, k, pooled)))

        C2, CF = SM[:, 4:8], SM[:, 20:24]
        RB1 = T[:, 6, :]

        def pe_between(pe, i):
            if i == 0:
                pe.wait_ge(*due("s2_added", 2 * KD))
                for q, acc in enumerate((ACC, ACC2)):
                    for t in range(TOK):
                        last = nc.tensor.matmul(PS[7][:, 4 * q + t:4 * q + t + 1], acc[:, t * P:(t + 1) * P], ONES[:, 0:1], start=True, stop=True)
                last.then_inc(S("s2_sum"), 1)
            else:
                pe_spread(pe, "s2", T[:, 0, :], PS[6])
                pe_spread(pe, "s2b", T[:, 1, :], PS[5])

        def dve_between(dve, step):
            dve_column(dve, step, "s2", PS[7][:, 0:4], C2, D, RMS_EPS)
            x = SC[:, 96:100]
            step(nc.vector.tensor_tensor(x, C2, C2, ALU.mult))
            step(nc.vector.tensor_tensor(x, x, PS[7][:, 4:8], ALU.mult))
            step(nc.vector.tensor_scalar(x, x, 1.0 / D, RMS_EPS, ALU.mult, ALU.add))
            inverse_root(step, CF, x, scratch(TOK))
            step(nc.vector.tensor_tensor(CF, CF, C2, ALU.mult))
            dve_diag(dve, step, "s2", C2, T[:, 0, :])
            dve_diag(dve, step, "s2b", CF, T[:, 1, :])
            dve.wait_ge(*due("s2_rb", 1))
            for k in range(KD):
                last = nc.vector.scalar_tensor_tensor(out=X[:, k, :], in0=X[:, k, :], scalar=vec("normf", k), in1=RB1, op0=ALU.mult, op1=ALU.mult)
            last.then_inc(S("x2"), 1)
            dve.wait_ge(*due("s2b_rb", 1))

        def act_between(act):
            act_rows(act, "s2", PS[6], RB1)
            act_rows(act, "s2b", PS[5], RB[:, :])
            act.dma_start(MK_RAW[:, :, :], dram["mem"]).then_inc(S("mem_in"), 16)

        PMK = PH["mem_k"]
        MKT = [(place("mem_k_t_a", 144 + 8, [3, MEM]), 3), (place("mem_k_t_b", 155 + 8, [3, MEM]), 3), (place("mem_k_t_c", YAT + 62.0625, [2, MEM]), 2)]
        MKT = [t[:, i, :] for t, n in MKT for i in range(n)]
        MK_RAW = place("mem_key_raw", YAT + 88, [KD, MEM])
        MK_LO = place("mem_key_lo", YAT + 88, [KD, MEM], F32R)
        MK_HI = place("mem_key_hi", 24, [KD, MEM], F32R)
        MSQ, MACC, MDIAG, MROW = T[:, 2, :].rearrange("p (a b) -> p a b", b=MEM), T[:, 3, 0:MEM], T[:, 3, MEM:2 * MEM], T[:, 5, 0:MEM]
        MCOL = SM[:, 8:8 + KM]

        def act_mem_squares(act):
            act.wait_ge(*due("mem_in", 16))
            for k in range(KD):
                if k >= 2:
                    act.wait_ge(*due("m_added", k - 1))
                nc.scalar.activation(MSQ[:, k % 2, :], MK_RAW[:, k, :], ACT.Square).then_inc(S("m_sq"), 1)

        def dve_mem_squares(dve):
            dve.wait_ge(*due("ffn1_yl", KF))
            for k in range(KD):
                dve.wait_ge(*due("m_sq", k + 1))
                if k == 0:
                    nc.vector.tensor_copy(MACC, MSQ[:, 0, :]).then_inc(S("m_added"), 1)
                else:
                    dve.wait_ge(*due("m_added", k))
                    nc.vector.tensor_tensor(MACC, MACC, MSQ[:, k % 2, :], ALU.add).then_inc(S("m_added"), 1)

        def pe_mem_norm(pe, r):
            if r == 0:
                pe_sum(pe, "m", MACC, PS[5], ntok=KM)
            else:
                pe_spread(pe, "m", MDIAG, PS[4], n=MEM)

        def act_mem_norm(act, r):
            if r == 1:
                act_rows(act, "m", PS[4], MROW, n=MEM)
                for k in range(KD):
                    act.wait_ge(*due("m_scaled", k + 1))
                    nc.scalar.activation(MK_HI[:, k, :], MK_RAW[:, k, :], ACT.Copy).then_inc(S("m_hi"), 1)

        def dve_mem_norm(dve, step, r):
            if r == 0:
                dve_column(dve, step, "m", PS[5][:, 0:KM], MCOL, D, RMS_EPS, n=KM)
                dve_diag(dve, step, "m", MCOL, MDIAG, n=KM)
            else:
                dve.wait_ge(*due("m_rb", 1))
                for k in range(KD):
                    nc.vector.scalar_tensor_tensor(out=MK_RAW[:, k, :], in0=MK_RAW[:, k, :], scalar=vec("mem_kv", k), in1=MROW, op0=ALU.mult, op1=ALU.mult).then_inc(S("m_scaled"), 1)
                for k in range(KD):
                    dve.wait_ge(*due("m_hi", k + 1))
                    nc.vector.tensor_tensor(MK_LO[:, k, :], MK_RAW[:, k, :], MK_HI[:, k, :].bitcast(F32), ALU.subtract).then_inc(S("m_lo"), 1)

        def key_bank(k):
            return PS[2 + k % 4][:, 0:MEM]

        def pe_mem_keys(pe):
            def body(r, parity, pair):
                if first(r):
                    pe.wait_ge(*due("m_lo", KD))
                for i in range(2):
                    if not (isinstance(r, int) and r < 2):
                        pe.wait_ge(*due("mk", r * 2 + (i - 3)))
                    feature_tile(pe, PMK, r, (2 * i, 2 * i + 1), key_bank(2 * parity + i), MK_HI, MK_LO)
                if first(r):
                    pe_sum(pe, "f1", ACC, PS[7])
                elif isinstance(r, int) and r == 1:
                    pe_spread(pe, "f1", DIAG, PS[6])
            rounds(pe, PMK, body)

        def act_mem_key(act, k):
            act.wait_ge(units_used, PMK.used(k // 2, 2 * (k % 2) + 1))
            nc.scalar.activation(MKT[k], key_bank(k), ACT.Copy).then_inc(S("mk"), 1)

        def act_mem_keys(act):
            for k in range(4):
                act_mem_key(act, k)
            act_rows(act, "f1", PS[6], RB[:, :])

            def before(k):
                if k == 4:
                    act.wait_ge(units_used, PMK.used(3, 3))
                if k < 4:
                    act_mem_key(act, 4 + k)
            act_join(act, "f1", "s3", "mix_pre", before)

        PFV, PFQ, PSM, PGQ, PGZ, PMO = (PH[n] for n in ("fox_v", "fox_qk", "small", "gdn_qkv", "gdn_z", "mix_out"))
        FQ = place("fox_q", YAT, [4, SEQ])
        FK = place("fox_k", YAT + 8, [4, SEQ])
        FV = place("fox_v_rows", YAT + 16, [TOK, SEQ])
        GQKV = place("gdn_qkv_t", YAT + 24, [12, SEQ])
        GZ = place("gdn_z_t", YAT + 48, [GH, SEQ])
        R_ = place("token_rows", YAT + 56, [SEQ])
        COLS = place("token_cols", YAT + 58, [TOK, P])
        ZAT = YAT + 64.0625
        G_XB = [place("gdn_xb_a", YAT + 60, [SEQ + 8]), place("gdn_xb_b", ZAT + 28.5, [SEQ + 8])]
        FS = place("fox_s", ZAT, [2, SEQ])
        FP = place("fox_p", ZAT + 4, [2, SEQ])
        FPT = place("fox_pt", ZAT + 8, [2, TOK, SEQ])
        MASKS = place("masks", ZAT + 24, [8, P])
        CM, INC = MASKS[:, 0, :], MASKS[:, 1, :]
        LEVELS = (1, 2, 4, 8, 16, 32)
        F_ROWS, B_ROWS, G_ROWS, E_ROWS = 0, 32, 64, 96

        def pool_causal_mask(pool):
            pool.wait_ge(units_used, PH["mem_k"].used(3, 3))
            nc.gpsimd.memset(CM, 0.0).then_inc(S("causal"), 1)
            pool.wait_ge(*due("causal", 1))
            nc.gpsimd.affine_select(out=CM, in_=CM, compare_op=ALU.is_ge, fill=-1e30, base=0, pattern=[[-1, P]], channel_multiplier=1).then_inc(S("causal"), 1)

        def pool_masks(pool):
            n = [0]

            def done(instruction):
                n[0] += 1
                instruction.then_inc(S("masks"), 1)
                pool.wait_ge(*due("masks", n[0]))

            def keep(m, op, pattern, base, cm, fill=0.0):
                done(nc.gpsimd.affine_select(out=m, in_=m, compare_op=op, fill=fill, base=base, pattern=pattern, channel_multiplier=cm))
            for i, b in enumerate(LEVELS):
                m = MASKS[:, 2 + i, :]
                done(nc.gpsimd.memset(m, 1.0))
                v = m.rearrange("p (n c) -> p n c", c=2 * b)
                keep(v, ALU.is_ge, [[-2 * b, P // (2 * b)], [0, 2 * b]], 0, 1)
                keep(v, ALU.is_ge, [[2 * b, P // (2 * b)], [0, 2 * b]], b - 1, -1)
                keep(v, ALU.is_ge, [[0, P // (2 * b)], [1, 2 * b]], -b, 0)
            done(nc.gpsimd.memset(INC, 1.0))
            v = INC.rearrange("p (n c) -> p n c", c=CH)
            keep(v, ALU.is_ge, [[-CH, P // CH], [0, CH]], 0, 1)
            keep(v, ALU.is_ge, [[CH, P // CH], [0, CH]], CH - 1, -1)
            keep(INC, ALU.is_ge, [[1, P]], 0, -1)

        N_MASKS = 4 * len(LEVELS) + 4

        def pe_mix_in(pe):
            def fox_v(r, parity, pair):
                if first(r):
                    pe.wait_ge(*due("f1_sq", KD))
                    pe.wait_ge(*due("mk", KD))
                token_tiles(pe, PFV, r, parity, PS[0:4], XH, XL, lambda k: pe.wait_ge(*due("s3_lo", k + 1)))
                if first(r):
                    pe_sum(pe, "s3", ACC, PS[7])
                else:
                    pe_spread(pe, "s3", DIAG, PS[6])
            rounds(pe, PFV, fox_v)

            for r in range(2):
                for j in range(4):
                    k = 4 * r + j
                    pe.wait_ge(units_ready, PSM.used(r, j))
                    wh, wl = WH[:, SLOT[j], :], WL[:, SLOT[j], :]
                    nc.tensor.matmul(PS[4], wh, XH[:, k, :], start=k == 0, stop=False)
                    nc.tensor.matmul(PS[4], wl, XH[:, k, :], start=False, stop=False)
                    nc.tensor.matmul(PS[4], wh, XL[:, k, :], start=False, stop=k == KD - 1).then_inc(units_used, 1)

            def fox_qk(r, parity, pair):
                if first(r):
                    pe.wait_ge(*due("fv", TOK))
                for i, read in enumerate(("fq", "fk")):
                    bank_free(pe, read, r)
                    feature_tile(pe, PFQ, r, (2 * i, 2 * i + 1), PS[2 * parity + i], XH, XL)
            rounds(pe, PFQ, fox_qk)

        NCONV, NTILES = 3 * GH, 4 * GH

        def mix_tile(t):
            r, i = divmod(t, 2)
            return (PGQ, r, i) if t < NCONV else (PGZ, r - NCONV // 2, i)

        def pe_mix_half(pe, t, half):
            ph, r, i = mix_tile(t)
            if half == 0 and t == 0:
                pe.wait_ge(*due("cols", 1))
            if half == 0 and t >= 2:
                if t - 1 <= NCONV:
                    pe.wait_ge(*due("g_xb", t - 1))
                else:
                    pe.wait_ge(*due("g_z", t - 1 - NCONV))
            j = 2 * i + half
            pe.wait_ge(units_ready, ph.used(r, j))
            for q in range(4):
                k = 4 * half + q
                wh, wl, ps = WH[:, SLOT[j] + q, :], WL[:, SLOT[j] + q, :], PS[5 + t % 2]
                nc.tensor.matmul(ps, wh, XH[:, k, :], start=k == 0, stop=False)
                nc.tensor.matmul(ps, wl, XH[:, k, :], start=False, stop=False)
                last = nc.tensor.matmul(ps, wh, XL[:, k, :], start=False, stop=k == KD - 1)
            last.then_inc(units_used, 1)

        def dve_mix_read(dve, t):
            ph, r, i = mix_tile(t)
            dve.wait_ge(units_used, ph.used(r, 2 * i + 1))
            if t < NCONV:
                if t >= 2:
                    dve.wait_ge(*due("g_conv", t - 1))
                nc.vector.tensor_tensor(G_XB[t % 2][:, 8:8 + SEQ], PS[5 + t % 2], RB[:, :], ALU.mult).then_inc(S("g_xb"), 1)
            else:
                if t >= NCONV + 2:
                    dve.wait_ge(*due("g_zs", t - NCONV - 1))
                nc.vector.tensor_tensor(T[:, 4 + t % 2, :], PS[5 + t % 2], RB[:, :], ALU.mult).then_inc(S("g_z"), 1)

        def dve_mix_taps(dve, t):
            dve.wait_ge(*due("g_c0", t + 1))
            acc = T[:, 2 + t % 2, :]
            for tap in range(3):
                conv = nc.vector.scalar_tensor_tensor(out=acc, in0=G_XB[t % 2][:, 5 + tap:5 + tap + SEQ], scalar=vec("gconv", NCONV * tap + t), in1=acc, op0=ALU.mult, op1=ALU.add)
                if tap < 2:
                    conv.then_inc(S("g_taps"), 1)
                    dve.wait_ge(*due("g_taps", 2 * t + tap + 1))
            conv.then_inc(S("g_conv"), 1)

        def act_mix_start(act, t):
            act.wait_ge(*due("g_xb", t + 1))
            nc.scalar.activation(T[:, 2 + t % 2, :], G_XB[t % 2][:, 8:8 + SEQ], ACT.Copy, scale=vec("gconv", 3 * NCONV + t)).then_inc(S("g_c0"), 1)

        def act_mix_end(act, t):
            if t < NCONV:
                act.wait_ge(*due("g_conv", t + 1))
                nc.scalar.activation(GQKV[:, t, :], T[:, 2 + t % 2, :], ACT.Silu).then_inc(S("g_qkv"), 1)
            else:
                act.wait_ge(*due("g_z", t - NCONV + 1))
                nc.scalar.activation(GZ[:, t - NCONV, :], T[:, 4 + t % 2, :], ACT.Silu).then_inc(S("g_zs"), 1)

        def act_mix_in(act):
            act.wait_ge(*due("s3_diag", 1))
            act.wait_ge(units_used, PFV.used(1, 3))
            for i in range(TOK):
                nc.scalar.activation(FV[:, i, :], PS[i], ACT.Copy, scale=COL[:, i:i + 1]).then_inc(S("fv"), 1)
            act_rows(act, "s3", PS[6], RB[:, :])
            act.wait_ge(*due("rows_x", 1))
            nc.scalar.activation(T[B_ROWS:B_ROWS + GH, 3, :], T[B_ROWS:B_ROWS + GH, 2, :], ACT.Tanh, scale=0.5).then_inc(S("beta_tanh"), 1)
            nc.scalar.activation(SM[64:68, 21:22], V_[64:68, VEC["a_log"]:VEC["a_log"] + 1], ACT.Exp).then_inc(S("a_exp"), 1)
            act_exp_neg(act, "rows", T[:, 4, :])

            act.wait_ge(*due("cols_t", 1))
            nc.scalar.activation(COLS[:, :, 0:100], PS[5].rearrange("p (t c) -> p t c", t=TOK)[:, :, 0:100], ACT.Copy).then_inc(S("cols"), 1)

        def pe_cols(pe):
            pe.wait_ge(*due("rows", 1))
            for i in range(TOK):
                last = nc.tensor.transpose(PS[5][:, i * P:i * P + 100], R_[0:100, i * P:(i + 1) * P], IDENT[0:100, 0:100])
            last.then_inc(S("cols_t"), 1)

        def dve_mix_in(dve, step):
            dve_column(dve, step, "s3", PS[7][:, 0:4], COL, D, RMS_EPS)
            dve_diag(dve, step, "s3", COL, DIAG)
            dve.wait_ge(*due("s3_rb", 1))

            X_, LP, E_, S2_ = T[:, 2, :], T[:, 6, :], T[:, 4, :], T[:, 5, :]
            dve.wait_ge(units_used, PSM.used(1, 3))
            step(nc.vector.tensor_tensor(X_, PS[4], RB[:, :], ALU.mult))
            nc.vector.tensor_scalar(X_, X_, vec("small_bias"), None, ALU.add).then_inc(S("rows_x"), 1)
            dve.wait_ge(*due("rows_x", 1))
            step(nc.vector.memset(R_[:, :], 0.0))
            for pad in G_XB:
                step(nc.vector.memset(pad[:, 0:8], 0.0))
            log1p_exp_neg_abs(dve, step, "rows", LP, X_, E_, S2_)
            f, b, g, e = (slice(n, n + 8 if n == 0 else n + GH) for n in (F_ROWS, B_ROWS, G_ROWS, E_ROWS))
            step(nc.vector.scalar_tensor_tensor(out=E_[f, :], in0=X_[f, :], scalar=0.0, in1=LP[f, :], op0=ALU.min, op1=ALU.subtract))
            step(nc.vector.tensor_tensor_scan(R_[f, :], ONES[f, 0:1].to_broadcast([8, SEQ]), E_[f, :], 0.0, ALU.mult, ALU.add))
            dve.wait_ge(*due("beta_tanh", 1))
            step(nc.vector.tensor_scalar(R_[b, :], T[b, 3, :], 0.5, 0.5, ALU.mult, ALU.add))
            dve.wait_ge(*due("a_exp", 1))
            step(nc.vector.scalar_tensor_tensor(out=E_[g, :], in0=X_[g, :], scalar=0.0, in1=LP[g, :], op0=ALU.max, op1=ALU.add))
            step(nc.vector.tensor_scalar(E_[g, :], E_[g, :], SM[g, 21:22], -1.0, ALU.mult, ALU.mult))
            step(nc.vector.memset(S2_[g, :], 1.0))
            step(nc.vector.memset(S2_[g, :].rearrange("p (n c) -> p n c", c=CH)[:, :, 0:1], 0.0))
            step(nc.vector.tensor_tensor_scan(R_[g, :], S2_[g, :], E_[g, :], 0.0, ALU.mult, ALU.add))
            chunks = R_[g, :].rearrange("p (n c) -> p n c", c=CH)
            nc.vector.tensor_tensor(R_[e, :].rearrange("p (n c) -> p n c", c=CH), chunks[:, :, CH - 1:CH].to_broadcast([GH, SEQ // CH, CH]), chunks, ALU.subtract).then_inc(S("rows"), 1)

            def fox_qk(r, parity, pair):
                dve.wait_ge(units_used, PFQ.used(r, 1))
                nc.vector.scalar_tensor_tensor(out=FQ[:, r, :], in0=PS[2 * parity], scalar=FOXD ** -0.5, in1=RB[:, :], op0=ALU.mult, op1=ALU.mult).then_inc(S("fq"), 1)
                dve.wait_ge(units_used, PFQ.used(r, 3))
                nc.vector.tensor_tensor(FK[:, r, :], PS[2 * parity + 1], RB[:, :], ALU.mult).then_inc(S("fk"), 1)
            rounds(dve, PFQ, fox_qk)
        STEPS = FOXH * TOK

        def row_of(pe, at, n, i, ps):
            sel = IDENT[at:at + n, at + i:at + i + 1].to_broadcast([n, P])
            return nc.tensor.matmul(ps, sel, R_[at:at + n, :], start=True, stop=True)

        def pe_fox(pe):
            pe.wait_ge(*due("fk", PFQ.rounds))
            for i in range(STEPS + 5):
                h, qt = divmod(i, TOK)
                if i < STEPS:
                    if qt == 0:
                        if h >= 1:
                            pe.wait_ge(*due("fx_rowc", h))
                        row_of(pe, F_ROWS, 8, h, PS[7]).then_inc(S("fx_row"), 1)
                    n, rows = (qt + 1) * P, slice(64 * (h % 2), 64 * (h % 2) + 64)
                    if i >= 2:
                        pe.wait_ge(*due("fx_sv", i - 1))
                    nc.tensor.matmul(PS[i % 2][:, 0:n], FQ[rows, h // 2, qt * P:(qt + 1) * P], FK[rows, h // 2, 0:n], start=True, stop=True).then_inc(S("fx_s"), 1)
                j = i - 2
                if 0 <= j < STEPS:
                    pe.wait_ge(*due("fx_p", j + 1))
                    if j >= 2:
                        pe.wait_ge(*due("fx_pt", j - 1))
                    for kt in range(j % TOK + 1):
                        last = nc.tensor.transpose(PS[2 + j % 2][:, kt * P:(kt + 1) * P], FP[:, j % 2, kt * P:(kt + 1) * P], IDENT[:, :])
                    last.then_inc(S("fx_t"), 1)
                if i >= 8 and qt == 0:
                    fox_out(pe, h - 2)
                if i < 2 * NTILES:
                    pe_mix_half(pe, *divmod(i, 2))

        def fox_out(pe, h):
            pe.wait_ge(*due("fx_pt", TOK * (h + 1)))
            if h >= 2 and h % 2 == 0:
                pe.wait_ge(*due("fx_oc", h // 2))
            half = slice(64 * (h % 2), 64 * (h % 2) + 64)
            for kt in range(TOK):
                last = nc.tensor.matmul(PS[4][half, kt * P:SEQ], FV[:, kt, h * FOXD:(h + 1) * FOXD], FPT[:, h % 2, kt, kt * P:SEQ],
                                        start=kt == 0, stop=kt == TOK - 1)
            last.then_inc(S("fx_o"), 1)

        def dve_fox(dve, step):
            MXC, SUMC = SC[:, 0:32], SC[:, 32:64]
            dve.wait_ge(*due("causal", 2))
            dve.wait_ge(*due("cols", 1))
            for i in range(STEPS + 1):
                h, qt = divmod(i, TOK)
                if i < STEPS:
                    n = (qt + 1) * P
                    s = FS[:, i % 2, :]
                    dve.wait_ge(*due("fx_rowc", h + 1))
                    dve.wait_ge(*due("fx_s", i + 1))
                    if i >= 2:
                        dve.wait_ge(*due("fx_e", i - 1))
                    nc.vector.scalar_tensor_tensor(out=s[:, 0:n], in0=PS[i % 2][:, 0:n], scalar=COLS[:, qt, F_ROWS + h:F_ROWS + h + 1], in1=T[:, h % 2, 0:n], op0=ALU.add, op1=ALU.subtract).then_inc(S("fx_sv"), 1)
                    dve.wait_ge(*due("fx_sv", i + 1))
                    step(nc.vector.tensor_tensor(s[:, n - P:n], s[:, n - P:n], CM, ALU.add))
                    step(nc.vector.reduce_max(MXC[:, i:i + 1], s[:, 0:n], axis=AX.X))
                    nc.vector.tensor_scalar(MXC[:, i:i + 1], MXC[:, i:i + 1], -1.0, None, ALU.mult).then_inc(S("fx_nm"), 1)
                if i >= 1:
                    j = i - 1
                    n = (j % TOK + 1) * P
                    dve.wait_ge(*due("fx_e", j + 1))
                    step(nc.vector.reciprocal(SUMC[:, j:j + 1], SUMC[:, j:j + 1]))
                    nc.vector.tensor_scalar(FP[:, j % 2, 0:n], FP[:, j % 2, 0:n], SUMC[:, j:j + 1], None, ALU.mult).then_inc(S("fx_p"), 1)
                t = i // 2
                if i % 2 and t < NTILES:
                    dve_mix_read(dve, t)
                elif i % 2 == 0 and 1 <= t <= NCONV:
                    dve_mix_taps(dve, t - 1)

        def pool_fox_lo(pool):
            for m in range(FOXH // 2):
                pool.wait_ge(*due("fx_hi", m + 1))
                nc.gpsimd.tensor_tensor(XL[:, m, :], FQ[:, m, :], XH[:, m, :].bitcast(F32), ALU.subtract).then_inc(S("fx_lo"), 1)

        def act_fox(act):
            MXC, SUMC = SC[:, 0:32], SC[:, 32:64]
            for i in range(STEPS + 3):
                h, qt = divmod(i, TOK)
                if i < STEPS:
                    if qt == 0:
                        act.wait_ge(*due("fx_row", h + 1))
                        if h >= 2:
                            act.wait_ge(*due("fx_sv", TOK * (h - 1)))
                        nc.scalar.activation(T[:, h % 2, :], PS[7], ACT.Copy).then_inc(S("fx_rowc"), 1)
                    n = (qt + 1) * P
                    act.wait_ge(*due("fx_nm", i + 1))
                    if i >= 2:
                        act.wait_ge(*due("fx_t", i - 1))
                    nc.scalar.activation(FP[:, i % 2, 0:n], FS[:, i % 2, 0:n], ACT.Exp, bias=MXC[:, i:i + 1], accum_out=SUMC[:, i:i + 1]).then_inc(S("fx_e"), 1)
                t = i // 2 - 1
                if i % 2 == 0 and 0 <= t < NCONV:
                    act_mix_start(act, t)
                elif i % 2 and 0 <= t < NTILES:
                    act_mix_end(act, t)
                j = i - 3
                if 0 <= j < STEPS:
                    jh, jq = divmod(j, TOK)
                    act.wait_ge(*due("fx_t", j + 1))
                    if jh >= 2 and jq == 0:
                        act.wait_ge(*due("fx_o", jh - 1))
                    nc.scalar.activation(FPT[:, jh % 2, 0:jq + 1, jq * P:(jq + 1) * P], PS[2 + j % 2][:, 0:(jq + 1) * P].rearrange("p (k q) -> p k q", q=P), ACT.Copy).then_inc(S("fx_pt"), 1)
                if i >= 8 and qt == 3 and h % 2 == 1 and i < STEPS:
                    act_fox_out(act, (h - 3) // 2)
            act_fox_out(act, FOXH // 2 - 1)

        def act_fox_out(act, m):
            act.wait_ge(*due("fx_o", 2 * m + 2))
            nc.scalar.activation(FQ[:, m, :], PS[4], ACT.Copy).then_inc(S("fx_oc"), 1)

        def act_fox_hi(act):
            act.wait_ge(units_used, PGZ.used(1, 3))
            act.wait_ge(*due("fx_oc", FOXH // 2))
            for m in range(FOXH // 2):
                nc.scalar.activation(XH[:, m, :], FQ[:, m, :], ACT.Copy).then_inc(S("fx_hi"), 1)

        GS = place("gdn_inv_t", YAT, [TOK, SEQ])
        GT = place("gdn_inv", YAT + 8, [TOK, SEQ])
        GLT = place("gdn_l_t", YAT + 16, [TOK, SEQ])
        GU_ = place("gdn_u", YAT + 8, [TOK, SEQ])
        GWN = place("gdn_w_t_neg", YAT + 16, [TOK, SEQ])
        GST = place("gdn_state", YAT + 32, [2, SEQ])
        GVN = place("gdn_v_new", YAT + 36, [2, SEQ])
        GAT = place("gdn_attn_t", YAT + 40, [TOK, SEQ])
        GR = place("gdn_g_rows", ZAT, [GH, SEQ])
        GC = place("gdn_level", ZAT, [TOK, SEQ])
        GO = place("gdn_o_t", ZAT, [GH, SEQ])
        EG = place("gdn_exp_g", ZAT + 8, [GH, SEQ])
        GKB = place("gdn_k_beta", ZAT + 16, [GH, SEQ])
        GKT = place("gdn_k_tail", ZAT + 16, [TOK, SEQ])
        GVB = place("gdn_v_beta", 40, [TOK, SEQ])
        GKE = place("gdn_k_beta_eg", 24, [TOK, SEQ])
        NC = SM[:, 32:64]
        CE = COLS[:, :, 104:124].rearrange("p t (a h) -> p t a h", h=GH)
        heads = lambda ap: ap.rearrange("p (h c) -> p h c", h=GH)
        across = lambda col: col.unsqueeze(2).to_broadcast([P, GH, P])
        every = lambda mask: mask.unsqueeze(1).to_broadcast([P, GH, P])
        tile_of = lambda p: slice(p * P, (p + 1) * P)

        def pe_norms(pe, name, src_ready, count, n_cols):
            for j in range(count):
                pe.wait_ge(*due(src_ready, j + 1))
                for i in range(TOK):
                    last = nc.tensor.matmul(PS[7][:, 4 * j + i:4 * j + i + 1], T[:, j % 2, tile_of(i)], ONES[:, 0:1], start=True, stop=True)
                last.then_inc(S(f"{name}_sums"), 1)

        def pe_spreads(pe, name, count):
            for j in range(count):
                pe.wait_ge(*due(f"{name}_diags", j + 1))
                if j >= 2:
                    pe.wait_ge(*due(f"{name}_scaled", j - 1))
                nc.tensor.matmul(PS[4 + j % 2], ONES[:, :], T[:, 2 + j % 2, :], start=True, stop=True).then_inc(S(f"{name}_spread"), 1)

        def act_squares(act, name, tiles):
            for j, tile in enumerate(tiles):
                if j >= 2:
                    act.wait_ge(*due(f"{name}_sums", j - 1))
                nc.scalar.activation(T[:, j % 2, :], tile, ACT.Square).then_inc(S(f"{name}_sq"), 1)

        def dve_diags(dve, name, cols, j):
            if j >= 2:
                dve.wait_ge(*due(f"{name}_spread", j - 1))
            nc.vector.tensor_tensor(
                heads(T[:, 2 + j % 2, :]), every(IDENT[:, :]),
                cols[:, 4 * j:4 * j + 4].unsqueeze(2).to_broadcast([P, TOK, P]), ALU.mult).then_inc(S(f"{name}_diags"), 1)

        def pe_gdn_products(pe):
            pe.wait_ge(*due("fx_e", STEPS))
            pe_norms(pe, "gl", "gl_sq", 8, 32)
            for h in range(GH):
                if h >= 2:
                    pe.wait_ge(*due("g_er", h - 1))
                elif h == 0:
                    pe.wait_ge(*due("fx_oc", FOXH // 2))
                row_of(pe, G_ROWS, GH, h, PS[h % 2]).then_inc(S("g_row"), 1)
            pe_spreads(pe, "gl", 8)
            for h in range(GH):
                if h >= 2:
                    pe.wait_ge(*due("g_kb", h - 1))
                row_of(pe, B_ROWS, GH, h, PS[2 + h % 2]).then_inc(S("g_brow"), 1)
            for p in range(TOK):
                if p < 2:
                    pe.wait_ge(*due("gl_scaled", 8))
                else:
                    pe.wait_ge(*due("g_vb", p - 1))
                for h in range(GH):
                    last = nc.tensor.transpose(PS[4 + p % 2][:, h * P:(h + 1) * P], GQKV[:, 8 + h, tile_of(p)], IDENT[:, :])
                last.then_inc(S("g_vt"), 1)
            pe.wait_ge(*due("g_er", GH))
            pe.wait_ge(*due("g_kb", GH))
            for p in range(TOK):
                if p >= 2:
                    pe.wait_ge(*due("g_lt1", p - 1))
                for h in range(GH):
                    last = nc.tensor.matmul(PS[p % 2][:, h * P:(h + 1) * P], GQKV[:, 4 + h, tile_of(p)], GKB[:, h, tile_of(p)], start=True, stop=True)
                last.then_inc(S("g_kk"), 1)
                if p >= 2:
                    pe.wait_ge(*due("g_at", p - 1))
                for h in range(GH):
                    last = nc.tensor.matmul(PS[2 + p % 2][:, h * P:(h + 1) * P], GQKV[:, 4 + h, tile_of(p)], GQKV[:, h, tile_of(p)], start=True, stop=True)
                last.then_inc(S("g_qk"), 1)

        def pe_turn_k(pe, p):
            if p >= 2:
                pe.wait_ge(*due("g_kt", p - 1))
            for h in range(GH):
                last = nc.tensor.transpose(PS[6 + p % 2][:, h * P:(h + 1) * P], GQKV[:, 4 + h, tile_of(p)], IDENT[:, :])
            last.then_inc(S("g_ktt"), 1)

        def dve_turned_k(dve, p):
            dve.wait_ge(*due("g_ktt", p + 1))
            nc.vector.tensor_tensor(heads(GKE[:, p, :]), heads(PS[6 + p % 2]), across(CE[:, p, 1, :]), ALU.mult).then_inc(S("g_ke"), 1)
            nc.vector.tensor_tensor(heads(GKT[:, p, :]), heads(PS[6 + p % 2]), across(CE[:, p, 2, :]), ALU.mult).then_inc(S("g_kt"), 1)

        def act_gdn_products(act):
            act.wait_ge(*due("g_qkv", NCONV))
            act_squares(act, "gl", [GQKV[:, j, :] for j in range(8)])
            nc.scalar.activation(CE[:, :, 0, :], COLS[:, :, G_ROWS:G_ROWS + GH], ACT.Exp).then_inc(S("g_ce"), 1)
            nc.scalar.activation(CE[:, :, 2, :], COLS[:, :, E_ROWS:E_ROWS + GH], ACT.Exp).then_inc(S("g_ce"), 1)
            for h in range(GH):
                act.wait_ge(*due("g_row", h + 1))
                nc.scalar.activation(GR[:, h, :], PS[h % 2], ACT.Copy).then_inc(S("g_gr"), 1)
                nc.scalar.activation(EG[:, h, :], PS[h % 2], ACT.Exp).then_inc(S("g_er"), 1)
            act_fox_hi(act)
            for p in range(TOK):
                act.wait_ge(*due("g_dec", p + 1))
                if p >= 2:
                    act.wait_ge(*due("g_lt1", p - 1))
                    act.wait_ge(*due("g_at", p - 1))
                nc.scalar.activation(T[:, DEXP[p % 2], :], T[:, DEC[p % 2], :], ACT.Exp).then_inc(S("g_dexp"), 1)

        DEC, DEXP = (0, 4), (1, 5)

        def dve_gdn_products(dve, step):
            def decay_exponent(p):
                for h in range(GH):
                    last = nc.vector.tensor_scalar(T[:, DEC[p % 2], h * P:(h + 1) * P], GR[:, h, tile_of(p)], COLS[:, p, G_ROWS + h:G_ROWS + h + 1], 0.0, ALU.subtract, ALU.min)
                last.then_inc(S("g_dec"), 1)
            x = SC[:, 96:128]
            dve.wait_ge(*due("gl_sums", 8))
            step(nc.vector.tensor_scalar(x, PS[7][:, 0:32], RMS_EPS, None, ALU.add))
            inverse_root(step, NC, x, scratch(32))
            step(nc.vector.tensor_scalar(NC[:, 0:16], NC[:, 0:16], GD ** -0.5, None, ALU.mult))
            dve_diags(dve, "gl", NC, 0)
            for j in range(8):
                if j < 7:
                    dve_diags(dve, "gl", NC, j + 1)
                dve.wait_ge(*due("gl_spread", j + 1))
                nc.vector.tensor_tensor(GQKV[:, j, :], GQKV[:, j, :], PS[4 + j % 2], ALU.mult).then_inc(S("gl_scaled"), 1)
            dve.wait_ge(*due("gl_scaled", 8))
            dve.wait_ge(*due("g_ce", 2))
            step(nc.vector.tensor_tensor(CE[:, :, 1, :], CE[:, :, 0, :], COLS[:, :, B_ROWS:B_ROWS + GH], ALU.mult))
            dve.wait_ge(*due("g_er", GH))
            decay_exponent(0)
            for h in range(GH):
                dve.wait_ge(*due("g_brow", h + 1))
                nc.vector.tensor_tensor(GKB[:, h, :], GQKV[:, 4 + h, :], PS[2 + h % 2], ALU.mult).then_inc(S("g_kb"), 1)
            decay_exponent(1)
            for p in range(TOK):
                dve.wait_ge(*due("g_vt", p + 1))
                nc.vector.tensor_tensor(heads(GVB[:, p, :]), heads(PS[4 + p % 2]), across(COLS[:, p, B_ROWS:B_ROWS + GH]), ALU.mult).then_inc(S("g_vb"), 1)
            dve.wait_ge(*due("masks", N_MASKS))
            for p in range(TOK):
                decay = T[:, DEXP[p % 2], :]
                dve.wait_ge(*due("g_dexp", p + 1))
                step(nc.vector.tensor_tensor(heads(decay), heads(decay), every(INC), ALU.mult))
                dve.wait_ge(*due("g_kk", p + 1))
                nc.vector.tensor_tensor(GLT[:, p, :], PS[p % 2], decay, ALU.mult).then_inc(S("g_lt1"), 1)
                dve.wait_ge(*due("g_qk", p + 1))
                nc.vector.tensor_tensor(GAT[:, p, :], PS[2 + p % 2], decay, ALU.mult).then_inc(S("g_at"), 1)
                if p + 2 < TOK:
                    decay_exponent(p + 2)
            dve.wait_ge(*due("fx_lo", FOXH // 2))

        def pool_levels(pool):
            for n, b in enumerate(LEVELS):
                for p in range(TOK):
                    if n == 0:
                        pool.wait_ge(*due("g_lt1", p + 1))
                        if p == 0:
                            pool.wait_ge(*due("g_dec", TOK))
                    else:
                        pool.wait_ge(*due("g_u", (n - 1) * TOK + p + 1))
                        if n == 1:
                            pool.wait_ge(*due("g_s", p + 1))
                    nc.gpsimd.tensor_tensor(heads(GC[:, p, :]), heads(GLT[:, p, :]), every(MASKS[:, 2 + n, :]), ALU.mult).then_inc(S("g_c"), 1)
                if n == 1:
                    for h in range(GH):
                        pool.wait_ge(*due("g_qk", TOK))
                        nc.gpsimd.tensor_tensor(GQKV[:, h, :], GQKV[:, h, :], EG[:, h, :], ALU.mult).then_inc(S("g_qe"), 1)

        def pe_levels(pe):
            for n, b in enumerate(LEVELS):
                for p in range(TOK):
                    m = n * TOK + p
                    pe.wait_ge(*due("g_c", m + 1))
                    if m >= TOK + 2:
                        pe.wait_ge(*due("g_uc", m - TOK - 1))
                    elif m >= 2:
                        pe.wait_ge(*due("g_t", m - 1))
                    else:
                        pe.wait_ge(*due("g_at", TOK))
                    if n:
                        pe.wait_ge(*due("g_t", (n - 1) * TOK + p + 1))
                    for h in range(GH):
                        c, o = GC[:, p, h * P:(h + 1) * P], PS[m % 2][:, h * P:(h + 1) * P]
                        if n == 0:
                            last = nc.tensor.transpose(o, c, IDENT[:, :])
                        else:
                            last = nc.tensor.matmul(o, c, GT[:, p, h * P:(h + 1) * P], start=True, stop=True)
                    last.then_inc(S("g_u"), 1)
                if n == 0:
                    continue
                for p in range(TOK):
                    m = n * TOK + p
                    pe.wait_ge(*due("g_uc", m - TOK + 1))
                    if m - TOK == 0:
                        pe.wait_ge(*due("g_vb", TOK))
                    if b < LEVELS[-1]:
                        if m - TOK >= 2:
                            pe.wait_ge(*due("g_t", m - 1))
                        for h in range(GH):
                            hh = slice(h * P, (h + 1) * P)
                            nc.tensor.matmul(PS[2 + p % 2][:, hh], GS[:, p, hh], T[:, p, hh], start=True, stop=True)
                    if m - TOK >= 2:
                        pe.wait_ge(*due("g_s", m - 1))
                    for h in range(GH):
                        hh = slice(h * P, (h + 1) * P)
                        last = nc.tensor.matmul(PS[4 + p % 2][:, hh], T[:, p, hh], GS[:, p, hh], start=True, stop=True)
                    last.then_inc(S("g_us"), 1)
                    if n == 1:
                        pe_turn_k(pe, p)

        def act_levels(act):
            for m in range(TOK, TOK * len(LEVELS)):
                act.wait_ge(*due("g_u", m + 1))
                if m >= 2 * TOK:
                    act.wait_ge(*due("g_us", m - 2 * TOK + 1))
                nc.scalar.activation(T[:, m % TOK, :], PS[m % 2], ACT.Copy).then_inc(S("g_uc"), 1)

        def dve_levels(dve, step):
            for n in range(len(LEVELS)):
                for p in range(TOK):
                    m = n * TOK + p
                    if n == 0:
                        dve.wait_ge(*due("g_u", m + 1))
                        nc.vector.scalar_tensor_tensor(out=heads(GT[:, p, :]), in0=heads(PS[m % 2]), scalar=-1.0, in1=every(IDENT[:, :]), op0=ALU.mult, op1=ALU.add).then_inc(S("g_t"), 1)
                        nc.vector.scalar_tensor_tensor(out=heads(GS[:, p, :]), in0=heads(GC[:, p, :]), scalar=-1.0, in1=every(IDENT[:, :]), op0=ALU.mult, op1=ALU.add).then_inc(S("g_s"), 1)
                    else:
                        dve.wait_ge(*due("g_us", m - TOK + 1))
                        dve.wait_ge(*due("g_t", m - TOK + 1))
                        dve.wait_ge(*due("g_s", m - TOK + 1))
                        if n < len(LEVELS) - 1:
                            nc.vector.tensor_tensor(GT[:, p, :], GT[:, p, :], PS[2 + p % 2], ALU.subtract).then_inc(S("g_t"), 1)
                        nc.vector.tensor_tensor(GS[:, p, :], GS[:, p, :], PS[4 + p % 2], ALU.subtract).then_inc(S("g_s"), 1)
                        if n == 1:
                            dve_turned_k(dve, p)

        NL = TOK * len(LEVELS)
        NCHUNK = SEQ // CH

        def pe_chunks(pe):
            for p in range(TOK):
                if p == 0:
                    pe.wait_ge(*due("g_s", NL))
                    pe.wait_ge(*due("g_ke", TOK))
                    pe.wait_ge(*due("g_uc", NL - TOK))
                if p >= 2:
                    pe.wait_ge(*due("g_wn", p - 1))
                for h in range(GH):
                    hh = slice(h * P, (h + 1) * P)
                    last = nc.tensor.matmul(PS[p % 2][:, hh], GKE[:, p, hh], GS[:, p, hh], start=True, stop=True)
                last.then_inc(S("g_w"), 1)
                if p >= 2:
                    pe.wait_ge(*due("g_uu", p - 1))
                for h in range(GH):
                    hh = slice(h * P, (h + 1) * P)
                    last = nc.tensor.matmul(PS[2 + p % 2][:, hh], GS[:, p, hh], GVB[:, p, hh], start=True, stop=True)
                last.then_inc(S("g_uraw"), 1)
            for i in range(NCHUNK):
                p, half = i // 2, slice(CH * (i % 2), CH * (i % 2) + CH)
                pe.wait_ge(*due("c_st", i + 1))
                if i == 0:
                    pe.wait_ge(*due("g_wn", TOK))
                    pe.wait_ge(*due("g_uu", TOK))
                    pe.wait_ge(*due("g_qe", GH))
                for h in range(GH):
                    last = nc.tensor.matmul(PS[i % 2][half, h * P:(h + 1) * P], GWN[:, p, h * P + CH * (i % 2):h * P + CH * (i % 2) + CH], GST[:, i % 2, h * P:(h + 1) * P], start=True, stop=True)
                last.then_inc(S("c_ws"), 1)
                if i % 2 == 0 and p >= 2:
                    pe.wait_ge(*due("c_oc", p - 1))
                for h in range(GH):
                    at = h * P + CH * (i % 2)
                    nc.tensor.matmul(PS[2 + p % 2][:, at:at + CH], GST[:, i % 2, h * P:(h + 1) * P], GQKV[:, h, i * CH:(i + 1) * CH], start=i % 2 == 0 and h == 0, stop=False)
                pe.wait_ge(*due("c_vn", i + 1))
                for h in range(GH):
                    hh = slice(h * P, (h + 1) * P)
                    last = nc.tensor.matmul(PS[4 + i % 2][:, hh], GKT[half, p, hh], GVN[half, p % 2, hh], start=True, stop=True)
                last.then_inc(S("c_kv"), 1)
                if i and i % 2 == 0:
                    pe_go_sums(pe, i // 2 - 1)
                if i % 2:
                    for h in range(GH):
                        hh = slice(h * P, (h + 1) * P)
                        last = nc.tensor.matmul(PS[2 + p % 2][:, hh], GVN[:, p % 2, hh], GAT[:, p, hh], start=False, stop=h == GH - 1)
                    last.then_inc(S("c_o"), 1)
            pe_go_sums(pe, TOK - 1)
            pe_spreads(pe, "go", GH)

        def pe_go_sums(pe, p):
            pe.wait_ge(*due("go_sq", p + 1))
            for h in range(GH):
                last = nc.tensor.matmul(PS[7][:, 4 * h + p:4 * h + p + 1], T[:, p % 2, tile_of(h)], ONES[:, 0:1], start=True, stop=True)
            last.then_inc(S("go_sums"), 1)

        def pool_gates(pool):
            for p in range(TOK):
                pool.wait_ge(*due("go_sq", p + 1))
                nc.gpsimd.tensor_tensor(GO[:, :, tile_of(p)], GO[:, :, tile_of(p)], GZ[:, :, tile_of(p)], ALU.mult).then_inc(S("go_gated"), 1)

        def act_chunks(act):
            for p in range(TOK):
                act.wait_ge(*due("g_w", p + 1))
                nc.scalar.activation(GWN[:, p, :], PS[p % 2], ACT.Copy, scale=-1.0).then_inc(S("g_wn"), 1)
                act.wait_ge(*due("g_uraw", p + 1))
                nc.scalar.activation(GU_[:, p, :], PS[2 + p % 2], ACT.Copy).then_inc(S("g_uu"), 1)
            for p in range(TOK):
                act.wait_ge(*due("c_o", p + 1))
                nc.scalar.activation(GO[:, :, tile_of(p)], heads(PS[2 + p % 2]), ACT.Copy).then_inc(S("c_oc"), 1)
                act.wait_ge(*due("c_oc", p + 1))
                if p >= 2:
                    act.wait_ge(*due("go_sums", p - 1))
                nc.scalar.activation(heads(T[:, p % 2, :]), GO[:, :, tile_of(p)], ACT.Square).then_inc(S("go_sq"), 1)
            for h in range(GH):
                act.wait_ge(*due("go_scaled", h + 1))
                nc.scalar.activation(XH[:, 4 + h, :], T[:, 4 + h % 2, :], ACT.Copy).then_inc(S("mx_hi"), 1)

        def dve_chunks(dve, step):
            dve.wait_ge(*due("g_kk", TOK))
            dve.wait_ge(*due("g_ktt", TOK))
            nc.vector.memset(GST[:, 0, :], 0.0).then_inc(S("c_st"), 1)
            dve.wait_ge(*due("g_uu", TOK))
            for i in range(NCHUNK):
                p, half, nxt = i // 2, slice(CH * (i % 2), CH * (i % 2) + CH), (i + 1) % 2
                dve.wait_ge(*due("c_st", i + 1))
                end = EG[:, :, i * CH + CH - 1:i * CH + CH].to_broadcast([P, GH, P])
                step(nc.vector.tensor_tensor(heads(GST[:, nxt, :]), heads(GST[:, i % 2, :]), end, ALU.mult))
                dve.wait_ge(*due("c_ws", i + 1))
                if i % 2 == 0 and p >= 2:
                    dve.wait_ge(*due("c_o", p - 1))
                nc.vector.tensor_tensor(GVN[half, p % 2, :], GU_[half, p, :], PS[i % 2][half, :], ALU.add).then_inc(S("c_vn"), 1)
                dve.wait_ge(*due("c_kv", i + 1))
                nc.vector.tensor_tensor(GST[:, nxt, :], GST[:, nxt, :], PS[4 + i % 2], ALU.add).then_inc(S("c_st"), 1)
            x, cols = SC[:, 96:112], SM[:, 32:48]
            dve.wait_ge(*due("go_sums", GH))
            step(nc.vector.tensor_scalar(x, PS[7][:, 0:16], 1.0 / GD, RMS_EPS, ALU.mult, ALU.add))
            inverse_root(step, cols, x, scratch(16))
            dve_diags(dve, "go", cols, 0)
            dve.wait_ge(*due("go_gated", TOK))
            for h in range(GH):
                if h < GH - 1:
                    dve_diags(dve, "go", cols, h + 1)
                dve.wait_ge(*due("go_spread", h + 1))
                nc.vector.scalar_tensor_tensor(out=T[:, 4 + h % 2, :], in0=GO[:, h, :], scalar=vec("out_norm"), in1=PS[4 + h % 2], op0=ALU.mult, op1=ALU.mult).then_inc(S("go_scaled"), 1)
                dve.wait_ge(*due("mx_hi", h + 1))
                nc.vector.tensor_tensor(XL[:, 4 + h, :], T[:, 4 + h % 2, :], XH[:, 4 + h, :].bitcast(F32), ALU.subtract).then_inc(S("mx_lo"), 1)

        PMV, PMQ, PMEMO = (PH[n] for n in ("mem_v", "mem_q", "mem_o"))
        F2 = place("branch_out_2", YAT, [KD, SEQ])
        MRAW = place("mem_raw", YAT + 16, [KD, MEM])
        MXH = place("mem_hi", YAT + 24, [KD, MEM], F32R)
        MXL = place("mem_lo", YAT + 32, [KD, MEM], F32R)
        MVR = place("mem_v_rows", YAT + 48, [KM, D])
        MQ = place("mem_q_t", YAT + 66, [KD, SEQ])
        MP = place("mem_p", YAT + 82, [2, MEM])
        MPT = place("mem_pt", YAT + 84, [2, KM, SEQ])

        def pe_branch(pe, ph, n, ready=None):
            def body(r, parity, pair):
                for i in range(2):
                    if not (isinstance(r, int) and r < 2):
                        pe.wait_ge(*due(f"{n}_sq", r * 2 + (i - 3)))
                    feature_tile(pe, ph, r, (2 * i, 2 * i + 1), PS[2 * parity + i], XH, XL, ready if first(r) and i == 0 else None)
            rounds(pe, ph, body)

        def act_branch(act, ph, n, to):
            def body(r, parity, pair):
                for i in range(2):
                    wait(act, units_used, ph.used(r, 2 * i + 1))
                    if not (isinstance(r, int) and r == 0):
                        wait(act, *due(f"{n}_added", r * 2 + (i - 1)))
                    nc.scalar.activation(to[:, r * 2 + i, :], PS[2 * parity + i], ACT.Copy).then_inc(S(f"{n}_f"), 1)
                    nc.scalar.activation(T[:, i, :], PS[2 * parity + i], ACT.Square).then_inc(S(f"{n}_sq"), 1)
            rounds(act, ph, body)

        def dve_branch(dve, ph, n):
            def body(r, parity, pair):
                for i in range(2):
                    dve.wait_ge(*due(f"{n}_sq", r * 2 + (i + 1)))
                    if first(r) and i == 0:
                        nc.vector.tensor_copy(ACC, T[:, i, :]).then_inc(S(f"{n}_added"), 1)
                    else:
                        dve.wait_ge(*due(f"{n}_added", r * 2 + i))
                        nc.vector.tensor_tensor(ACC, ACC, T[:, i, :], ALU.add).then_inc(S(f"{n}_added"), 1)
            rounds(dve, ph, body)

        def act_mem_prepare(act):
            act.wait_ge(units_used, PMO.used(0, 0))
            act.dma_start(MRAW[:, :, :], dram["mem"]).then_inc(S("mem_in"), 16)
            act.wait_ge(*due("mem_in", 32))
            for k in range(KD):
                nc.scalar.activation(MXH[:, k, :], MRAW[:, k, :], ACT.Copy, scale=vec("mem_kv", k)).then_inc(S("m2_hi"), 1)

        def dve_mem_prepare(dve):
            dve.wait_ge(*due("mem_in", 32))
            for k in range(KD):
                dve.wait_ge(*due("m2_hi", k + 1))
                nc.vector.scalar_tensor_tensor(out=MXL[:, k, :], in0=MRAW[:, k, :], scalar=vec("mem_kv", k), in1=MXH[:, k, :].bitcast(F32), op0=ALU.mult, op1=ALU.subtract).then_inc(S("m2_lo"), 1)

        def pe_mem_kv(pe):
            def values(r, parity, pair):
                if first(r):
                    pe.wait_ge(*due("m2_lo", KD))

                def free(i):
                    if not (isinstance(r, int) and r < 2):
                        pe.wait_ge(*due("mv", pair * 2 + (i - 1)))
                token_tiles(pe, PMV, r, parity, PS[4:6], MXH, MXL, None, free)
                if first(r):
                    pe_sum(pe, "mx", ACC, PS[7])
                elif isinstance(r, int) and r == 1:
                    pe_spread(pe, "mx", DIAG, PS[6])
            rounds(pe, PMV, values)

            def queries(r, parity, pair):
                if first(r):
                    pe.wait_ge(*due("mx_sq", KD))
                for i in range(2):
                    if not (isinstance(r, int) and r < 2):
                        pe.wait_ge(*due("mq", r * 2 + (i - 3)))
                    feature_tile(pe, PMQ, r, (2 * i, 2 * i + 1), PS[2 * parity + i], XH, XL,
                                 (lambda k: pe.wait_ge(*due("s4_lo", k + 1))) if first(r) and i == 0 else None)
                    if first(r):
                        if i == 0:
                            pe_sum(pe, "s4", ACC, PS[7])
                        else:
                            pe_spread(pe, "s4", DIAG, PS[6])
            rounds(pe, PMQ, queries)

        def act_mem_kv(act):
            def values(n):
                act.wait_ge(units_used, PMV.used(2 * n + 1, 3))
                for i in range(KM):
                    nc.scalar.activation(MVR[:, i, n * SEQ:(n + 1) * SEQ], PS[4 + i], ACT.Copy, scale=MCOL[:, i:i + 1]).then_inc(S("mv"), 1)
            values(0)
            act_rows(act, "mx", PS[6], RB[:, :])
            act_join(act, "mx", "s4", "mem_pre", lambda k: values(1) if k == 4 else None)
            act_rows(act, "s4", PS[6], RB[:, :])

        def dve_mem_kv(dve, step):
            dve_column(dve, step, "mx", PS[7][:, 0:4], COL, D, RMS_EPS)
            dve_diag(dve, step, "mx", COL, DIAG)
            dve_join(dve, step, "mx", "mix_post", 1.0, "s4", "mem_pre", f=F2)
            dve_column(dve, step, "s4", PS[7][:, 0:4], COL, D, RMS_EPS)
            dve_diag(dve, step, "s4", COL, DIAG)
            dve.wait_ge(*due("s4_rb", 1))

            def queries(r, parity, pair):
                for i in range(2):
                    dve.wait_ge(units_used, PMQ.used(r, 2 * i + 1))
                    nc.vector.scalar_tensor_tensor(out=MQ[:, r * 2 + i, :], in0=PS[2 * parity + i], scalar=MHD ** -0.5, in1=RB[:, :], op0=ALU.mult, op1=ALU.mult).then_inc(S("mq"), 1)
            rounds(dve, PMQ, queries)

        MSTEPS = MH * TOK

        def pe_mem_attention(pe):
            pe.wait_ge(*due("mq", KD))
            for i in range(MSTEPS + 5):
                h, qt = divmod(i, TOK)
                if i < MSTEPS:
                    if i >= 2:
                        pe.wait_ge(*due("ma_e", i - 1))
                    for d in range(2):
                        last = nc.tensor.matmul(PS[i % 2][:, 0:MEM], MQ[:, 2 * h + d, tile_of(qt)], MKT[2 * h + d], start=d == 0, stop=d == 1)
                    last.then_inc(S("ma_s"), 1)
                j = i - 2
                if 0 <= j < MSTEPS:
                    pe.wait_ge(*due("ma_p", j + 1))
                    if j >= 2:
                        pe.wait_ge(*due("ma_pt", j - 1))
                    for kt in range(KM):
                        last = nc.tensor.transpose(PS[2 + j % 2][:, kt * P:(kt + 1) * P], MP[:, j % 2, kt * P:(kt + 1) * P], IDENT[:, :])
                    last.then_inc(S("ma_t"), 1)
                if i >= 8 and qt == 0:
                    g = h - 2
                    pe.wait_ge(*due("ma_pt", TOK * (g + 1)))
                    for d in range(2):
                        if g >= 1:
                            pe.wait_ge(*due("ma_lo", 2 * (g - 1) + d + 1))
                        for kt in range(KM):
                            last = nc.tensor.matmul(PS[4 + d], MVR[:, kt, (2 * g + d) * P:(2 * g + d + 1) * P], MPT[:, g % 2, kt, :], start=kt == 0, stop=kt == KM - 1)
                        last.then_inc(S("ma_o"), 1)

        def act_mem_attention(act):
            MXC, SUMC = SC[:, 0:32], SC[:, 32:64]
            for i in range(MSTEPS + 4):
                h, qt = divmod(i, TOK)
                if i < MSTEPS:
                    act.wait_ge(*due("ma_nm", i + 1))
                    if i >= 2:
                        act.wait_ge(*due("ma_t", i - 1))
                    nc.scalar.activation(MP[:, i % 2, :], PS[i % 2][:, 0:MEM], ACT.Exp, bias=MXC[:, i:i + 1], accum_out=SUMC[:, i:i + 1]).then_inc(S("ma_e"), 1)
                j = i - 3
                if 0 <= j < MSTEPS:
                    jh, jq = divmod(j, TOK)
                    act.wait_ge(*due("ma_t", j + 1))
                    if jh >= 2 and jq == 0:
                        act.wait_ge(*due("ma_o", 2 * (jh - 1)))
                    nc.scalar.activation(MPT[:, jh % 2, :, tile_of(jq)], PS[2 + j % 2][:, 0:MEM].rearrange("p (k q) -> p k q", q=P), ACT.Copy).then_inc(S("ma_pt"), 1)
                if i >= 8 and qt == 3:
                    for d in range(2):
                        act_mem_hi(act, 2 * (h - 2) + d)
            for d in range(2):
                act_mem_hi(act, 2 * (MH - 1) + d)

        def act_mem_hi(act, t):
            act.wait_ge(*due("ma_o", t + 1))
            nc.scalar.activation(XH[:, t, :], PS[4 + t % 2], ACT.Copy).then_inc(S("ma_hi"), 1)

        def dve_mem_attention(dve, step):
            MXC, SUMC = SC[:, 0:32], SC[:, 32:64]

            def lo(t):
                dve.wait_ge(*due("ma_hi", t + 1))
                nc.vector.tensor_tensor(XL[:, t, :], PS[4 + t % 2], XH[:, t, :].bitcast(F32), ALU.subtract).then_inc(S("ma_lo"), 1)
            for i in range(MSTEPS + 4):
                h, qt = divmod(i, TOK)
                if i < MSTEPS:
                    dve.wait_ge(*due("ma_s", i + 1))
                    step(nc.vector.reduce_max(MXC[:, i:i + 1], PS[i % 2][:, 0:MEM], axis=AX.X))
                    nc.vector.tensor_scalar(MXC[:, i:i + 1], MXC[:, i:i + 1], -1.0, None, ALU.mult).then_inc(S("ma_nm"), 1)
                if 1 <= i <= MSTEPS:
                    j = i - 1
                    dve.wait_ge(*due("ma_e", j + 1))
                    step(nc.vector.reciprocal(SUMC[:, j:j + 1], SUMC[:, j:j + 1]))
                    nc.vector.tensor_scalar(MP[:, j % 2, :], MP[:, j % 2, :], SUMC[:, j:j + 1], None, ALU.mult).then_inc(S("ma_p"), 1)
                if i >= 8 and qt == 3:
                    for d in range(2):
                        lo(2 * (h - 2) + d)
            for d in range(2):
                lo(2 * (MH - 1) + d)

        block = ctx.enter_context(nc.Block())
        end = phases[-1].name
        reached = lambda name: name in active
        full = reached("ffn2_down")

        @block.sync
        def _(sp):
            sp_loads(sp)
            last = {"a_out": "a_x", "b_out": "b_x", "ffn1_down": "f1_x", "mix_out": "mx_x", "mem_o": "mo_x", "ffn2_down": "f2_x"}[end]
            for k in range(KD):
                sp.wait_ge(*(x_ready("f2", k, True) if full else due(last, k + 1)))
                sp.dma_start(out[:, k, :], X[:, k, :]).then_inc(S("stored"), 16)
            sp.wait_ge(*due("stored", 16 * KD))

        @block.gpsimd
        def _(pool):
            pool_setup(pool)
            pool_split(pool)
            if full:
                pool_residuals(pool, "f2", "ffn2_post", 0.5, F)

        @block.tensor
        def _(pe):
            pe_a_v(pe)
            pe_a_ug(pe)
            pe_a_out(pe)
            if reached("b_out"):
                pe_b_in(pe)
                pe_b_out(pe)
            if reached("ffn1_down"):
                pe_ffn_up(pe, "ffn1", "s2", ("b_x", KD), lambda i: pe_between(pe, i))
                pe_ffn_down(pe, "ffn1", "f1", lambda r: pe_mem_norm(pe, r))
                pe_mem_keys(pe)
            if reached("mix_out"):
                pe_mix_in(pe)
                pe_cols(pe)
                pe_fox(pe)
                pe_gdn_products(pe)
                pe_levels(pe)
                pe_chunks(pe)
                pe_branch(pe, PMO, "mx", lambda k: pe.wait_ge(*due("mx_lo", max(k - 3, 1))))
            if reached("mem_o"):
                pe_mem_kv(pe)
                pe_mem_attention(pe)
                pe_branch(pe, PMEMO, "mo", lambda k: pe.wait_ge(*due("ma_lo", k + 1)))
                pe_sum(pe, "mo", ACC, PS[7])
                pe_spread(pe, "mo", DIAG, PS[6])
            if reached("ffn2_down"):
                def between(i):
                    if i == 0:
                        pe_sum(pe, "s5", ACC, PS[7])
                    else:
                        pe_spread(pe, "s5", DIAG, PS[6])
                pe_ffn_up(pe, "ffn2", "s5", ("mo_sq", KD), between)
                pe_ffn_down(pe, "ffn2", "f2")
                pe_sum(pe, "f2", ACC, PS[7])
                pe_spread(pe, "f2", DIAG, PS[6])

        @block.scalar
        def _(act):
            act_setup(act)
            act_lru_cols(act)
            act_a_v(act)
            act_a_ug(act)
            act_a_out(act)
            if reached("b_out"):
                act_b_loads(act)
                act_b_in(act)
                act_b_out(act)
            if reached("ffn1_down"):
                act_between(act)
                act_ffn_up(act, "ffn1")
                act_mem_squares(act)
                act_ffn_down(act, "ffn1", "f1", lambda r: act_mem_norm(act, r))
                act_mem_keys(act)
            if reached("mix_out"):
                act_mix_in(act)
                act_fox(act)
                act_gdn_products(act)
                act_levels(act)
                act_chunks(act)
                act_mem_prepare(act)
                act_branch(act, PMO, "mx", F2)
            if reached("mem_o"):
                act_mem_kv(act)
                act_mem_attention(act)
                act_branch(act, PMEMO, "mo", F2)
                act_rows(act, "mo", PS[6], RB[:, :])
                act_join(act, "mo", "s5", "ffn2_pre", pooled=full)
            if reached("ffn2_down"):
                act_rows(act, "s5", PS[6], RB[:, :])
                act_ffn_up(act, "ffn2")
                act_ffn_down(act, "ffn2", "f2")
                act_rows(act, "f2", PS[6], RB[:, :])

        @block.vector
        def _(dve):
            step = Chain(dve, S("vector_steps"))
            dve_setup(dve, step)
            dve_lru_cols(dve, step)
            dve_a_v(dve, step)
            dve_a_ug(dve, step)
            dve_a_out(dve, step)
            if reached("b_out"):
                dve_b_in(dve, step)
                dve_b_out(dve, step)
            if reached("ffn1_down"):
                dve_between(dve, step)
                dve_ffn_up(dve, step, "ffn1")
                dve_mem_squares(dve)
                dve_ffn_down(dve, step, "ffn1", "f1", lambda r: dve_mem_norm(dve, step, r))
                dve_join(dve, step, "f1", "ffn1_post", 0.5, "s3", "mix_pre")
            if reached("mix_out"):
                dve_mix_in(dve, step)
                dve_fox(dve, step)
                dve_gdn_products(dve, step)
                dve_levels(dve, step)
                dve_chunks(dve, step)
                dve_mem_prepare(dve)
                dve_branch(dve, PMO, "mx")
            if reached("mem_o"):
                dve_mem_kv(dve, step)
                dve_mem_attention(dve, step)
                dve_branch(dve, PMEMO, "mo")
                dve_column(dve, step, "mo", PS[7][:, 0:4], COL, D, RMS_EPS)
                dve_diag(dve, step, "mo", COL, DIAG)
                dve_join(dve, step, "mo", "mem_post", 1.0, "s5", "ffn2_pre", f=F2, pooled=full)
            if reached("ffn2_down"):
                dve_column(dve, step, "s5", PS[7][:, 0:4], COL, D, RMS_EPS)
                dve_diag(dve, step, "s5", COL, DIAG)
                dve.wait_ge(*due("s5_rb", 1))
                dve_ffn_up(dve, step, "ffn2")
                dve_ffn_down(dve, step, "ffn2", "f2")
                dve.wait_ge(*due("f2_rb", 1))
                for k in range(KD):
                    if k not in POOL_TILES:
                        dve_residual(dve, step, "f2", k, "ffn2_post", 0.5, F, True)
    return nc



def _cols(w, m):
    k = w.shape[0] // P
    return w[:, m * P:(m + 1) * P].reshape(k, P, P).transpose(1, 0, 2)


def _tiles(w, order):
    return np.stack([np.concatenate([_cols(w, a), _cols(w, b)], 1).reshape(P, -1) for a, b in order])


def _singles(w):
    return np.stack([_cols(w, m).reshape(P, -1) for m in range(w.shape[1] // P)])


def _moving(w):
    n = w.shape[1] // 512
    return w.reshape(2, 4, P, n, 512).transpose(3, 0, 2, 1, 4).reshape(2 * n, P, 4 * 512)


def _vec(v):
    return v.reshape(-1, P).T


def layout(i):
    a = {}
    a["x"] = i["x"][0].T.reshape(KD, P, SEQ).transpose(1, 0, 2)
    w = i["a_w_in"][0]
    a["a_v"] = _moving(w[:, AW:2 * AW])
    a["a_ug"] = _tiles(w, [(m, 2 * KA + m) for m in range(KA)])
    a["a_out"] = _singles(i["a_w_out"][0])
    a["a_w_s"] = i["a_w_s"][0].transpose(2, 0, 1)
    a["a_b_s"] = i["a_b_s"][0].reshape(-1)
    w = i["b_w_in"][0]
    a["b_in"] = _tiles(w, [(m, KB + m) for m in range(KB)])
    a["b_gates"] = np.stack([i["b_gate_a_w"][0], i["b_gate_x_w"][0]], 1).transpose(2, 0, 1, 3).reshape(P, -1)
    a["b_out"] = _singles(i["b_w_out"][0])
    for f in ("ffn1", "ffn2"):
        both = np.concatenate([i[f"{f}_w_gate_2"][0], i[f"{f}_w_up_2"][0]], 1)
        a[f"{f}_up"] = _tiles(both, [(m, KF + m) for m in range(KF)])
        a[f"{f}_down"] = _singles(i[f"{f}_w_down_2"][0])
    w = i["w_in_2"][0]
    FOX, GDN = FOXH * FOXD, GH * GD
    at = np.cumsum([0, FOX, FOX, FOX, FOXH, GDN, GDN, GDN, GDN, GH, GH])
    part = [w[:, at[n]:at[n + 1]] for n in range(10)]
    a["fox_v"] = _moving(part[2])
    a["fox_qk"] = _tiles(np.concatenate(part[0:2], 1), [(m, 4 + m) for m in range(4)])
    small = np.zeros((D, P), w.dtype)
    small[:, 0:FOXH], small[:, 32:32 + GH], small[:, 64:64 + GH] = part[3], part[8], part[9]
    a["small"] = _cols(small, 0).reshape(P, 2, 4 * P).transpose(1, 0, 2)
    qkv = np.concatenate(part[4:7], 1)
    a["gdn_qkv"] = _tiles(qkv, [(m, m + 1) for m in range(0, 12, 2)])
    a["gdn_z"] = _tiles(part[7], [(0, 1), (2, 3)])
    a["mix_out"] = _tiles(i["w_out_2"][0], [(m, m + 1) for m in range(0, 8, 2)])
    pairs = [(m, m + 1) for m in range(0, 8, 2)]
    kv = i["mem_w_kv_2"][0]
    a["mem_k"], a["mem_v"] = _tiles(kv[:, :D], pairs), _moving(kv[:, D:])
    a["mem_q"], a["mem_o"] = _tiles(i["mem_w_q_2"][0], pairs), _tiles(i["mem_w_o_2"][0], pairs)
    a["mem"] = i["mem_2"][0].T.reshape(KD, P, MEM).transpose(1, 0, 2)
    column = lambda n, v: np.concatenate([np.zeros(n, v.dtype), v, np.zeros(P - n - len(v), v.dtype)])
    small_bias = np.zeros(P, w.dtype)
    small_bias[0:FOXH], small_bias[64:64 + GH] = i["fox_f_bias_2"][0], i["gdn_dt_bias_2"][0]
    vecs = {
        "norm0": i["norm_w"][0], "norm1": i["norm_w"][1], "normf": i["norm_f_w"],
        "a_ln_w": i["a_ln_w"][0], "a_ln_b": i["a_ln_b"][0], "conv": i["b_conv_w"][0].reshape(-1),
        "conv_b": i["b_conv_b"][0], "gate_a_b": i["b_gate_a_b"][0], "gate_x_b": i["b_gate_x_b"][0],
        "lam": i["b_lambda"][0], "ffn1_pre": i["ffn1_pre_norm_2"][0], "ffn1_post": i["ffn1_post_norm_2"][0],
        "mix_pre": i["mix_pre_norm_2"][0], "mix_post": i["mix_post_norm_2"][0],
        "gconv": i["gdn_conv_w_2"][0].reshape(-1), "out_norm": i["gdn_out_norm_2"][0],
        "mem_pre": i["mem_pre_norm_2"][0], "mem_kv": i["mem_kv_norm_2"][0], "mem_post": i["mem_post_norm_2"][0],
        "ffn2_pre": i["ffn2_pre_norm_2"][0], "ffn2_post": i["ffn2_post_norm_2"][0],
        "small_bias": small_bias, "a_log": column(64, i["gdn_a_log_2"][0]),
    }
    a["vecs"] = np.concatenate([_vec(vecs[name]) for name, _ in VEC_SIZES], 1)
    return a


def kernel(**inputs):
    import concourse.bacc as bacc
    from concourse.bass_utils import run_bass_kernel_spmd

    arrays = {f"in_{n}": np.ascontiguousarray(a) for n, a in layout({n: np.asarray(v) for n, v in inputs.items()}).items()}
    nc = bacc.Bacc("TRN2", target_bir_lowering=False, num_devices=1)
    dram = {n[3:]: nc.dram_tensor(n, a.shape, mybir.dt.from_np(a.dtype), kind="ExternalInput").ap() for n, a in arrays.items()}
    out = nc.dram_tensor("out", (P, KD, SEQ), F32, kind="ExternalOutput").ap()
    build(nc, dram, out)
    r = run_bass_kernel_spmd(nc, [arrays], core_ids=[0]).results[0]["out"]
    return r.transpose(1, 0, 2).reshape(D, SEQ).T.reshape(1, SEQ, D)
```
